# Optimizing a Trainium2 kernel written in Bass

```python
import math
import jax, jax.numpy as jnp
from jax import lax
import numpy as np

D_MODEL = 1024
BATCH = 1
SEQ = 512
DEPTH = 1
DEC_BATCH = 8
DEC_SEQ = 4
PAST_LEN = 2048
PAGE_SIZE = 128

SSD_HEADS = 8
SSD_HEAD_DIM = 64
SSD_INNER = SSD_HEADS * SSD_HEAD_DIM
SSD_GROUPS = 2
SSD_STATE = 128
SSD_CONV = 4
SSD_CHUNK = 128
CONV_DIM = SSD_INNER + 2 * SSD_GROUPS * SSD_STATE

ATT_HEADS = 8
ATT_HEAD_DIM = 64
ATT_INNER = ATT_HEADS * ATT_HEAD_DIM
IDX_HEADS = 8
IDX_DIM = 64
TOPK_MAX = 256
Q_BLOCK = 128

N_BUCKETS = 32
MAX_DISTANCE = 128

MEM_TOKENS = 256
MEM_HEADS = 4
MEM_HEAD_DIM = 128
MEM_INNER = MEM_HEADS * MEM_HEAD_DIM

PEER_HEADS = 8
PEER_KEYS = 128
PEER_EXPERTS = PEER_KEYS * PEER_KEYS
PEER_HALF = 128
PEER_QDIM = 2 * PEER_HALF
PEER_TOPK = 16
PEER_BLOCK = 128

MIX_WIDTH = SSD_INNER + ATT_INNER
IN_SPLITS = (SSD_INNER, CONV_DIM, SSD_HEADS, ATT_INNER, ATT_INNER, ATT_INNER, IDX_HEADS * IDX_DIM, IDX_DIM, IDX_HEADS)
IN_COLS = sum(IN_SPLITS)
ALPHA = (2.0 * DEPTH) ** 0.25
BETA = (8.0 * DEPTH) ** -0.25
LN_EPS = 1e-5

kernel_name = "hymba_ssd_dsa_peer_decode_step"

def layer_norm(x, g, b):
    xf = x.astype(jnp.float32)
    mu = jnp.mean(xf, axis=-1, keepdims=True)
    var = jnp.mean(jnp.square(xf - mu), axis=-1, keepdims=True)
    return ((xf - mu) * lax.rsqrt(var + LN_EPS)).astype(x.dtype) * g + b

def gated_rmsnorm(y, z, w):
    h = (y * jax.nn.silu(z)).astype(jnp.float32)
    h = h * lax.rsqrt(jnp.mean(h * h, axis=-1, keepdims=True) + LN_EPS)
    return h.astype(y.dtype) * w

def project_in(x, w_in):
    b, L, _ = x.shape
    points = [int(p) for p in np.cumsum(IN_SPLITS)[:-1]]
    z, xbc, dt_raw, q, k, v, q_idx, k_idx, w_idx = jnp.split(x @ w_in, points, axis=-1)
    q = q.reshape(b, L, ATT_HEADS, ATT_HEAD_DIM)
    k = k.reshape(b, L, ATT_HEADS, ATT_HEAD_DIM)
    v = v.reshape(b, L, ATT_HEADS, ATT_HEAD_DIM)
    q_idx = q_idx.reshape(b, L, IDX_HEADS, IDX_DIM) * (IDX_DIM ** -0.5)
    w_idx = w_idx * (IDX_HEADS ** -0.5)
    return z, xbc, dt_raw, q, k, v, q_idx, k_idx, w_idx

def causal_conv(xbc, buf, w, bias):
    L = xbc.shape[1]
    full = jnp.concatenate([buf, xbc], axis=1)
    out = full[:, 0:L] * w[0]
    for tap in range(1, SSD_CONV):
        out = out + full[:, tap:tap + L] * w[tap]
    return jax.nn.silu(out + bias), full[:, -(SSD_CONV - 1):]

def ssd_scan(x, dt, A, B, C, h0, chunk):
    b, L, H, P = x.shape
    nc = L // chunk
    rep = H // SSD_GROUPS
    B = jnp.repeat(B, rep, axis=2)
    C = jnp.repeat(C, rep, axis=2)
    xd = x * dt[..., None]
    a = (dt * A).astype(jnp.float32)
    resh = lambda t: t.reshape((b, nc, chunk) + t.shape[2:])
    xd, a, B, C = resh(xd), resh(a), resh(B), resh(C)
    a_cum = jnp.cumsum(a, axis=2)
    seg = a_cum[:, :, :, None, :] - a_cum[:, :, None, :, :]
    causal = jnp.tril(jnp.ones((chunk, chunk), dtype=bool))[None, None, :, :, None]
    decay = jnp.exp(jnp.where(causal, seg, -jnp.inf)).astype(x.dtype)
    scores = jnp.einsum('bcihn,bcjhn->bcijh', C, B)
    y_diag = jnp.einsum('bcijh,bcjhp->bcihp', scores * decay, xd)
    decay_to_end = jnp.exp(a_cum[:, :, -1:, :] - a_cum).astype(x.dtype)
    chunk_states = jnp.einsum('bcjhn,bcjh,bcjhp->bchpn', B, decay_to_end, xd)
    chunk_decay = jnp.exp(a_cum[:, :, -1, :]).astype(x.dtype)

    def step(h, inp):
        s, d = inp
        return h * d[:, :, None, None] + s, h

    h_final, h_starts = lax.scan(step, h0, (jnp.moveaxis(chunk_states, 1, 0), jnp.moveaxis(chunk_decay, 1, 0)))
    h_starts = jnp.moveaxis(h_starts, 0, 1)
    y_off = jnp.einsum('bcihn,bchpn,bcih->bcihp', C, h_starts, jnp.exp(a_cum).astype(x.dtype))
    return (y_diag + y_off).reshape(b, L, H, P), h_final

def ssd_mixer(z, xbc, dt_raw, conv_buf, h0, chunk, conv_w, conv_b, dt_bias, a_log, d_skip, norm_w):
    xbc_c, new_buf = causal_conv(xbc, conv_buf, conv_w, conv_b)
    xs, Bm, Cm = jnp.split(xbc_c, [SSD_INNER, SSD_INNER + SSD_GROUPS * SSD_STATE], axis=-1)
    b, L, _ = xs.shape
    xs = xs.reshape(b, L, SSD_HEADS, SSD_HEAD_DIM)
    Bm = Bm.reshape(b, L, SSD_GROUPS, SSD_STATE)
    Cm = Cm.reshape(b, L, SSD_GROUPS, SSD_STATE)
    dt = jax.nn.softplus(dt_raw + dt_bias)
    A = -jnp.exp(a_log)
    y, h = ssd_scan(xs, dt, A, Bm, Cm, h0, chunk)
    y = y + xs * d_skip[:, None]
    return gated_rmsnorm(y.reshape(b, L, SSD_INNER), z, norm_w), h, new_buf

def rel_bucket(dist):
    n = jnp.maximum(dist, 0)
    max_exact = N_BUCKETS // 2
    nf = jnp.maximum(n, 1).astype(jnp.float32)
    large = max_exact + (jnp.log(nf / max_exact) / math.log(MAX_DISTANCE / max_exact) * (N_BUCKETS - max_exact)).astype(jnp.int32)
    large = jnp.minimum(large, N_BUCKETS - 1)
    return jnp.where(n < max_exact, n, large)

def indexer_scores(q_idx, w_idx, k_idx):
    s = jax.nn.relu(jnp.einsum('bthd,bsd->bths', q_idx, k_idx))
    return jnp.einsum('bths,bth->bts', s, w_idx).astype(jnp.float32)

def sparse_attend(q, k_sel, v_sel, valid, bias):
    logits = jnp.einsum('bthd,btkhd->bthk', q, k_sel).astype(jnp.float32) * (ATT_HEAD_DIM ** -0.5)
    logits = logits + jnp.moveaxis(bias, -1, 2).astype(jnp.float32)
    logits = jnp.where(valid[:, :, None, :], logits, -jnp.inf)
    p = jax.nn.softmax(logits, axis=-1).astype(v_sel.dtype)
    return jnp.einsum('bthk,btkhd->bthd', p, v_sel)

def dsa_prompt(q, k, v, q_idx, w_idx, k_idx, rel_bias):
    b, S = q.shape[:2]
    topk = min(TOPK_MAX, S // 4)
    key_pos = jnp.arange(S)
    bidx = jnp.arange(b)[:, None, None]

    def block(i):
        t0 = i * Q_BLOCK
        qb = lax.dynamic_slice_in_dim(q, t0, Q_BLOCK, axis=1)
        qib = lax.dynamic_slice_in_dim(q_idx, t0, Q_BLOCK, axis=1)
        wib = lax.dynamic_slice_in_dim(w_idx, t0, Q_BLOCK, axis=1)
        pos_q = t0 + jnp.arange(Q_BLOCK)
        sc = indexer_scores(qib, wib, k_idx)
        sc = jnp.where(key_pos[None, None, :] <= pos_q[None, :, None], sc, -jnp.inf)
        _, sel = lax.top_k(sc, topk)
        valid = sel <= pos_q[None, :, None]
        bias = rel_bias[rel_bucket(pos_q[None, :, None] - sel)]
        return sparse_attend(qb, k[bidx, sel], v[bidx, sel], valid, bias)

    out = lax.map(block, jnp.arange(S // Q_BLOCK))
    return jnp.moveaxis(out, 0, 1).reshape(b, S, ATT_INNER)

def dsa_sample(q, k_new, v_new, q_idx, w_idx, kidx_new, cache_k, cache_v, cache_kidx, page_table, rel_bias):
    b, T = q.shape[:2]
    past = page_table.shape[1] * PAGE_SIZE
    L = past + T
    topk = min(TOPK_MAX, L // 4)
    kidx_past = cache_kidx[page_table].reshape(b, past, IDX_DIM)
    kidx_all = jnp.concatenate([kidx_past, kidx_new], axis=1)
    pos_q = past + jnp.arange(T)
    key_pos = jnp.arange(L)
    sc = indexer_scores(q_idx, w_idx, kidx_all)
    sc = jnp.where(key_pos[None, None, :] <= pos_q[None, :, None], sc, -jnp.inf)
    _, sel = lax.top_k(sc, topk)
    valid = sel <= pos_q[None, :, None]
    bidx = jnp.arange(b)[:, None, None]
    in_past = (sel < past)[..., None, None]
    sp = jnp.minimum(sel, past - 1)
    phys = page_table[bidx, sp // PAGE_SIZE]
    off = sp % PAGE_SIZE
    sn = jnp.clip(sel - past, 0, T - 1)
    k_sel = jnp.where(in_past, cache_k[phys, off], k_new[bidx, sn])
    v_sel = jnp.where(in_past, cache_v[phys, off], v_new[bidx, sn])
    bias = rel_bias[rel_bucket(pos_q[None, :, None] - sel)]
    return sparse_attend(q, k_sel, v_sel, valid, bias).reshape(b, T, ATT_INNER)

def mem_kv(mem, w_ck, w_cv):
    b, M, _ = mem.shape
    return (mem @ w_ck).reshape(b, M, MEM_HEADS, MEM_HEAD_DIM), (mem @ w_cv).reshape(b, M, MEM_HEADS, MEM_HEAD_DIM)

def mem_attend(h, mk, mv, w_cq, w_co):
    b, L, _ = h.shape
    q = (h @ w_cq).reshape(b, L, MEM_HEADS, MEM_HEAD_DIM)
    logits = jnp.einsum('blhd,bmhd->bhlm', q, mk).astype(jnp.float32) * (MEM_HEAD_DIM ** -0.5)
    p = jax.nn.softmax(logits, axis=-1).astype(mv.dtype)
    o = jnp.einsum('bhlm,bmhd->blhd', p, mv).reshape(b, L, MEM_INNER)
    return o @ w_co

def peer(h, wq, subkeys, u, v):
    shp = h.shape
    xt = h.reshape(-1, D_MODEL)
    n = xt.shape[0]
    nb = -(-n // PEER_BLOCK)
    xt = jnp.pad(xt, ((0, nb * PEER_BLOCK - n), (0, 0))).reshape(nb, PEER_BLOCK, D_MODEL)

    def block(xb):
        q = (xb @ wq).reshape(PEER_BLOCK, PEER_HEADS, 2, PEER_HALF)
        s = jnp.einsum('thpd,hpkd->thpk', q, subkeys).astype(jnp.float32)
        s_top, i_top = lax.top_k(s, PEER_TOPK)
        cand = (s_top[:, :, 0, :, None] + s_top[:, :, 1, None, :]).reshape(PEER_BLOCK, PEER_HEADS, PEER_TOPK * PEER_TOPK)
        cand_idx = (i_top[:, :, 0, :, None] * PEER_KEYS + i_top[:, :, 1, None, :]).reshape(PEER_BLOCK, PEER_HEADS, PEER_TOPK * PEER_TOPK)
        g_s, g_i = lax.top_k(cand, PEER_TOPK)
        e = jnp.take_along_axis(cand_idx, g_i, axis=-1)
        g = jax.nn.softmax(g_s, axis=-1).astype(xb.dtype)
        act = jax.nn.gelu(jnp.einsum('thed,td->the', u[e], xb))
        return jnp.einsum('the,thed->td', g * act, v[e])

    out = lax.map(block, xt).reshape(-1, D_MODEL)[:n]
    return out.reshape(shp)

def finish_layer(x, mixed, mk, mv, w_out, ln1_g, ln1_b, w_cq, w_co, ln2_g, ln2_b, peer_wq, peer_subkeys, peer_u, peer_v, ln3_g, ln3_b):
    h = layer_norm(ALPHA * x + mixed @ w_out, ln1_g, ln1_b)
    h = layer_norm(ALPHA * h + mem_attend(h, mk, mv, w_cq, w_co), ln2_g, ln2_b)
    return layer_norm(ALPHA * h + peer(h, peer_wq, peer_subkeys, peer_u, peer_v), ln3_g, ln3_b)

def setup_inputs(seed: int = 0) -> dict:
    key = jax.random.key(seed)
    ks = jax.random.split(key, 40)
    f32 = jnp.float32
    nrm = lambda k, shape, s=1.0: s * jax.random.normal(k, shape, f32)
    n_pages = PAST_LEN // PAGE_SIZE
    n_used = DEC_BATCH * n_pages
    n_pool = (5 * n_used) // 4 + 1
    page_table = jax.random.permutation(ks[0], n_pool)[:n_used].reshape(DEC_BATCH, n_pages).astype(jnp.int32)
    dt0 = jnp.exp(jax.random.uniform(ks[1], (SSD_HEADS,), f32, math.log(1e-3), math.log(1e-1)))
    return {
        "x_prompt": nrm(ks[2], (BATCH, SEQ, D_MODEL)),
        "mem_prompt": nrm(ks[3], (BATCH, MEM_TOKENS, D_MODEL)),
        "x_sample": nrm(ks[4], (DEC_BATCH, DEC_SEQ, D_MODEL)),
        "cache_k": nrm(ks[5], (n_pool, PAGE_SIZE, ATT_HEADS, ATT_HEAD_DIM)),
        "cache_v": nrm(ks[6], (n_pool, PAGE_SIZE, ATT_HEADS, ATT_HEAD_DIM)),
        "cache_kidx": nrm(ks[7], (n_pool, PAGE_SIZE, IDX_DIM)),
        "cache_mem_k": nrm(ks[8], (DEC_BATCH, MEM_TOKENS, MEM_HEADS, MEM_HEAD_DIM)),
        "cache_mem_v": nrm(ks[9], (DEC_BATCH, MEM_TOKENS, MEM_HEADS, MEM_HEAD_DIM)),
        "state_ssm": nrm(ks[10], (DEC_BATCH, SSD_HEADS, SSD_HEAD_DIM, SSD_STATE), 0.1),
        "state_conv": nrm(ks[11], (DEC_BATCH, SSD_CONV - 1, CONV_DIM)),
        "page_table": page_table,
        "w_in": nrm(ks[12], (D_MODEL, IN_COLS), D_MODEL ** -0.5),
        "conv_w": nrm(ks[13], (SSD_CONV, CONV_DIM), SSD_CONV ** -0.5),
        "conv_b": nrm(ks[14], (CONV_DIM,), 0.01),
        "dt_bias": dt0 + jnp.log(-jnp.expm1(-dt0)),
        "a_log": jnp.log(jax.random.uniform(ks[15], (SSD_HEADS,), f32, 1.0, 16.0)),
        "d_skip": 1.0 + nrm(ks[16], (SSD_HEADS,), 0.01),
        "ssd_norm_w": 1.0 + nrm(ks[17], (SSD_INNER,), 0.01),
        "rel_bias": nrm(ks[18], (N_BUCKETS, ATT_HEADS), 0.5),
        "w_out": nrm(ks[19], (MIX_WIDTH, D_MODEL), BETA * MIX_WIDTH ** -0.5),
        "ln1_g": 1.0 + nrm(ks[20], (D_MODEL,), 0.01),
        "ln1_b": nrm(ks[21], (D_MODEL,), 0.01),
        "w_cq": nrm(ks[22], (D_MODEL, MEM_INNER), D_MODEL ** -0.5),
        "w_ck": nrm(ks[23], (D_MODEL, MEM_INNER), D_MODEL ** -0.5),
        "w_cv": nrm(ks[24], (D_MODEL, MEM_INNER), D_MODEL ** -0.5),
        "w_co": nrm(ks[25], (MEM_INNER, D_MODEL), BETA * MEM_INNER ** -0.5),
        "ln2_g": 1.0 + nrm(ks[26], (D_MODEL,), 0.01),
        "ln2_b": nrm(ks[27], (D_MODEL,), 0.01),
        "peer_wq": nrm(ks[28], (D_MODEL, PEER_HEADS * PEER_QDIM), D_MODEL ** -0.5),
        "peer_subkeys": nrm(ks[29], (PEER_HEADS, 2, PEER_KEYS, PEER_HALF), PEER_HALF ** -0.5),
        "peer_u": nrm(ks[30], (PEER_EXPERTS, D_MODEL), D_MODEL ** -0.5),
        "peer_v": nrm(ks[31], (PEER_EXPERTS, D_MODEL), BETA * PEER_HEADS ** -0.5),
        "ln3_g": 1.0 + nrm(ks[32], (D_MODEL,), 0.01),
        "ln3_b": nrm(ks[33], (D_MODEL,), 0.01),
    }

def reference(x_prompt, mem_prompt, x_sample, cache_k, cache_v, cache_kidx, cache_mem_k, cache_mem_v,
              state_ssm, state_conv, page_table, w_in, conv_w, conv_b, dt_bias, a_log, d_skip, ssd_norm_w,
              rel_bias, w_out, ln1_g, ln1_b, w_cq, w_ck, w_cv, w_co, ln2_g, ln2_b,
              peer_wq, peer_subkeys, peer_u, peer_v, ln3_g, ln3_b):
    b_p = x_prompt.shape[0]
    z, xbc, dt_raw, q, k_p, v_p, q_idx, kidx_p, w_idx = project_in(x_prompt, w_in)
    conv0 = jnp.zeros((b_p, SSD_CONV - 1, CONV_DIM), x_prompt.dtype)
    h0 = jnp.zeros((b_p, SSD_HEADS, SSD_HEAD_DIM, SSD_STATE), x_prompt.dtype)
    ssd_out, ssm_p, conv_p = ssd_mixer(z, xbc, dt_raw, conv0, h0, SSD_CHUNK, conv_w, conv_b, dt_bias, a_log, d_skip, ssd_norm_w)
    att_out = dsa_prompt(q, k_p, v_p, q_idx, w_idx, kidx_p, rel_bias)
    memk_p, memv_p = mem_kv(mem_prompt, w_ck, w_cv)
    y_prompt = finish_layer(x_prompt, jnp.concatenate([ssd_out, att_out], axis=-1), memk_p, memv_p,
                            w_out, ln1_g, ln1_b, w_cq, w_co, ln2_g, ln2_b, peer_wq, peer_subkeys, peer_u, peer_v, ln3_g, ln3_b)

    t_s = x_sample.shape[1]
    z, xbc, dt_raw, q, k_s, v_s, q_idx, kidx_s, w_idx = project_in(x_sample, w_in)
    ssd_out, ssm_s, conv_s = ssd_mixer(z, xbc, dt_raw, state_conv, state_ssm, t_s, conv_w, conv_b, dt_bias, a_log, d_skip, ssd_norm_w)
    att_out = dsa_sample(q, k_s, v_s, q_idx, w_idx, kidx_s, cache_k, cache_v, cache_kidx, page_table, rel_bias)
    y_sample = finish_layer(x_sample, jnp.concatenate([ssd_out, att_out], axis=-1), cache_mem_k, cache_mem_v,
                            w_out, ln1_g, ln1_b, w_cq, w_co, ln2_g, ln2_b, peer_wq, peer_subkeys, peer_u, peer_v, ln3_g, ln3_b)

    return (y_prompt, y_sample, k_p, v_p, kidx_p, memk_p, memv_p, ssm_p, conv_p, k_s, v_s, kidx_s, ssm_s, conv_s)


_drawn_inputs = setup_inputs


def setup_inputs(seed=0):
    import zlib

    import numpy as np

    out = dict(_drawn_inputs(seed))
    spreads = {}
    factors = {'conv_b': 3.202,
     'd_skip': 35.098,
     'ssd_norm_w': 151.983,
     'ln1_g': 62.067,
     'ln1_b': 59.095,
     'ln2_g': 49.932,
     'ln2_b': 58.642,
     'ln3_g': 164.717,
     'ln3_b': 170.594,
     'cache_k': 4.758,
     'cache_v': 3.798,
     'cache_kidx': 3.902,
     'rel_bias': 5.6}
    for name, (base, spread) in spreads.items():
        noise = np.random.default_rng([zlib.crc32(name.encode()), seed]).standard_normal(out[name].shape)
        drawn = base * np.exp(spread * noise) if base else spread * noise
        out[name] = __import__('jax').numpy.asarray(drawn.astype(out[name].dtype))
    for name, factor in factors.items():
        out[name] = (out[name] * factor).astype(out[name].dtype)
    return out
```

```python
from contextlib import ExitStack

import numpy as np
import concourse.bass as bass
from concourse import mybir

F32 = mybir.dt.float32
F32R = mybir.dt.float32r
I32 = mybir.dt.int32
U32 = mybir.dt.uint32
ALU = mybir.AluOpType
ACT = mybir.ActivationFunctionType
AX_X = mybir.AxisListType.X

P = 128
D = 1024
KD = D // P
SEQ, NB, TS = 512, 8, 4
NS = NB * TS
NT = SEQ + NS
NTILE = SEQ // P + 1
STILE = NTILE - 1
H, HD = 8, 64
CONV = 1024
NPAGE, PAGE = 16, 128
PAST = NPAGE * PAGE
NKEY = PAST + NS
NBUCKET = 32
MH, MD, MEM = 4, 128, 256
PH, NKEYS, TOPK = 8, 128, 16
ALPHA = 2.0 ** 0.25
EPS = 1e-5
NOT_SELECTED = -1e30
NOT_CAUSAL = -2e38
PICKED = -3e38

OFF_Z, OFF_XBC, OFF_DT, OFF_Q, OFF_K, OFF_V, OFF_QI, OFF_KI, OFF_WI = (
    0, 512, 1536, 1544, 2056, 2568, 3080, 3592, 3656)
B_XBC, B_Q, B_K, B_QI, B_KI, NBLK = 0, 8, 12, 16, 20, 21
S_DT, S_KI, S_WI, NSMALL = 0, 8, 72, 80
VEC = {}
_at = 0
for _name, _n in (("ssd_norm_w", 512), ("dt_bias", H), ("a_log", H), ("d_skip", H), ("bias_far", H)):
    VEC[_name] = (_at, _n)
    _at += _n
NVEC = _at


def rows(t):
    return P if t < STILE else NS


def cols(t):
    return slice(t * P, t * P + rows(t))


class Link:

    def __init__(self, eng, own):
        self.eng, self.own, self.count = eng, own, {}

    def count_up(self, ins, sem):
        self.count[id(sem)] = self.count.get(id(sem), 0) + 1
        ins.then_inc(sem, 1)

    def __call__(self, ins, sem=None):
        sem = self.own if sem is None else sem
        self.count_up(ins, sem)
        self.eng.wait_ge(sem, self.count[id(sem)])


class Ctx:

    def __init__(self, nc, A):
        self.nc, self.A = nc, A
        self.stack, self.sems = ExitStack(), []
        self.bank = [self.stack.enter_context(nc.psum_tensor(f"bank{i}", [P, 512], F32)) for i in range(8)]

    def keep(self, stack, name, shape, side="left"):
        return stack.enter_context(self.nc.sbuf_tensor(name, shape, F32, side=side))

    def sem(self, name, software_dma=False):
        s = self.nc.alloc_semaphore(name)
        if not software_dma:
            self.sems.append(s)
        return s

    def reset_semaphores(self):
        spans = []
        for num in sorted(s.num for s in self.sems):
            if spans and spans[-1][1] == num:
                spans[-1][1] = num + 1
            else:
                spans.append([num, num + 1])
        with self.nc.Block() as block:
            @block.gpsimd
            def _(pool):
                for lo, hi in spans:
                    pool.sem_clear(range(lo, hi))
        for s in self.sems:
            self.nc.release_semaphore(s)
        self.sems = []


def stage_project(c):
    nc, A, bank = c.nc, c.A, c.bank
    RING = 4
    with ExitStack() as es:
        def sb(name, shape, dt=F32):
            return es.enter_context(nc.sbuf_tensor(name, shape, dt))
        xT = sb("xT", [P, KD, NT])
        wblk = sb("wblk", [P, RING, KD, P])
        wrow = sb("wrow", [P, 2, KD, 512])
        wsmall = sb("wsmall", [P, KD, NSMALL])
        krow = sb("krow", [P, 2, NTILE, P])
        crow = sb("crow", [NS + 3, CONV])
        x_in, small_in, state_in = c.sem("x_in"), c.sem("wsmall_in"), c.sem("state_conv_in")
        blk_in = [c.sem(f"wblk_in{i}") for i in range(RING)]
        row_in = [c.sem(f"wrow_in{i}") for i in range(2)]
        blk_mm, blk_act, blk_dve = c.sem("blk_mm"), c.sem("blk_act"), c.sem("blk_dve")
        row_mm, row_ev = c.sem("row_mm"), c.sem("row_ev")
        pad_done, store = c.sem("pad_done"), c.sem("proj_store", True)
        kst = [c.sem(f"krow_store{i}", True) for i in range(2)]
        NROW = 3 * NTILE

        with nc.Block() as block:
            @block.sync
            def _(sp):
                sp.dma_start(xT[:], A["xT"]).then_inc(x_in, 16)
                for j in range(NBLK):
                    if j >= RING:
                        sp.wait_ge(blk_mm, j - RING + 1)
                    sp.dma_start(wblk[:, j % RING], A["w_blk"][j]).then_inc(blk_in[j % RING], 16)
                    if j == 2:
                        sp.dma_start(c.convin_s[:, :, :, 0:3], A["state_convT"]).then_inc(state_in, 16)
                for i in range(2):
                    sp.dma_start(wrow[:, i], A["w_row"][i]).then_inc(row_in[i], 16)
                sp.dma_start(wsmall[:], A["w_small"]).then_inc(small_in, 16)
                sp.wait_ge(state_in, 16)

            @block.tensor
            def _(pe):
                pe.wait_ge(x_in, 16)
                for j in range(NBLK):
                    pe.wait_ge(blk_in[j % RING], 16 * (j // RING + 1))
                    if j >= 2:
                        pe.wait_ge(blk_act, j - 1)
                        pe.wait_ge(blk_dve, j - 1)
                    big, little, tall = bank[j % 2], bank[2 + j % 2], bank[4 + j % 2]
                    for k in range(KD):
                        nc.tensor.matmul(big[:], wblk[:, j % RING, k], xT[:, k, 0:SEQ],
                                         start=k == 0, stop=k == KD - 1)
                    for k in range(KD):
                        last = nc.tensor.matmul(little[:, 0:NS], wblk[:, j % RING, k], xT[:, k, SEQ:NT],
                                                start=k == 0, stop=k == KD - 1)
                    if j < B_Q:
                        for k in range(KD):
                            last = nc.tensor.matmul(tall[0:NS + 3, 0:P], xT[:, k, SEQ - 3:NT],
                                                    wblk[:, j % RING, k], start=k == 0, stop=k == KD - 1)
                    if B_K <= j < B_QI:
                        for t in range(NTILE):
                            dst = tall[:, t * P:(t + 1) * P] if t < STILE else bank[6 + j % 2][0:NS, 0:P]
                            for k in range(KD):
                                last = nc.tensor.matmul(dst, xT[:, k, cols(t)], wblk[:, j % RING, k],
                                                        start=k == 0, stop=k == KD - 1)
                    last.then_inc(blk_mm, 1)
                n = 0
                for i in range(3):
                    if i < 2:
                        pe.wait_ge(row_in[i], 16)
                    else:
                        pe.wait_ge(small_in, 16)
                    for t in range(NTILE):
                        if n < 2:
                            pe.wait_ge(blk_act, NBLK)
                            pe.wait_ge(blk_dve, NBLK)
                        if n >= 4:
                            pe.wait_ge(row_ev, n - 3)
                        w = wrow[:, i] if i < 2 else wsmall
                        width = 512 if i < 2 else NSMALL
                        for k in range(KD):
                            last = nc.tensor.matmul(bank[n % 4][0:rows(t), 0:width], xT[:, k, cols(t)],
                                                    w[:, k, 0:width], start=k == 0, stop=k == KD - 1)
                        last.then_inc(row_mm, 1)
                        n += 1

            @block.scalar
            def _(act):
                for j in range(NBLK):
                    act.wait_ge(blk_mm, j + 1)
                    big = bank[j % 2]
                    if j < B_Q:
                        dst = c.convin_p[:, j, 3:3 + SEQ]
                    elif j < B_K:
                        dst = c.qT[:, j - B_Q, 0:SEQ]
                    elif j < B_QI:
                        dst = c.kT[:, j - B_K, 0:SEQ]
                    elif j < B_KI:
                        dst = c.qiT[:, j - B_QI, 0:SEQ]
                    else:
                        dst = c.kiT[:, 0:SEQ]
                    nc.scalar.activation(dst, big[:], ACT.Copy).then_inc(blk_act, 1)
                n = 0
                for i in range(3):
                    for t in range(NTILE):
                        act.wait_ge(row_mm, n + 1)
                        dst = (c.z, c.v, c.small)[i]
                        nc.scalar.activation(dst[0:rows(t), t], bank[n % 4][0:rows(t), 0:dst.shape[2]],
                                             ACT.Copy).then_inc(row_ev, 1)
                        n += 1

            @block.vector
            def _(dve):
                nc.vector.memset(c.convin_p[:, :, 0:3], 0.0).then_inc(pad_done, 1)
                for j in range(NBLK):
                    dve.wait_ge(blk_mm, j + 1)
                    little, tall = bank[2 + j % 2], bank[4 + j % 2]
                    if j < B_Q:
                        dve.wait_ge(state_in, 16)
                        dst = c.convin_s[:, j, :, 3:3 + TS]
                    elif j < B_K:
                        dst = c.qT[:, j - B_Q, SEQ:NT]
                    elif j < B_QI:
                        dst = c.kT[:, j - B_K, SEQ:NT]
                    elif j < B_KI:
                        dst = c.qiT[:, j - B_QI, SEQ:NT]
                    else:
                        dst = c.kiT[:, SEQ:NT]
                    src = little[:, 0:NS]
                    if j < B_Q:
                        src = src.rearrange("p (b t) -> p b t", b=NB)
                    last = nc.vector.tensor_copy(dst, src)
                    if j < B_Q:
                        last = nc.vector.tensor_copy(crow[:, j * P:(j + 1) * P], tall[0:NS + 3, 0:P])
                    if B_K <= j < B_QI:
                        if j >= B_K + 2:
                            dve.wait_ge(kst[j % 2], 32)
                        nc.vector.tensor_copy(krow[:, j % 2, 0:STILE],
                                              tall[:].rearrange("p (t n) -> p t n", t=STILE))
                        last = nc.vector.tensor_copy(krow[0:NS, j % 2, STILE], bank[6 + j % 2][0:NS, 0:P])
                    last.then_inc(blk_dve, 1)
                dve.wait_ge(pad_done, 1)

            @block.gpsimd
            def _(pool):
                pool.wait_ge(blk_dve, B_Q)
                pool.dma_start(A["conv_p"][0], crow[0:3, :]).then_inc(store, 16)
                for b in range(NB):
                    pool.dma_start(A["conv_s"][b], crow[3 + TS * b + 1:3 + TS * (b + 1), :]).then_inc(store, 16)
                for j in range(B_K, B_QI):
                    pool.wait_ge(blk_dve, j + 1)
                    o = (j - B_K) * P
                    pool.dma_start(A["k_p"].rearrange("(t p) n -> p t n", p=P)[:, :, o:o + P],
                                   krow[:, j % 2, 0:STILE]).then_inc(kst[j % 2], 16)
                    pool.dma_start(A["k_s"][:, o:o + P], krow[0:NS, j % 2, STILE]).then_inc(kst[j % 2], 16)
                pool.wait_ge(row_ev, NROW)
                pool.dma_start(A["v_p"].rearrange("(t p) n -> p t n", p=P), c.v[:, 0:STILE]).then_inc(store, 16)
                pool.dma_start(A["v_s"], c.v[0:NS, STILE]).then_inc(store, 16)
                pool.dma_start(A["kidx_p"].rearrange("(t p) n -> p t n", p=P),
                               c.small[:, 0:STILE, S_KI:S_KI + HD]).then_inc(store, 16)
                pool.dma_start(A["kidx_s"], c.small[0:NS, STILE, S_KI:S_KI + HD]).then_inc(store, 16)
                pool.wait_ge(store, 16 * (1 + NB + 4))
                pool.wait_ge(kst[0], 64)
                pool.wait_ge(kst[1], 64)


def stage_ssd(c):
    nc, A, bank = c.nc, c.A, c.bank
    with ExitStack() as es:
        def sb(name, shape, dt=F32):
            return es.enter_context(nc.sbuf_tensor(name, shape, dt))
        convw, convb = sb("convw", [P, KD, 4]), sb("convb", [P, KD])
        acc = sb("conv_acc", [P, 2, NT])
        xbcT = sb("xbcT", [P, KD, NT])
        xsN, BN = sb("xsN", [P, 512]), sb("BN", [P, 256])
        dtN, aN = sb("dtN", [P, NTILE, H]), sb("aN", [P, NTILE, H])
        negA = sb("negA", [P, H])
        u, w1, w2 = sb("sp_u", [P, NTILE, H]), sb("sp_1", [P, NTILE, H]), sb("sp_2", [P, NTILE, H])
        aexp = sb("aexp", [P, H, P])
        seg, M = sb("seg", [P, H, P]), sb("Mdecay", [P, H, P])
        Sm = sb("Smask", [P, 2, P])
        acum, last_, dte, ea, edl = (sb(n, [P, H]) for n in ("acum", "alast", "dte", "ea", "edl"))
        xd, xdd, y, t1 = (sb(n, [P, 512]) for n in ("xd", "xdd", "yssd", "yt"))
        hT = sb("stateT", [P, 512])
        rms = sb("rms", [P, 4])
        CTm = sb("CTm", [P, 2, NB, NS])
        stT = sb("stT", [P, NB, 512])
        stN = sb("stN", [P, NB, 4, P])
        aexp64 = sb("aexp64", [NS, H, HD])
        xddm = sb("xddm", [NS, NB, 512])
        eD = sb("eD", [P, 4, NB])
        ssmo = sb("ssmo", [P, 4, P])

        conv_in, st_in = c.sem("ssd_in"), c.sem("state_in")
        conv_done, xbc_ready = c.sem("conv_done"), c.sem("xbc_ready")
        d_own, a_own = c.sem("ssd_dve"), c.sem("ssd_act")
        names = ("dt_pre", "dt_e", "tr_mm", "tr_ev", "a_ready", "cum_mm", "seg_pre", "decay", "ea_pre", "ea_done",
                 "m_ready", "y_mm", "y_done", "sz_done", "rms_pre", "rms_sqrt", "yn_ready", "ynT_mm", "ynT_ev",
                 "xdd_ready", "st_mm", "h_ready", "ho_mm", "ho_ev", "ns_mm", "ns_ev", "eD_mm", "eD_done", "ctm")
        s = {n: c.sem("ssd_" + n) for n in names}
        store = c.sem("ssd_store")
        vec = lambda name, n=P: c.vecs[0:n, VEC[name][0]:VEC[name][0] + VEC[name][1]]

        def by_head(ap, n, width=HD):
            return ap.unsqueeze(2).to_broadcast([n, H, width])

        with nc.Block() as block:
            @block.sync
            def _(sp):
                sp.dma_start(convw[:], A["conv_w"]).then_inc(conv_in, 16)
                sp.dma_start(convb[:], A["conv_b"]).then_inc(conv_in, 16)
                sp.dma_start(stT[:], A["state_ssmT"]).then_inc(st_in, 16)
                sp.dma_start(stN[:], A["state_ssm"]).then_inc(st_in, 16)
                sp.wait_ge(s["ho_ev"], 1)
                sp.dma_start(A["ssm_p"].rearrange("(k p) n -> p k n", p=P), ssmo[:]).then_inc(store, 16)
                sp.wait_ge(s["ns_ev"], NB)
                sp.dma_start(A["ssm_s"].rearrange("b (k p) n -> p b k n", p=P), stN[:]).then_inc(store, 16)
                sp.wait_ge(store, 32)

            @block.tensor
            def _(pe):
                pe.wait_ge(xbc_ready, 2 * KD)
                for t in range(NTILE):
                    n = rows(t)
                    sample = t == STILE
                    tri = c.tri if not sample else c.triS
                    if t:
                        pe.wait_ge(s["ynT_ev"], t)
                        pe.wait_ge(s["y_done"], t)
                        pe.wait_ge(s["h_ready"], t)
                    for k in range(6):
                        dst = bank[0][0:n, k * P:(k + 1) * P] if k < 4 else bank[1][0:n, (k - 4) * P:(k - 3) * P]
                        ins = nc.tensor.transpose(dst, xbcT[:, k, cols(t)], c.ident[:])
                    ins.then_inc(s["tr_mm"], 1)
                    pe.wait_ge(s["a_ready"], t + 1)
                    nc.tensor.matmul(bank[2][0:n, 0:H], tri[0:n, 0:n], aN[0:n, t], start=True, stop=True)
                    nc.tensor.matmul(bank[2][0:n, H:2 * H], c.ones[0:n, 0:n] if not sample else c.onesS[:],
                                     aN[0:n, t], start=True, stop=True)
                    for h in range(H):
                        nc.tensor.matmul(bank[3 + h // 4][0:n, (h % 4) * n:(h % 4 + 1) * n], aexp[0:n, h, 0:n],
                                         tri[0:n, 0:n], start=True, stop=True)
                    for g in range(2):
                        ins = nc.tensor.matmul(bank[5][0:n, g * n:(g + 1) * n], xbcT[:, 4 + g, cols(t)],
                                               xbcT[:, 6 + g, cols(t)], start=True, stop=True)
                    ins.then_inc(s["cum_mm"], 1)
                    pe.wait_ge(s["m_ready"], t + 1)
                    for h in range(H):
                        ins = nc.tensor.matmul(bank[6][0:n, h * HD:(h + 1) * HD], M[0:n, h, 0:n],
                                               xd[0:n, h * HD:(h + 1) * HD], start=True, stop=True)
                    if sample:
                        pe.wait_ge(st_in, 32)
                        pe.wait_ge(s["ctm"], 1)
                        for g in range(2):
                            for b in range(NB):
                                ins = nc.tensor.matmul(bank[7][0:n, g * 256:(g + 1) * 256], CTm[:, g, b],
                                                       stT[:, b, g * 256:(g + 1) * 256],
                                                       start=b == 0, stop=b == NB - 1)
                    elif t:
                        for g in range(2):
                            ins = nc.tensor.matmul(bank[7][0:n, g * 256:(g + 1) * 256], xbcT[:, 6 + g, cols(t)],
                                                   hT[:, g * 256:(g + 1) * 256], start=True, stop=True)
                    ins.then_inc(s["y_mm"], 1)
                    if not sample:
                        pe.wait_ge(s["xdd_ready"], t + 1)
                        for g in range(2):
                            ins = nc.tensor.matmul(bank[0][:, g * 256:(g + 1) * 256], BN[:, g * P:(g + 1) * P],
                                                   xdd[:, g * 256:(g + 1) * 256], start=True, stop=True)
                        ins.then_inc(s["st_mm"], 1)
                    pe.wait_ge(s["yn_ready"], t + 1)
                    for k in range(4):
                        ins = nc.tensor.transpose(bank[1][:, k * n:(k + 1) * n], y[0:n, k * P:(k + 1) * P],
                                                  c.ident[0:n, 0:n])
                    ins.then_inc(s["ynT_mm"], 1)
                pe.wait_ge(s["h_ready"], STILE)
                for k in range(4):
                    ins = nc.tensor.transpose(bank[3][:, k * P:(k + 1) * P], hT[:, k * P:(k + 1) * P], c.ident[:])
                ins.then_inc(s["ho_mm"], 1)
                pe.wait_ge(s["xdd_ready"], NTILE)
                for k in range(4):
                    ins = nc.tensor.matmul(bank[2][:, 64 + k * NB:64 + (k + 1) * NB],
                                           aexp64[:].rearrange("p h d -> p (h d)")[:, k * P:(k + 1) * P],
                                           c.bsel[:], start=True, stop=True)
                ins.then_inc(s["eD_mm"], 1)
                for b in range(NB):
                    if b >= 2:
                        pe.wait_ge(s["ns_ev"], b - 1)
                    for k in range(4):
                        ins = nc.tensor.matmul(bank[4 + b % 2][:, k * P:(k + 1) * P], xddm[:, b, k * P:(k + 1) * P],
                                               BN[0:NS, (k // 2) * P:(k // 2 + 1) * P], start=True, stop=True)
                    ins.then_inc(s["ns_mm"], 1)

            @block.scalar
            def _(act):
                link = Link(act, a_own)
                act.wait_ge(s["dt_pre"], 1)
                link(nc.scalar.activation(negA[:], vec("a_log"), ACT.Exp), s["dt_e"])
                link(nc.scalar.activation(u[:], w1[:], ACT.Exp), s["dt_e"])
                for k in range(KD):
                    act.wait_ge(conv_done, 2 * (k + 1))
                    nc.scalar.activation(xbcT[:, k, 0:SEQ], acc[:, k % 2, 0:SEQ], ACT.Silu,
                                         bias=convb[:, k:k + 1]).then_inc(xbc_ready, 1)
                    nc.scalar.activation(xbcT[:, k, SEQ:NT], acc[:, k % 2, SEQ:NT], ACT.Silu,
                                         bias=convb[:, k:k + 1]).then_inc(xbc_ready, 1)
                for t in range(NTILE):
                    n = rows(t)
                    nc.scalar.activation(c.z[0:n, t], c.z[0:n, t], ACT.Silu).then_inc(s["sz_done"], 1)
                for t in range(NTILE):
                    n = rows(t)
                    act.wait_ge(s["seg_pre"], t + 1)
                    nc.scalar.activation(seg[0:n, :, 0:n], seg[0:n, :, 0:n], ACT.Exp).then_inc(s["decay"], 1)
                    nc.scalar.activation(ea[0:n, :], acum[0:n, :], ACT.Exp).then_inc(s["ea_done"], 1)
                    nc.scalar.activation(dte[0:n, :], dte[0:n, :], ACT.Exp).then_inc(s["ea_done"], 1)
                    nc.scalar.activation(edl[0:n, :], last_[0:n, :], ACT.Exp).then_inc(s["ea_done"], 1)
                    act.wait_ge(s["rms_pre"], t + 1)
                    nc.scalar.activation(rms[0:n, 1:2], rms[0:n, 1:2], ACT.Sqrt).then_inc(s["rms_sqrt"], 1)
                    act.wait_ge(s["ynT_mm"], t + 1)
                    nc.scalar.activation(c.mixedT[:, 0:4, cols(t)],
                                         bank[1][:, 0:4 * n].rearrange("p (k n) -> p k n", k=4),
                                         ACT.Copy).then_inc(s["ynT_ev"], 1)
                act.wait_ge(s["ho_mm"], 1)
                nc.scalar.activation(ssmo[:], bank[3][:].rearrange("p (k n) -> p k n", k=4),
                                     ACT.Copy).then_inc(s["ho_ev"], 1)
                act.wait_ge(s["eD_mm"], 1)
                nc.scalar.activation(eD[:], bank[2][:, 64:64 + 4 * NB].rearrange("p (k b) -> p k b", k=4),
                                     ACT.Exp).then_inc(s["eD_done"], 1)

            @block.vector
            def _(dve):
                V = nc.vector
                link = Link(dve, d_own)
                link(V.memset(aN[:], 0.0))
                for t in range(NTILE):
                    link(V.tensor_tensor(dtN[0:rows(t), t], c.small[0:rows(t), t, S_DT:S_DT + H],
                                         vec("dt_bias", rows(t)), ALU.add))
                link(V.memset(w1[:], 0.0))
                for t in range(NTILE):
                    n = rows(t)
                    link(V.tensor_scalar(w1[0:n, t], dtN[0:n, t], -1.0, None, ALU.mult))
                    link(V.tensor_tensor(w1[0:n, t], w1[0:n, t], dtN[0:n, t], ALU.min),
                         s["dt_pre"] if t == STILE else None)
                dve.wait_ge(s["dt_e"], 2)
                link(V.tensor_scalar(negA[:], negA[:], -1.0, None, ALU.mult))
                link(V.tensor_scalar(w1[:], u[:], 2.0, None, ALU.add))
                link(V.reciprocal(w1[:], w1[:]))
                link(V.tensor_tensor(u[:], u[:], w1[:], ALU.mult))
                link(V.tensor_tensor(w1[:], u[:], u[:], ALU.mult))
                link(V.tensor_scalar(w2[:], w1[:], 1 / 19, 1 / 17, ALU.mult, ALU.add))
                for q in (15, 13, 11, 9, 7, 5, 3, 1):
                    link(V.tensor_tensor(w2[:], w2[:], w1[:], ALU.mult))
                    link(V.tensor_scalar(w2[:], w2[:], 1 / q, None, ALU.add))
                link(V.tensor_tensor(w2[:], w2[:], u[:], ALU.mult))
                for t in range(NTILE):
                    n = rows(t)
                    link(V.tensor_scalar(dtN[0:n, t], dtN[0:n, t], 0.0, None, ALU.max))
                    link(V.scalar_tensor_tensor(dtN[0:n, t], w2[0:n, t], 2.0, dtN[0:n, t], ALU.mult, ALU.add))
                    link(V.tensor_tensor(aN[0:n, t], dtN[0:n, t], negA[0:n, :], ALU.mult))
                dve.wait_ge(conv_in, 32)
                for k in range(KD):
                    if k >= 2:
                        dve.wait_ge(xbc_ready, 2 * (k - 1))
                    ap = acc[:, k % 2, 0:SEQ]
                    as_ = acc[:, k % 2, SEQ:NT].rearrange("p (b t) -> p b t", b=NB)
                    for tap in range(4):
                        w = convw[:, k, tap:tap + 1]
                        sem = conv_done if tap == 3 else None
                        xp, xs = c.convin_p[:, k, tap:tap + SEQ], c.convin_s[:, k, :, tap:tap + TS]
                        if tap == 0:
                            link(V.tensor_scalar(ap, xp, w, None, ALU.mult))
                            link(V.tensor_scalar(as_, xs, w, None, ALU.mult))
                        else:
                            link(V.scalar_tensor_tensor(ap, xp, w, ap, ALU.mult, ALU.add), sem)
                            link(V.scalar_tensor_tensor(as_, xs, w, as_, ALU.mult, ALU.add), sem)
                dve.wait_ge(xbc_ready, 2 * KD)
                for g in range(2):
                    link(V.tensor_tensor(CTm[:, g], xbcT[:, 6 + g, SEQ:NT].unsqueeze(1).to_broadcast([P, NB, NS]),
                                         c.bcol[:], ALU.mult), s["ctm"] if g else None)
                for t in range(NTILE):
                    n = rows(t)
                    sample = t == STILE
                    hd = lambda ap: ap[0:n, :].rearrange("p (h d) -> p h d", h=H)
                    if t:
                        dve.wait_ge(s["cum_mm"], t)
                        dve.wait_ge(s["st_mm"], t)
                    link(V.tensor_copy(aexp[0:n, :, 0:n], by_head(aN[0:n, t], n, n)), s["a_ready"])
                    dve.wait_ge(s["tr_mm"], t + 1)
                    link(V.tensor_copy(xsN[0:n, :], bank[0][0:n, :]))
                    link(V.tensor_copy(BN[0:n, :], bank[1][0:n, 0:256]))
                    if t:
                        dve.wait_ge(s["y_mm"], t)
                    link(V.tensor_tensor(hd(xd), hd(xsN), by_head(dtN[0:n, t], n), ALU.mult))
                    dve.wait_ge(s["cum_mm"], t + 1)
                    link(V.tensor_copy(acum[0:n, :], bank[2][0:n, 0:H]))
                    link(V.tensor_copy(last_[0:n, :], bank[2][0:n, H:2 * H]))
                    link(V.tensor_tensor(dte[0:n, :], last_[0:n, :], acum[0:n, :], ALU.subtract))
                    for q in range(2):
                        link(V.tensor_tensor(seg[0:n, 4 * q:4 * q + 4, 0:n],
                                             bank[3 + q][0:n, 0:4 * n].rearrange("p (h i) -> p h i", h=4),
                                             acum[0:n, 4 * q:4 * q + 4].unsqueeze(2).to_broadcast([n, 4, n]),
                                             ALU.subtract))
                    link(V.tensor_scalar(seg[0:n, :, 0:n], seg[0:n, :, 0:n], 0.0, None, ALU.min), s["seg_pre"])
                    tri = c.tri[0:n, 0:n] if not sample else c.triS[:]
                    link(V.tensor_tensor(Sm[0:n, :, 0:n], bank[5][0:n, 0:2 * n].rearrange("p (g i) -> p g i", g=2),
                                         tri.unsqueeze(1).to_broadcast([n, 2, n]), ALU.mult))
                    dve.wait_ge(s["decay"], t + 1)
                    for g in range(2):
                        link(V.tensor_tensor(M[0:n, 4 * g:4 * g + 4, 0:n], seg[0:n, 4 * g:4 * g + 4, 0:n],
                                             Sm[0:n, g, 0:n].unsqueeze(1).to_broadcast([n, 4, n]), ALU.mult),
                             s["m_ready"] if g else None)
                    dve.wait_ge(s["ea_done"], 3 * (t + 1))
                    link(V.tensor_tensor(hd(xdd), hd(xd), by_head(dte[0:n, :], n), ALU.mult),
                         s["xdd_ready"] if not sample else None)
                    if t:
                        dve.wait_ge(s["ynT_mm"], t)
                    link(V.tensor_tensor(hd(y), hd(xsN), by_head(vec("d_skip", n), n), ALU.mult))
                    dve.wait_ge(s["y_mm"], t + 1)
                    if t:
                        link(V.tensor_tensor(hd(t1), hd(bank[7]), by_head(ea[0:n, :], n), ALU.mult))
                        link(V.tensor_tensor(y[0:n, :], y[0:n, :], t1[0:n, :], ALU.add))
                    link(V.tensor_tensor(y[0:n, :], y[0:n, :], bank[6][0:n, :], ALU.add), s["y_done"])
                    if not sample:
                        dve.wait_ge(s["st_mm"], t + 1)
                        if t:
                            link(V.tensor_tensor(hd(hT), hd(hT), by_head(edl[:], P), ALU.mult))
                            link(V.tensor_tensor(hT[:], hT[:], bank[0][:], ALU.add), s["h_ready"])
                        else:
                            link(V.tensor_copy(hT[:], bank[0][:]), s["h_ready"])
                    dve.wait_ge(s["sz_done"], t + 1)
                    link(V.tensor_tensor(y[0:n, :], y[0:n, :], c.z[0:n, t], ALU.mult))
                    link(V.tensor_tensor_reduce(out=t1[0:n, :], in0=y[0:n, :], in1=y[0:n, :], scale=1.0, scalar=0.0,
                                                op0=ALU.mult, op1=ALU.add, accum_out=rms[0:n, 0:1]))
                    link(V.tensor_scalar(rms[0:n, 1:2], rms[0:n, 0:1], 1 / 512, EPS, ALU.mult, ALU.add), s["rms_pre"])
                    dve.wait_ge(s["rms_sqrt"], t + 1)
                    link(V.reciprocal(rms[0:n, 2:3], rms[0:n, 1:2]))
                    link(V.scalar_tensor_tensor(y[0:n, :], y[0:n, :], rms[0:n, 2:3], vec("ssd_norm_w", n),
                                                ALU.mult, ALU.mult), s["yn_ready"])
                link(V.tensor_copy(aexp64[:], by_head(aN[0:NS, STILE], NS)))
                for b in range(NB):
                    link(V.tensor_scalar(xddm[:, b], xdd[0:NS, :], c.bsel[:, b:b + 1], None, ALU.mult),
                         s["xdd_ready"] if b == NB - 1 else None)
                dve.wait_ge(s["eD_done"], 1)
                for b in range(NB):
                    dve.wait_ge(s["ns_mm"], b + 1)
                    for k in range(4):
                        link(V.scalar_tensor_tensor(stN[:, b, k], stN[:, b, k], eD[:, k, b:b + 1],
                                                    bank[4 + b % 2][:, k * P:(k + 1) * P], ALU.mult, ALU.add),
                             s["ns_ev"] if k == 3 else None)


def stage_dsa_prompt(c):
    nc, A, bank = c.nc, c.A, c.bank
    NTP = SEQ // P
    BW = 2 * P
    topk = min(256, SEQ // 4)
    with ExitStack() as es:
        def sb(name, shape, dt=F32):
            return es.enter_context(nc.sbuf_tensor(name, shape, dt))
        relb = sb("relb", [NBUCKET, H])
        relx = sb("relx", [NBUCKET, H, P])
        onehot = sb("onehot", [NBUCKET, 3 * P])
        spread = sb("spread", [P, H, 3 * P])
        T = sb("Tbias", [P, H, BW])
        relu = sb("relu", [P, 2, SEQ])
        sc = sb("scores", [P, SEQ])
        wi = sb("wi", [P, H])
        m8 = sb("max8", [P, 8])
        msk = sb("mask", [P, 2, SEQ])
        L = sb("logits", [P, 2, SEQ])
        E = sb("probs", [P, 2, SEQ])
        PT = sb("probsT", [P, 2, NTP, P])
        mx, den, rden = sb("mx", [P, H]), sb("den", [P, H]), sb("rden", [P, H])
        o = sb("att", [P, 512])
        scratch = nc.dram_tensor("bias_scratch", [P, H * 3 * P], F32, kind="Internal").ap()

        names = ("in", "relx", "sp_mm", "sp_ev", "sp_st", "T_in", "idx_mm", "relu", "relu_used", "mask",
                 "qk_mm", "logit", "exp", "tr_mm", "pt", "pv_mm", "att", "attT_mm", "attT")
        s = {n: c.sem("dsap_" + n) for n in names}
        d_own = c.sem("dsap_dve")

        with nc.Block() as block:
            @block.sync
            def _(sp):
                sp.dma_start(relb[:], A["rel_bias"]).then_inc(s["in"], 16)
                sp.dma_start(onehot[:], A["bucket_rev"]).then_inc(s["in"], 16)
                sp.wait_ge(s["sp_ev"], H)
                sp.dma_start(scratch[:, :], spread[:].rearrange("p h m -> p (h m)")).then_inc(s["sp_st"], 16)
                sp.wait_ge(s["sp_st"], 16)
                skew = bass.AP(scratch.tensor, P - 1, [[H * 3 * P - 1, P], [3 * P, H], [1, BW]])
                sp.dma_start(T[:], skew).then_inc(s["T_in"], 16)
                sp.wait_ge(s["T_in"], 16)

            @block.tensor
            def _(pe):
                pe.wait_ge(s["in"], 32)
                pe.wait_ge(s["relx"], 1)
                for h in range(H):
                    if h >= 2:
                        pe.wait_ge(s["sp_ev"], h - 1)
                    nc.tensor.matmul(bank[h % 2][:, 0:3 * P], relx[:, h], onehot[:], start=True,
                                     stop=True).then_inc(s["sp_mm"], 1)
                pe.wait_ge(s["sp_ev"], H)

                def scores(t):
                    nk = (t + 1) * P
                    for h in range(H):
                        n = t * H + h
                        if n >= 2:
                            pe.wait_ge(s["relu"], n - 1)
                        lo = HD * (h % 2)
                        nc.tensor.matmul(bank[h % 2][:, 0:nk], c.qiT[lo:lo + HD, h // 2, cols(t)],
                                         c.kiT[lo:lo + HD, 0:nk], start=True, stop=True).then_inc(s["idx_mm"], 1)

                def attend(t):
                    nk = (t + 1) * P

                    def tail(h):
                        n = t * H + h
                        pe.wait_ge(s["exp"], n + 1)
                        if n >= 2:
                            pe.wait_ge(s["pt"], n - 1)
                        for k in range(t + 1):
                            ins = nc.tensor.transpose(bank[4 + h % 2][:, k * P:(k + 1) * P],
                                                      E[:, h % 2, k * P:(k + 1) * P], c.ident[:])
                        ins.then_inc(s["tr_mm"], 1)
                        pe.wait_ge(s["pt"], n + 1)
                        for k in range(t + 1):
                            ins = nc.tensor.matmul(bank[6][:, h * HD:(h + 1) * HD], PT[:, h % 2, k],
                                                   c.v[:, k, h * HD:(h + 1) * HD], start=k == 0, stop=k == t)
                        ins.then_inc(s["pv_mm"], 1)

                    for h in range(H):
                        n = t * H + h
                        if n >= 2:
                            pe.wait_ge(s["logit"], n - 1)
                        lo = HD * (h % 2)
                        nc.tensor.matmul(bank[2 + h % 2][:, 0:nk], c.qT[lo:lo + HD, h // 2, cols(t)],
                                         c.kT[lo:lo + HD, h // 2, 0:nk], start=True, stop=True).then_inc(s["qk_mm"], 1)
                        if h == 0 and t:
                            pe.wait_ge(s["att"], t)
                        if h:
                            tail(h - 1)
                    tail(H - 1)
                    pe.wait_ge(s["att"], t + 1)
                    if t:
                        pe.wait_ge(s["attT"], t)
                    for k in range(4):
                        ins = nc.tensor.transpose(bank[7][:, k * P:(k + 1) * P], o[:, k * P:(k + 1) * P], c.ident[:])
                    ins.then_inc(s["attT_mm"], 1)

                scores(0)
                for t in range(NTP):
                    if t + 1 < NTP:
                        scores(t + 1)
                    attend(t)

            @block.scalar
            def _(act):
                def relus(t):
                    nk = (t + 1) * P
                    for h in range(H):
                        n = t * H + h
                        act.wait_ge(s["idx_mm"], n + 1)
                        if n >= 2:
                            act.wait_ge(s["relu_used"], n - 1)
                        nc.scalar.activation(relu[:, h % 2, 0:nk], bank[h % 2][:, 0:nk], ACT.Relu,
                                             scale=HD ** -0.5).then_inc(s["relu"], 1)

                def attend(t):
                    nk = (t + 1) * P
                    for h in range(H):
                        n = t * H + h
                        act.wait_ge(s["logit"], n + 1)
                        if n >= 2:
                            act.wait_ge(s["tr_mm"], n - 1)
                        nc.scalar.activation(E[:, h % 2, 0:nk], L[:, h % 2, 0:nk], ACT.Exp, bias=mx[:, h:h + 1],
                                             accum_out=den[:, h:h + 1]).then_inc(s["exp"], 1)
                        act.wait_ge(s["tr_mm"], n + 1)
                        if n >= 2:
                            act.wait_ge(s["pv_mm"], n - 1)
                        nc.scalar.activation(PT[:, h % 2, 0:t + 1], bank[4 + h % 2][:, 0:nk].rearrange(
                            "p (k q) -> p k q", q=P), ACT.Copy).then_inc(s["pt"], 1)
                    act.wait_ge(s["attT_mm"], t + 1)
                    nc.scalar.activation(c.mixedT[:, 4:8, cols(t)], bank[7][:].rearrange("p (k q) -> p k q", k=4),
                                         ACT.Copy).then_inc(s["attT"], 1)

                relus(0)
                for t in range(NTP):
                    if t + 1 < NTP:
                        relus(t + 1)
                    attend(t)

            @block.vector
            def _(dve):
                V = nc.vector
                link = Link(dve, d_own)
                dve.wait_ge(s["in"], 32)
                link(V.tensor_copy(relx[:], relb[:].unsqueeze(2).to_broadcast([NBUCKET, H, P])), s["relx"])
                for h in range(H):
                    dve.wait_ge(s["sp_mm"], h + 1)
                    link(V.tensor_copy(spread[:, h], bank[h % 2][:, 0:3 * P]), s["sp_ev"])

                def select(t):
                    nk = (t + 1) * P
                    link(V.tensor_scalar(wi[:], c.small[:, t, S_WI:S_WI + H], H ** -0.5, None, ALU.mult))
                    for h in range(H):
                        dve.wait_ge(s["relu"], t * H + h + 1)
                        if h == 0:
                            link(V.tensor_scalar(sc[:, 0:nk], relu[:, 0, 0:nk], wi[:, 0:1], None, ALU.mult),
                                 s["relu_used"])
                        else:
                            link(V.scalar_tensor_tensor(sc[:, 0:nk], relu[:, h % 2, 0:nk], wi[:, h:h + 1],
                                                        sc[:, 0:nk], ALU.mult, ALU.add), s["relu_used"])
                    own = sc[:, t * P:nk]
                    link(V.tensor_tensor(own, own, c.low[:], ALU.mult))
                    link(V.tensor_tensor(own, own, c.lowneg[:], ALU.add))
                    if nk > topk:
                        for _ in range(topk // 8):
                            link(V.max(m8[:], sc[:, 0:nk]))
                            link(V.match_replace(sc[:, 0:nk], m8[:], sc[:, 0:nk], PICKED))
                        link(V.tensor_scalar(msk[:, t % 2, 0:nk], sc[:, 0:nk], -2.9e38, NOT_SELECTED, ALU.is_gt,
                                             ALU.mult))
                    else:
                        link(V.tensor_scalar(msk[:, t % 2, 0:nk], sc[:, 0:nk], -1.9e38, NOT_SELECTED, ALU.is_lt,
                                             ALU.mult))

                def attend(t):
                    nk = (t + 1) * P
                    far = max(0, nk - BW)
                    for h in range(H):
                        n = t * H + h
                        dve.wait_ge(s["qk_mm"], n + 1)
                        if n >= 2:
                            dve.wait_ge(s["exp"], n - 1)
                        ps, l = bank[2 + h % 2], L[:, h % 2]
                        a = VEC["bias_far"][0] + h
                        if far:
                            link(V.tensor_scalar(l[:, 0:far], ps[:, 0:far], HD ** -0.5, c.vecs[:, a:a + 1],
                                                 ALU.mult, ALU.add))
                        link(V.scalar_tensor_tensor(l[:, far:nk], ps[:, far:nk], HD ** -0.5,
                                                    T[:, h, BW - (nk - far):BW], ALU.mult, ALU.add))
                        link(V.tensor_tensor(l[:, 0:nk], l[:, 0:nk], msk[:, t % 2, 0:nk], ALU.add))
                        if t:
                            dve.wait_ge(s["exp"], t * H)
                        link(V.reduce_max(mx[:, h:h + 1], l[:, 0:nk], AX_X))
                        link(V.tensor_scalar(mx[:, h:h + 1], mx[:, h:h + 1], -1.0, None, ALU.mult), s["logit"])
                    dve.wait_ge(s["exp"], (t + 1) * H)
                    link(V.reciprocal(rden[:], den[:]))
                    dve.wait_ge(s["pv_mm"], (t + 1) * H)
                    if t:
                        dve.wait_ge(s["attT_mm"], t)
                    link(V.tensor_tensor(o[:].rearrange("p (h d) -> p h d", h=H),
                                         bank[6][:].rearrange("p (h d) -> p h d", h=H),
                                         rden[:].unsqueeze(2).to_broadcast([P, H, HD]), ALU.mult), s["att"])

                select(0)
                dve.wait_ge(s["T_in"], 16)
                for t in range(NTP):
                    if t + 1 < NTP:
                        select(t + 1)
                    attend(t)


def stage_dsa_sample(c):
    nc, A, bank = c.nc, c.A, c.bank
    HT = H * TS
    HB = NB // 2
    NKC = PAST // 512
    topk = min(256, (PAST + TS) // 4)
    UP = 512 // PAGE
    RING = 6
    with ExitStack() as es:
        def sb(name, shape, dt=F32):
            return es.enter_context(nc.sbuf_tensor(name, shape, dt))
        pt = sb("ptab", [1, NB * NPAGE], I32)
        kiS = sb("kiS", [HD, 2, PAST])
        qiS = sb("qiS", [HD, NB, H, TS])
        odd = sb("qi_odd", [HD, 4, NS])
        wv = sb("wv", [HT, NB])
        wx = sb("wx", [NS, H, TS])
        tsel = sb("tsel", [NS, TS])
        Wsel = sb("Wsel", [HT, NB, NS])
        Pm = sb("PmS", [P, NKEY])
        rS = Pm[0:HT, :]
        sc = sb("scS", [NS, NKEY])
        m8 = sb("m8S", [NS, 8])
        msk = sb("mskS", [NS, NKEY])
        relb = sb("relbS", [NBUCKET, H])
        RB = sb("RB", [NBUCKET, TS, HB, H, TS])
        oh = sb("ohS", [NBUCKET, PAST + TS])
        ohn = sb("ohn", [NBUCKET, TS, NS])
        exp_rows = sb("exp_rows", [NS, 2, P])
        hmask = sb("hmask", [P, 4, H])
        omask = sb("omask", [HT, 512])
        tsum = sb("tsum", [HT, TS])
        wmask = sb("wmask", [HT, NB, NS])
        Q = sb("Qblk", [P, HB, 4, P])
        ring = sb("kvring", [P, RING, UP * 512])
        PT = sb("PTS", [P, NPAGE + 1, P])
        mx, ngm, den, dsum, rden = sb("mxS", [P, NKC + 1]), sb("ngm", [P, 1]), sb("denS", [P, NKC + 1]), \
            sb("dsum", [P, 1]), sb("rdenS", [P, 1])
        Om = sb("Om", [HT, 2, 512])

        names = ("pt_in", "c_in", "odd_in", "wx", "wv_mm", "ki_in0", "ki_in1", "q_ready", "w_ready", "idx_mm", "relu",
                 "sel_mm", "sc_ready", "mask", "rb", "qblk", "log_mm", "max", "exp", "prob", "tr_mm", "pt",
                 "pv_mm", "om", "ot_mm", "ot", "half")
        s = {n: c.sem("dsas_" + n, n == "odd_in") for n in names}
        kv_in = [c.sem(f"kv_in{i}") for i in range(RING)]
        kv_used = c.sem("kv_used")
        d_own, a_own = c.sem("dsas_dve"), c.sem("dsas_act")

        def unit(g, kind, b, q):
            return ((g * 2 + kind) * HB + b) * NKC + q

        with nc.Block() as block:
            @block.sync
            def _(sp):
                for dst, src in ((relb, "rel_bias"), (oh, "bucket_past"), (ohn, "bucket_new"),
                                 (exp_rows, "expand_rows"), (hmask, "head_mask"), (omask, "out_mask"),
                                 (tsel, "t_sel"), (tsum, "t_sum"), (wmask, "w_mask")):
                    sp.dma_start(dst[:], A[src]).then_inc(s["c_in"], 16)
                sp.dma_start(pt[:], A["page_table"]).then_inc(s["pt_in"], 16)
                sp.wait_ge(s["pt_in"], 16)
                for b in range(NB):
                    if b >= 2:
                        sp.wait_ge(s["idx_mm"], (NKC + 1) * (b - 1))
                    for j in range(NPAGE):
                        page = sp.value_load(pt[0:1, b * NPAGE + j:b * NPAGE + j + 1], min_val=0,
                                             max_val=A["kidxT"].shape[0] - 1)
                        sp.dma_start(kiS[:, b % 2, j * PAGE:(j + 1) * PAGE],
                                     A["kidxT"][bass.ds(page, 1)].rearrange("a d n -> d (a n)")
                                     ).then_inc(s[f"ki_in{b % 2}"], 16)
                n = 0
                for g in range(2):
                    for src in (A["kT_pages"], A["v_pages"]):
                        for at in range(g * HB * NPAGE, (g + 1) * HB * NPAGE, UP):
                            if n >= RING:
                                sp.wait_ge(kv_used, n - RING + 1)
                            for j in range(UP):
                                page = sp.value_load(pt[0:1, at + j:at + j + 1], min_val=0,
                                                     max_val=src.shape[0] - 1)
                                sp.dma_start(ring[:, n % RING, j * 512:(j + 1) * 512],
                                             src[bass.ds(page, 1)].rearrange("a p n -> p (a n)")
                                             ).then_inc(kv_in[n % RING], 16)
                            n += 1

            @block.gpsimd
            def _(pool):
                pool.dma_start(odd[:], c.qiT[HD:P, :, SEQ:NT]).then_inc(s["odd_in"], 16)
                pool.wait_ge(s["odd_in"], 16)

            @block.scalar
            def _(act):
                for b in range(NB):
                    for q in range(NKC + 1):
                        n = b * (NKC + 1) + q
                        act.wait_ge(s["idx_mm"], n + 1)
                        if b and q == 0:
                            act.wait_ge(s["sel_mm"], b)
                        w = 512 if q < NKC else NS
                        nc.scalar.activation(rS[:, q * 512:q * 512 + w], bank[4 + q % 3][0:HT, 0:w],
                                             ACT.Relu, scale=HD ** -0.5).then_inc(s["relu"], 1)
                for q in range(NKC + 1):
                    w = 512 if q < NKC else NS
                    src = bank[q] if q < NKC else bank[7]
                    if q == 0:
                        act.wait_ge(s["sel_mm"], NB)
                    nc.scalar.activation(sc[:, q * 512:q * 512 + w], src[0:NS, 0:w], ACT.Copy
                                         ).then_inc(s["sc_ready"], 1)
                for g in range(2):
                    act.wait_ge(s["max"], g + 1)
                    if g:
                        act.wait_ge(s["tr_mm"], 5 * g)
                    for q in range(NKC + 1):
                        w = 512 if q < NKC else NS
                        nc.scalar.activation(Pm[:, q * 512:q * 512 + w], bank[q][:, 0:w], ACT.Exp, bias=ngm[:, 0:1],
                                             accum_out=den[:, q:q + 1]).then_inc(s["exp"], 1)
                    for q in range(5):
                        act.wait_ge(s["tr_mm"], 5 * g + q + 1)
                        if g and q == 0:
                            act.wait_ge(s["pv_mm"], HB * g)
                        if q < 4:
                            nc.scalar.activation(PT[:, 4 * q:4 * q + 4],
                                                 bank[5 + q % 2][:].rearrange("p (k r) -> p k r", k=4),
                                                 ACT.Copy).then_inc(s["pt"], 1)
                        else:
                            nc.scalar.activation(PT[0:NS, NPAGE], bank[5 + q % 2][0:NS, 0:P], ACT.Copy
                                                 ).then_inc(s["pt"], 1)
                    act.wait_ge(s["ot_mm"], HB * (g + 1))
                    nc.scalar.activation(c.mixedT[:, 4:8, SEQ + HB * TS * g:SEQ + HB * TS * (g + 1)],
                                         bank[7][:, 128:128 + 4 * HB * TS].rearrange("p (k r) -> p k r", k=4),
                                         ACT.Copy).then_inc(s["ot"], 1)

            @block.tensor
            def _(pe):
                pe.wait_ge(s["wx"], 1)
                nc.tensor.matmul(bank[7][0:HT, 0:NB], wx[:].rearrange("r h t -> r (h t)"), c.bsel[:], start=True,
                                 stop=True).then_inc(s["wv_mm"], 1)
                pe.wait_ge(s["q_ready"], 1)
                pe.wait_ge(s["w_ready"], 1)
                for b in range(NB):
                    pe.wait_ge(s[f"ki_in{b % 2}"], 16 * NPAGE * (b // 2 + 1))
                    lhsT = qiS[:, b].rearrange("d h t -> d (h t)")
                    for q in range(NKC + 1):
                        n = b * (NKC + 1) + q
                        if q >= 3:
                            pe.wait_ge(s["relu"], n - 2)
                        elif b:
                            pe.wait_ge(s["relu"], b * (NKC + 1))
                        w, rhs = (512, kiS[:, b % 2, q * 512:(q + 1) * 512]) if q < NKC else (
                            NS, c.kiT[0:HD, SEQ:NT])
                        nc.tensor.matmul(bank[4 + q % 3][0:HT, 0:w], lhsT, rhs, start=True,
                                         stop=True).then_inc(s["idx_mm"], 1)
                    for q in range(NKC + 1):
                        pe.wait_ge(s["relu"], b * (NKC + 1) + q + 1)
                        w = 512 if q < NKC else NS
                        ins = nc.tensor.matmul(bank[q if q < NKC else 7][0:NS, 0:w], Wsel[:, b],
                                               rS[:, q * 512:q * 512 + w], start=b == 0, stop=b == NB - 1)
                    ins.then_inc(s["sel_mm"], 1)

                for g in range(2):
                    if g == 0:
                        pe.wait_ge(s["mask"], 1)
                        pe.wait_ge(s["rb"], 1)
                    pe.wait_ge(s["qblk"], g + 1)
                    if g:
                        pe.wait_ge(s["exp"], 5 * g)
                    for q in range(NKC + 1):
                        w = 512 if q < NKC else NS
                        nc.tensor.matmul(bank[q][:, 0:w], exp_rows[:, g], msk[:, q * 512:q * 512 + w],
                                         start=True, stop=False)
                        for t in range(TS):
                            rhs = oh[:, q * 512 + TS - 1 - t:q * 512 + TS - 1 - t + 512] if q < NKC else ohn[:, t]
                            nc.tensor.matmul(bank[q][:, 0:w], RB[:, t].rearrange("k b h t -> k (b h t)"), rhs,
                                             start=False, stop=False)
                    for b in range(HB):
                        for q in range(NKC):
                            n = unit(g, 0, b, q)
                            pe.wait_ge(kv_in[n % RING], 16 * UP * (n // RING + 1))
                            kk = ring[:, n % RING].rearrange("p (j k n) -> p k j n", j=UP, k=4)
                            for k in range(4):
                                ins = nc.tensor.matmul(bank[q][:], Q[:, b, k], kk[:, k], start=False,
                                                       stop=b == HB - 1 and k == 3)
                            ins.then_inc(kv_used, 1)
                        for k in range(4):
                            ins = nc.tensor.matmul(bank[NKC][:, 0:NS], Q[:, b, k], c.kT[:, k, SEQ:NT], start=False,
                                                   stop=b == HB - 1 and k == 3)
                    ins.then_inc(s["log_mm"], 1)
                    pe.wait_ge(s["prob"], g + 1)
                    for q in range(5):
                        if q >= 2:
                            pe.wait_ge(s["pt"], 5 * g + q - 1)
                        for k in range(4 * q, min(4 * q + 4, NPAGE + 1)):
                            m = P if k < NPAGE else NS
                            ins = nc.tensor.transpose(bank[5 + q % 2][0:m, (k % 4) * P:(k % 4 + 1) * P],
                                                      Pm[:, k * P:k * P + m], c.ident[:])
                        ins.then_inc(s["tr_mm"], 1)
                    pe.wait_ge(s["pt"], 5 * (g + 1))

                    def out_T(b):
                        pe.wait_ge(s["om"], g * HB + b + 1)
                        for k in range(4):
                            at = 128 + k * HB * TS + b * TS
                            ins = nc.tensor.matmul(bank[7][:, at:at + TS], Om[:, b % 2, k * P:(k + 1) * P], tsum[:],
                                                   start=True, stop=True)
                        ins.then_inc(s["ot_mm"], 1)

                    for b in range(HB):
                        n0 = g * HB + b
                        if n0 >= 2:
                            pe.wait_ge(s["om"], n0 - 1)
                        for q in range(NKC):
                            n = unit(g, 1, b, q)
                            pe.wait_ge(kv_in[n % RING], 16 * UP * (n // RING + 1))
                            for j in range(UP):
                                ins = nc.tensor.matmul(bank[5 + b % 2][0:HT, :],
                                                       PT[:, q * UP + j, b * HT:(b + 1) * HT],
                                                       ring[:, n % RING, j * 512:(j + 1) * 512],
                                                       start=q == 0 and j == 0, stop=False)
                            ins.then_inc(kv_used, 1)
                        nc.tensor.matmul(bank[5 + b % 2][0:HT, :], PT[0:NS, NPAGE, b * HT:(b + 1) * HT],
                                         c.v[0:NS, STILE], start=False, stop=True).then_inc(s["pv_mm"], 1)
                        if b == 0 and g:
                            pe.wait_ge(s["ot"], g)
                        if b:
                            out_T(b - 1)
                    out_T(HB - 1)

            @block.vector
            def _(dve):
                V = nc.vector
                link = Link(dve, d_own)
                dve.wait_ge(s["c_in"], 16 * 9)
                dve.wait_ge(s["odd_in"], 16)
                qi = qiS[:].rearrange("d b (k two) t -> d two k b t", two=2)
                for k in range(4):
                    link(V.tensor_copy(qi[:, 0, k], c.qiT[0:HD, k, SEQ:NT].rearrange("d (b t) -> d b t", b=NB)))
                    link(V.tensor_copy(qi[:, 1, k], odd[:, k].rearrange("d (b t) -> d b t", b=NB)),
                         s["q_ready"] if k == 3 else None)
                link(V.tensor_tensor(wx[:], c.small[0:NS, STILE, S_WI:S_WI + H].unsqueeze(2).to_broadcast([NS, H, TS]),
                                     tsel[:].unsqueeze(1).to_broadcast([NS, H, TS]), ALU.mult), s["wx"])
                dve.wait_ge(s["wv_mm"], 1)
                link(V.tensor_scalar(wv[:], bank[7][0:HT, 0:NB], H ** -0.5, None, ALU.mult))
                link(V.tensor_tensor(Wsel[:], wmask[:], wv[:].unsqueeze(2).to_broadcast([HT, NB, NS]), ALU.mult),
                     s["w_ready"])
                link(V.memset(RB[:], 0.0))
                for t in range(TS):
                    link(V.tensor_copy(RB[:, t, :, :, t], relb[:].unsqueeze(1).to_broadcast([NBUCKET, HB, H])),
                         s["rb"] if t == TS - 1 else None)
                dve.wait_ge(s["sc_ready"], NKC + 1)
                new = sc[:, PAST:NKEY]
                link(V.tensor_tensor(new, new, c.lowS[:], ALU.mult))
                link(V.tensor_tensor(new, new, c.lowSneg[:], ALU.add))
                for _ in range(topk // 8):
                    link(V.max(m8[:], sc[:]))
                    link(V.match_replace(sc[:], m8[:], sc[:], PICKED))
                link(V.tensor_scalar(msk[:], sc[:], -2.9e38, NOT_SELECTED, ALU.is_gt, ALU.mult), s["mask"])
                for g in range(2):
                    if g:
                        dve.wait_ge(s["log_mm"], g)
                    link(V.memset(Q[:], 0.0))
                    for b in range(HB):
                        own = Q[:, b, :, b * HT:(b + 1) * HT].rearrange("p k (h t) -> p k h t", t=TS)
                        at = SEQ + (g * HB + b) * TS
                        for k in range(4):
                            link(V.tensor_tensor(own[:, k],
                                                 c.qT[:, k, at:at + TS].unsqueeze(1).to_broadcast([P, H, TS]),
                                                 hmask[:, k].unsqueeze(2).to_broadcast([P, H, TS]), ALU.mult),
                                 s["qblk"] if b == HB - 1 and k == 3 else None)
                    dve.wait_ge(s["log_mm"], g + 1)
                    for q in range(NKC + 1):
                        link(V.reduce_max(mx[:, q:q + 1], bank[q][:, 0:512 if q < NKC else NS], AX_X))
                    link(V.reduce_max(ngm[:], mx[:], AX_X))
                    link(V.tensor_scalar(ngm[:], ngm[:], -1.0, None, ALU.mult), s["max"])
                    dve.wait_ge(s["exp"], 5 * (g + 1))
                    link(V.reduce_sum(dsum[:], den[:], AX_X))
                    link(V.reciprocal(rden[:], dsum[:]))
                    link(V.tensor_scalar(Pm[:], Pm[:], rden[:, 0:1], None, ALU.mult), s["prob"])
                    for b in range(HB):
                        n0 = g * HB + b
                        dve.wait_ge(s["pv_mm"], n0 + 1)
                        if n0 >= 2:
                            dve.wait_ge(s["ot_mm"], n0 - 1)
                        link(V.tensor_tensor(Om[:, b % 2], bank[5 + b % 2][0:HT, :], omask[:], ALU.mult), s["om"])


def layer_norm(c, link, r, mv, n, gb, out, pre, sqrt_done, count, done):
    V = c.nc.vector
    for q in range(2):
        link(V.bn_stats(mv[0:n, 6 * q:6 * q + 6], r[0:n, q * 512:(q + 1) * 512]))
    link(V.bn_aggr(mv[0:n, 12:14], mv[0:n, 0:12]))
    link(V.tensor_scalar(mv[0:n, 14:15], mv[0:n, 13:14], EPS, None, ALU.add), pre)
    link.eng.wait_ge(sqrt_done, count)
    link(V.reciprocal(mv[0:n, 15:16], mv[0:n, 14:15]))
    link(V.tensor_scalar(r[0:n, :], r[0:n, :], mv[0:n, 12:13], mv[0:n, 15:16], ALU.subtract, ALU.mult))
    link(V.tensor_tensor(r[0:n, :], r[0:n, :], gb[0:n, 0], ALU.mult))
    link(V.tensor_tensor(out[0:n, :], r[0:n, :], gb[0:n, 1], ALU.add), done)


def stage_mix(c):
    nc, A, bank = c.nc, c.A, c.bank
    with ExitStack() as es:
        def sb(name, shape, dt=F32):
            return es.enter_context(nc.sbuf_tensor(name, shape, dt))
        w = sb("w_out", [P, KD, D])
        x = sb("x_rows", [P, NTILE, D])
        r = sb("resid", [P, 2, D])
        mv = sb("mv", [P, 16])
        gb = sb("ln1", [P, 2, D])
        s = {n: c.sem("mix_" + n) for n in ("in", "mm", "res", "pre", "sqrt", "h", "tr_mm", "tr")}
        d_own = c.sem("mix_dve")
        with nc.Block() as block:
            @block.sync
            def _(sp):
                sp.dma_start(w[:], A["w_out"]).then_inc(s["in"], 16)
                sp.dma_start(x[:, 0:STILE], A["x_rows"][0:SEQ].rearrange("(t p) n -> p t n", p=P)).then_inc(s["in"], 16)
                sp.dma_start(x[0:NS, STILE], A["x_rows"][SEQ:NT]).then_inc(s["in"], 16)
                sp.dma_start(gb[:], A["ln1"].to_broadcast([P, 2, D])).then_inc(s["in"], 16)

            @block.tensor
            def _(pe):
                pe.wait_ge(s["in"], 64)

                def trans(t):
                    n = rows(t)
                    pe.wait_ge(s["h"], t + 1)
                    if t:
                        pe.wait_ge(s["tr"], t)
                    for k in range(KD):
                        ins = nc.tensor.transpose(bank[4 + k // 4][:, (k % 4) * n:(k % 4 + 1) * n],
                                                  c.h[0:n, t, k * P:(k + 1) * P], c.ident[0:n, 0:n])
                    ins.then_inc(s["tr_mm"], 1)

                for t in range(NTILE):
                    if t >= 2:
                        pe.wait_ge(s["res"], t - 1)
                    for q in range(2):
                        for k in range(KD):
                            ins = nc.tensor.matmul(bank[2 * (t % 2) + q][0:rows(t), :], c.mixedT[:, k, cols(t)],
                                                   w[:, k, q * 512:(q + 1) * 512], start=k == 0, stop=k == KD - 1)
                    ins.then_inc(s["mm"], 1)
                    if t:
                        trans(t - 1)
                trans(STILE)

            @block.scalar
            def _(act):
                for t in range(NTILE):
                    n = rows(t)
                    act.wait_ge(s["pre"], t + 1)
                    nc.scalar.activation(mv[0:n, 14:15], mv[0:n, 14:15], ACT.Sqrt).then_inc(s["sqrt"], 1)
                    act.wait_ge(s["tr_mm"], t + 1)
                    nc.scalar.activation(c.hT[:, 0:4, cols(t)], bank[4][:, 0:4 * n].rearrange("p (k n) -> p k n", k=4),
                                         ACT.Copy)
                    nc.scalar.activation(c.hT[:, 4:8, cols(t)], bank[5][:, 0:4 * n].rearrange("p (k n) -> p k n", k=4),
                                         ACT.Copy).then_inc(s["tr"], 1)

            @block.vector
            def _(dve):
                V = nc.vector
                link = Link(dve, d_own)
                dve.wait_ge(s["in"], 64)
                for t in range(NTILE):
                    n = rows(t)
                    dve.wait_ge(s["mm"], t + 1)
                    for q in range(2):
                        cs = slice(q * 512, (q + 1) * 512)
                        link(V.scalar_tensor_tensor(r[0:n, t % 2, cs], x[0:n, t, cs], ALPHA,
                                                    bank[2 * (t % 2) + q][0:n, :], ALU.mult, ALU.add),
                             s["res"] if q else None)
                    layer_norm(c, link, r[:, t % 2], mv, n, gb, c.h[:, t], s["pre"], s["sqrt"], t + 1,
                               s["h"])


def stage_memory(c):
    nc, A, bank = c.nc, c.A, c.bank
    with ExitStack() as es:
        def sb(name, shape, dt=F32):
            return es.enter_context(nc.sbuf_tensor(name, shape, dt))
        wck, wcv, wcq = sb("w_ck", [P, KD, 512]), sb("w_cv", [P, KD, 512]), sb("w_cq", [P, KD, 512])
        wco = sb("w_co", [P, MH, D])
        memT = sb("memT", [P, KD, MEM])
        mkT, mv_ = sb("mkT", [P, MH, MEM]), sb("mv_rows", [P, 2, 512])
        mko = sb("mk_rows", [P, 2, 512])
        mkS, mvS = sb("mkS", [P, 2, MH, MEM]), sb("mvS", [P, 2, 2, 512])
        q = sb("q_mem", [P, MH, NT])
        qm = sb("qm", [P, MH, NB, NS])
        Pm = sb("p_mem", [P, MH, MEM])
        PT = sb("pT_mem", [P, MH, 2, P])
        oT = sb("oT_mem", [P, MH, P])
        mx, den, rden = sb("mx_m", [P, MH]), sb("den_m", [P, MH]), sb("rden_m", [P, MH])
        r = sb("resid2", [P, D])
        st = sb("mv2", [P, 16])
        gb = sb("ln2", [P, 2, D])
        names = ("in", "kv_mm", "kv_ev", "mko", "q_mm", "q_ev", "qm", "log_mm", "max", "exp", "prob", "trp_mm", "pt",
                 "o_mm", "oT", "co_mm", "res", "pre", "sqrt", "h", "tr_mm", "tr", "ks0", "ks1", "vs0", "vs1", "vs_used",
                 "ks_used", "store", "gb")
        s = {n: c.sem("mem_" + n, n == "store") for n in names}
        d_own = c.sem("mem_dve")
        SCALE = MD ** -0.5
        with nc.Block() as block:
            @block.sync
            def _(sp):
                for dst, src in ((memT, "memT"), (wck, "w_ck"), (wcv, "w_cv"), (wcq, "w_cq"), (wco, "w_co")):
                    sp.dma_start(dst[:], A[src]).then_inc(s["in"], 16)
                sp.dma_start(gb[:], A["ln2"].to_broadcast([P, 2, D])).then_inc(s["gb"], 16)
                for b in range(NB):
                    if b >= 2:
                        sp.wait_ge(s["ks_used"], b - 1)
                    sp.dma_start(mkS[:, b % 2], A["cmkT"][b]).then_inc(s[f"ks{b % 2}"], 16)
                for b in range(NB):
                    if b >= 2:
                        sp.wait_ge(s["vs_used"], b - 1)
                    sp.dma_start(mvS[:, b % 2], A["cmv"][b].rearrange("(k p) n -> p k n", p=P)).then_inc(s[f"vs{b % 2}"], 16)

            @block.gpsimd
            def _(pool):
                pool.wait_ge(s["mko"], 4)
                pool.dma_start(A["memk_p"].rearrange("(k p) n -> p k n", p=P), mko[:]).then_inc(s["store"], 16)
                pool.dma_start(A["memv_p"].rearrange("(k p) n -> p k n", p=P), mv_[:]).then_inc(s["store"], 16)
                pool.wait_ge(s["store"], 32)

            @block.tensor
            def _(pe):
                pe.wait_ge(s["in"], 80)
                for i in range(4):
                    for k in range(KD):
                        ins = nc.tensor.matmul(bank[i][:], memT[:, k, (i % 2) * P:(i % 2 + 1) * P],
                                               (wck, wcv)[i // 2][:, k], start=k == 0, stop=k == KD - 1)
                    ins.then_inc(s["kv_mm"], 1)
                for h in range(MH):
                    for k in range(KD):
                        ins = nc.tensor.matmul(bank[4 + h // 2][:, (h % 2) * MEM:(h % 2 + 1) * MEM],
                                               wck[:, k, h * P:(h + 1) * P], memT[:, k], start=k == 0, stop=k == KD - 1)
                    ins.then_inc(s["kv_mm"], 1)
                pe.wait_ge(s["mko"], 4)
                for h in range(MH):
                    if h >= 2:
                        pe.wait_ge(s["q_ev"], h - 1)
                    for k in range(KD):
                        nc.tensor.matmul(bank[h % 2][:], wcq[:, k, h * P:(h + 1) * P], c.hT[:, k, 0:SEQ],
                                         start=k == 0, stop=k == KD - 1)
                    for k in range(KD):
                        ins = nc.tensor.matmul(bank[2 + h % 2][:, 0:NS], wcq[:, k, h * P:(h + 1) * P],
                                               c.hT[:, k, SEQ:NT], start=k == 0, stop=k == KD - 1)
                    ins.then_inc(s["q_mm"], 1)
                pe.wait_ge(s["q_ev"], MH)
                pe.wait_ge(s["kv_ev"], 4)
                for t in range(NTILE):
                    n = rows(t)
                    sample = t == STILE
                    if not sample:
                        for h in range(MH):
                            ins = nc.tensor.matmul(bank[h // 2][:, (h % 2) * MEM:(h % 2 + 1) * MEM], q[:, h, cols(t)],
                                                   mkT[:, h], start=True, stop=True)
                    else:
                        pe.wait_ge(s["qm"], 1)
                        for b in range(NB):
                            pe.wait_ge(s[f"ks{b % 2}"], 16 * (b // 2 + 1))
                            for h in range(MH):
                                ins = nc.tensor.matmul(bank[h if h < 2 else h + 4][0:NS, 0:MEM],
                                                       qm[:, h, b], mkS[:, b % 2, h],
                                                       start=b == 0, stop=b == NB - 1)
                            if b < NB - 1:
                                ins.then_inc(s["ks_used"], 1)
                    ins.then_inc(s["log_mm"], 1)
                    pe.wait_ge(s["prob"], t + 1)
                    for h in range(MH):
                        for m in range(2):
                            ins = nc.tensor.transpose(bank[2 + m][:, h * n:(h + 1) * n],
                                                      Pm[0:n, h, m * P:(m + 1) * P], c.ident[0:n, 0:n])
                    ins.then_inc(s["trp_mm"], 1)
                    pe.wait_ge(s["pt"], 2 * (t + 1))
                    if not sample:
                        for h in range(MH):
                            for m in range(2):
                                ins = nc.tensor.matmul(bank[4][:, h * P:(h + 1) * P], mv_[:, m, h * P:(h + 1) * P],
                                                       PT[:, h, m, 0:n], start=m == 0, stop=m == 1)
                    else:
                        for b in range(NB):
                            pe.wait_ge(s[f"vs{b % 2}"], 16 * (b // 2 + 1))
                            for h in range(MH):
                                for m in range(2):
                                    ins = nc.tensor.matmul(bank[4][:, h * n + b * TS:h * n + (b + 1) * TS],
                                                           mvS[:, b % 2, m, h * P:(h + 1) * P],
                                                           PT[:, h, m, b * TS:(b + 1) * TS], start=m == 0, stop=m == 1)
                            if b < NB - 1:
                                ins.then_inc(s["vs_used"], 1)
                    ins.then_inc(s["o_mm"], 1)
                    pe.wait_ge(s["oT"], t + 1)
                    for half in range(2):
                        for h in range(MH):
                            ins = nc.tensor.matmul(bank[5 + half][0:n, :], oT[:, h, 0:n],
                                                   wco[:, h, half * 512:(half + 1) * 512], start=h == 0, stop=h == MH - 1)
                    ins.then_inc(s["co_mm"], 1)
                    pe.wait_ge(s["h"], t + 1)
                    for k in range(KD):
                        ins = nc.tensor.transpose(bank[(4, 7)[k // 4]][:, (k % 4) * n:(k % 4 + 1) * n],
                                                  c.h[0:n, t, k * P:(k + 1) * P], c.ident[0:n, 0:n])
                    ins.then_inc(s["tr_mm"], 1)
                    pe.wait_ge(s["tr"], t + 1)

            @block.scalar
            def _(act):
                act.wait_ge(s["kv_mm"], 4 + MH)
                for h in range(MH):
                    nc.scalar.activation(mkT[:, h], bank[4 + h // 2][:, (h % 2) * MEM:(h % 2 + 1) * MEM],
                                         ACT.Copy).then_inc(s["kv_ev"], 1)
                for h in range(MH):
                    act.wait_ge(s["q_mm"], h + 1)
                    nc.scalar.activation(q[:, h, 0:SEQ], bank[h % 2][:], ACT.Copy)
                    nc.scalar.activation(q[:, h, SEQ:NT], bank[2 + h % 2][:, 0:NS], ACT.Copy).then_inc(s["q_ev"], 1)
                for t in range(NTILE):
                    n = rows(t)
                    act.wait_ge(s["max"], t + 1)
                    for h in range(MH):
                        src = bank[h // 2][:, (h % 2) * MEM:(h % 2 + 1) * MEM] if t < STILE else \
                            bank[h if h < 2 else h + 4][0:NS, 0:MEM]
                        nc.scalar.activation(Pm[0:n, h], src, ACT.Exp, bias=mx[0:n, h:h + 1], scale=SCALE,
                                             accum_out=den[0:n, h:h + 1]).then_inc(s["exp"], 1)
                    act.wait_ge(s["trp_mm"], t + 1)
                    for m in range(2):
                        nc.scalar.activation(PT[:, :, m, 0:n], bank[2 + m][:, 0:MH * n].rearrange(
                            "p (h n) -> p h n", h=MH), ACT.Copy).then_inc(s["pt"], 1)
                    act.wait_ge(s["o_mm"], t + 1)
                    nc.scalar.activation(oT[:, :, 0:n], bank[4][:, 0:MH * n].rearrange("p (h n) -> p h n", h=MH),
                                         ACT.Copy).then_inc(s["oT"], 1)
                    act.wait_ge(s["pre"], t + 1)
                    nc.scalar.activation(st[0:n, 14:15], st[0:n, 14:15], ACT.Sqrt).then_inc(s["sqrt"], 1)
                    act.wait_ge(s["tr_mm"], t + 1)
                    nc.scalar.activation(c.hT[:, 0:4, cols(t)], bank[4][:, 0:4 * n].rearrange("p (k n) -> p k n", k=4),
                                         ACT.Copy)
                    nc.scalar.activation(c.hT[:, 4:8, cols(t)], bank[7][:, 0:4 * n].rearrange("p (k n) -> p k n", k=4),
                                         ACT.Copy).then_inc(s["tr"], 1)

            @block.vector
            def _(dve):
                V = nc.vector
                link = Link(dve, d_own)
                dve.wait_ge(s["gb"], 16)
                for i in range(4):
                    dve.wait_ge(s["kv_mm"], i + 1)
                    link(V.tensor_copy((mko, mv_)[i // 2][:, i % 2], bank[i][:]), s["mko"])
                dve.wait_ge(s["q_ev"], MH)
                for h in range(MH):
                    link(V.tensor_tensor(qm[:, h], q[:, h, SEQ:NT].unsqueeze(1).to_broadcast([P, NB, NS]), c.bcol[:],
                                         ALU.mult), s["qm"] if h == MH - 1 else None)
                for t in range(NTILE):
                    n = rows(t)
                    dve.wait_ge(s["log_mm"], t + 1)
                    if t < STILE:
                        for half in range(2):
                            link(V.reduce_max(mx[:, 2 * half:2 * half + 2],
                                              bank[half][:].rearrange("p (h m) -> p h m", h=2), AX_X))
                    else:
                        for h in range(MH):
                            link(V.reduce_max(mx[0:n, h:h + 1], bank[h if h < 2 else h + 4][0:NS, 0:MEM], AX_X))
                    link(V.tensor_scalar(mx[0:n, :], mx[0:n, :], -SCALE, None, ALU.mult), s["max"])
                    dve.wait_ge(s["exp"], MH * (t + 1))
                    link(V.reciprocal(rden[0:n, :], den[0:n, :]))
                    link(V.tensor_tensor(Pm[0:n], Pm[0:n], rden[0:n, :].unsqueeze(2).to_broadcast([n, MH, MEM]),
                                         ALU.mult), s["prob"])
                    dve.wait_ge(s["co_mm"], t + 1)
                    for half in range(2):
                        cs = slice(half * 512, (half + 1) * 512)
                        link(V.scalar_tensor_tensor(r[0:n, cs], c.h[0:n, t, cs], ALPHA, bank[5 + half][0:n, :],
                                                    ALU.mult, ALU.add), s["res"] if half else None)
                    layer_norm(c, link, r, st, n, gb, c.h[:, t], s["pre"], s["sqrt"], t + 1, s["h"])


def stage_route(c):
    nc, A, bank = c.nc, c.A, c.bank
    NJ = 2 * PH
    RING = 3
    with ExitStack() as es:
        def sb(name, shape, dt=F32):
            return es.enter_context(nc.sbuf_tensor(name, shape, dt))
        wq = sb("wq", [P, RING, KD, P])
        sk = sb("subkeys", [P, NJ, NKEYS])
        qp = sb("qp", [P, 2, NT])
        S = sb("S", [P, NTILE, NJ * NKEYS])
        work = sb("work", [P, NJ, NKEYS])
        v16 = sb("v16", [P, NJ, TOPK])
        i16 = sb("i16", [P, NJ, TOPK], U32)
        i16f = sb("i16f", [P, NJ, TOPK])
        cand = sb("cand", [P, PH, TOPK * TOPK])
        gs, gi = sb("gs", [P, PH, TOPK]), sb("gi", [P, PH, TOPK], U32)
        ab = sb("ab", [P, 2, PH * TOPK], U32)
        abf = sb("abf", [P, 2, PH * TOPK])
        eq = sb("eq", [P, PH * TOPK, TOPK])
        gm, gsum = sb("gm", [P, PH, TOPK]), sb("gsum", [P, PH])
        res = sb("res", [P, 3, P])
        sk_in, q_mm, q_ev = c.sem("sk_in"), c.sem("rq_mm"), c.sem("rq_ev")
        wq_in = [c.sem(f"wq_in{i}") for i in range(RING)]
        s_mm, s_ev, zero = c.sem("rs_mm"), c.sem("rs_ev"), c.sem("r_zero")
        g_pre, g_exp, res_ready, res_mm, res_ev = (c.sem("r_" + n) for n in
                                                   ("g_pre", "g_exp", "res", "res_mm", "res_ev"))
        d_own = c.sem("route_dve")

        with nc.Block() as block:
            @block.sync
            def _(sp):
                sp.dma_start(sk[:], A["subkeysT"]).then_inc(sk_in, 16)
                for j in range(NJ):
                    if j >= RING:
                        sp.wait_ge(q_mm, j - RING + 1)
                    sp.dma_start(wq[:, j % RING], A["wq_blk"][j]).then_inc(wq_in[j % RING], 16)

            @block.tensor
            def _(pe):
                pe.sem_inc(res_mm, 1)
                pe.wait_ge(sk_in, 16)

                def scores(j):
                    pe.wait_ge(q_ev, 2 * (j + 1))
                    if j >= 2:
                        pe.wait_ge(s_ev, 2 * (j - 1))
                    for t in range(NTILE):
                        dst = bank[4 + j % 2][:, t * P:(t + 1) * P] if t < STILE else bank[6 + j % 2][0:NS, 0:P]
                        ins = nc.tensor.matmul(dst, qp[:, j % 2, cols(t)], sk[:, j], start=True, stop=True)
                    ins.then_inc(s_mm, 1)

                for j in range(NJ):
                    pe.wait_ge(wq_in[j % RING], 16 * (j // RING + 1))
                    if j >= 2:
                        pe.wait_ge(q_ev, 2 * (j - 1))
                    for k in range(KD):
                        nc.tensor.matmul(bank[j % 2][:], wq[:, j % RING, k], c.hT[:, k, 0:SEQ],
                                         start=k == 0, stop=k == KD - 1)
                    for k in range(KD):
                        ins = nc.tensor.matmul(bank[2 + j % 2][:, 0:NS], wq[:, j % RING, k], c.hT[:, k, SEQ:NT],
                                               start=k == 0, stop=k == KD - 1)
                    ins.then_inc(q_mm, 1)
                    if j:
                        scores(j - 1)
                scores(NJ - 1)
                for t in range(NTILE):
                    pe.wait_ge(res_ready, t + 1)
                    if t == 0:
                        pe.wait_ge(q_ev, 2 * NJ)
                    else:
                        pe.wait_ge(res_ev, t)
                    for q in range(3):
                        ins = nc.tensor.transpose(bank[0][:, q * P:(q + 1) * P], res[:, q], c.ident[:])
                    ins.then_inc(res_mm, 1)

            @block.scalar
            def _(act):
                def scores(j):
                    act.wait_ge(s_mm, j + 1)
                    if j == 0:
                        act.wait_ge(zero, 1)
                    nc.scalar.activation(S[:, 0:STILE, j * NKEYS:(j + 1) * NKEYS],
                                         bank[4 + j % 2][:].rearrange("p (t n) -> p t n", t=STILE),
                                         ACT.Copy).then_inc(s_ev, 1)
                    nc.scalar.activation(S[0:NS, STILE, j * NKEYS:(j + 1) * NKEYS], bank[6 + j % 2][0:NS, 0:P],
                                         ACT.Copy).then_inc(s_ev, 1)

                for j in range(NJ):
                    act.wait_ge(q_mm, j + 1)
                    if j >= 2:
                        act.wait_ge(s_mm, j - 1)
                    nc.scalar.activation(qp[:, j % 2, 0:SEQ], bank[j % 2][:], ACT.Copy).then_inc(q_ev, 1)
                    nc.scalar.activation(qp[:, j % 2, SEQ:NT], bank[2 + j % 2][:, 0:NS], ACT.Copy).then_inc(q_ev, 1)
                    if j:
                        scores(j - 1)
                scores(NJ - 1)
                for t in range(NTILE):
                    act.wait_ge(g_pre, t + 1)
                    nc.scalar.activation(gm[:], gm[:], ACT.Exp).then_inc(g_exp, 1)
                    act.wait_ge(res_mm, t + 2)
                    n = rows(t)
                    nc.scalar.activation(c.slots[:, :, cols(t)],
                                         bank[0][:, 0:3 * P].rearrange("p (q n) -> p q n", q=3)[:, :, 0:n],
                                         ACT.Copy).then_inc(res_ev, 1)

            @block.vector
            def _(dve):
                V = nc.vector
                V.memset(S[:, STILE], 0.0).then_inc(zero, 1)
                dve.wait_ge(s_ev, 2 * NJ)
                with dve.Fori(0, NTILE) as ti:
                    dve.sem_clear(d_own)
                    link = Link(dve, d_own)

                    def top16(val, idx, x):
                        link(V.max(val[:, 0:8], x))
                        link(V.max_index(idx[:, 0:8], val[:, 0:8], x))
                        link(V.match_replace(x, val[:, 0:8], x, PICKED))
                        link(V.max(val[:, 8:16], x))
                        link(V.max_index(idx[:, 8:16], val[:, 8:16], x))

                    link(V.tensor_copy(work[:].rearrange("p j n -> p (j n)").unsqueeze(1), S[:, bass.ds(ti, 1)]))
                    for j in range(NJ):
                        top16(v16[:, j], i16[:, j], work[:, j])
                    v = v16[:].rearrange("p (h two) a -> p two h a", two=2)
                    c4 = cand[:].rearrange("p h (a b) -> p h a b", a=TOPK)
                    link(V.tensor_tensor(c4, v[:, 0].unsqueeze(3).to_broadcast([P, PH, TOPK, TOPK]),
                                         v[:, 1].unsqueeze(2).to_broadcast([P, PH, TOPK, TOPK]), ALU.add))
                    for h in range(PH):
                        top16(gs[:, h], gi[:, h], cand[:, h])
                    flat = gi[:].rearrange("p h a -> p (h a)")
                    link(V.tensor_scalar(ab[:, 0], flat, 4, None, ALU.logical_shift_right))
                    link(V.tensor_scalar(ab[:, 1], flat, TOPK - 1, None, ALU.bitwise_and))
                    link(V.tensor_copy(abf[:], ab[:]))
                    link(V.tensor_copy(i16f[:], i16[:]))
                    V.tensor_tensor(gm[:], gs[:], gs[:, :, 0:1].to_broadcast([P, PH, TOPK]),
                                    ALU.subtract).then_inc(g_pre, 1)
                    if16 = i16f[:].rearrange("p (h two) a -> p two h a", two=2)
                    dve.wait_ge(res_mm, ti + 1)
                    for q in range(2):
                        e3 = eq[:]
                        link(V.tensor_tensor(e3, abf[:, q].unsqueeze(2).to_broadcast([P, PH * TOPK, TOPK]),
                                             c.iota[:, 0:TOPK].unsqueeze(1).to_broadcast([P, PH * TOPK, TOPK]),
                                             ALU.is_equal))
                        e4 = eq[:].rearrange("p (h s) a -> p h s a", h=PH)
                        link(V.tensor_tensor(e4, e4, if16[:, q].unsqueeze(2).to_broadcast([P, PH, TOPK, TOPK]),
                                             ALU.mult))
                        link(V.reduce_sum(res[:, q], e3, AX_X))
                    dve.wait_ge(g_exp, ti + 1)
                    link(V.reduce_sum(gsum[:], gm[:], AX_X))
                    link(V.reciprocal(gsum[:], gsum[:]))
                    V.tensor_tensor(res[:, 2].rearrange("p (h s) -> p h s", h=PH), gm[:],
                                    gsum[:].unsqueeze(2).to_broadcast([P, PH, TOPK]), ALU.mult).then_inc(res_ready, 1)
                    dve.wait_ge(res_ready, ti + 1)


GS = 4
NG = NKEYS // GS
TB = 64
NTB = SEQ // TB
GCOL = GS * NT
U_START = 2


def stage_gates(c):
    nc, A, bank = c.nc, c.A, c.bank
    with ExitStack() as es:
        def sb(name, shape, dt=F32):
            return es.enter_context(nc.sbuf_tensor(name, shape, dt))
        hot_i, hot_j, raw_j = (sb(n, [P, 2, 4, P]) for n in ("hot_i", "hot_j", "raw_j"))
        G = sb("Gtile", [P, 2, NKEYS, TB])
        hi_ready, hj_ready, rj_ready = c.sem("hot_i"), c.sem("hot_j"), c.sem("raw_j")
        g_mm, g_ev = c.sem("g_mm"), c.sem("g_ev")
        stored = [c.sem(f"g_stored{i}") for i in range(2)]
        blocks = [(b * TB, TB // 8) for b in range(NTB)] + [(SEQ, NS // 8)]

        def rounds(eng, body):
            first = 0
            for b, (tok0, count) in enumerate(blocks):
                with eng.Fori(0, count) as r:
                    for u in range(2):
                        body(r * 8 + (tok0 + 4 * u), r * 2 + (2 * first + u), r * 8 + 4 * u, b, u)
                first += count
                yield b, 2 * first

        with nc.Block() as block:
            @block.vector
            def _(dve):
                def body(tok, n, at, b, u):
                    dve.wait_ge(g_mm, n + 1)
                    for q, (hot, ready) in enumerate(((raw_j, rj_ready), (hot_i, hi_ready))):
                        nc.vector.tensor_tensor(hot[:, u], c.iota[:].unsqueeze(1).to_broadcast([P, 4, P]),
                                                c.slots[:, 1 - q, bass.ds(tok, 4)].unsqueeze(2).to_broadcast([P, 4, P]),
                                                ALU.is_equal).then_inc(ready, 1)
                for _ in rounds(dve, body):
                    pass

            @block.gpsimd
            def _(pool):
                def body(tok, n, at, b, u):
                    pool.wait_ge(rj_ready, n + 1)
                    nc.gpsimd.tensor_tensor(hot_j[:, u], raw_j[:, u],
                                            c.slots[:, 2, bass.ds(tok, 4)].unsqueeze(2).to_broadcast([P, 4, P]),
                                            ALU.mult).then_inc(hj_ready, 1)
                for _ in rounds(pool, body):
                    pass

            @block.tensor
            def _(pe):
                pe.sem_inc(g_mm, 2)
                def body(tok, n, at, b, u):
                    pe.wait_ge(hi_ready, n + 1)
                    pe.wait_ge(hj_ready, n + 1)
                    pe.wait_ge(g_ev, n + 1)
                    for q in range(4):
                        ins = nc.tensor.matmul(bank[u][:, q * P:(q + 1) * P], hot_i[:, u, q], hot_j[:, u, q],
                                               start=True, stop=True)
                    ins.then_inc(g_mm, 1)
                for _ in rounds(pe, body):
                    pass

            @block.scalar
            def _(act):
                act.sem_inc(g_ev, 2)
                def body(tok, n, at, b, u):
                    act.wait_ge(g_mm, n + 3)
                    nc.scalar.activation(G[:, b % 2, :, bass.ds(at, 4)].rearrange("p j t -> p t j"),
                                         bank[u][:].rearrange("p (t j) -> p t j", t=4), ACT.Copy).then_inc(g_ev, 1)
                for b, _ in rounds(act, body):
                    if b + 1 < len(blocks) and b >= 1:
                        act.wait_ge(stored[(b + 1) % 2], 16 * ((b - 1) // 2 + 1))

            @block.sync
            def _(sp):
                first = 0
                for b, (tok0, count) in enumerate(blocks):
                    first += count
                    w = TB if b < NTB else NS
                    sp.wait_ge(g_ev, 2 * first + 2)
                    dst = A["gates"][:, :, b * GS * TB:b * GS * TB + GS * w]
                    if b < NTB:
                        sp.dma_start(dst.rearrange("g p n -> p g n"),
                                     G[:, b % 2].rearrange("p (g j) t -> p g (j t)", j=GS)).then_inc(stored[b % 2], 16)
                    else:
                        for j in range(GS):
                            sp.dma_start(dst[:, :, j * NS:(j + 1) * NS].rearrange("g p t -> p g t"),
                                         G[:, b % 2].rearrange("p (g j) t -> p j g t", j=GS)[:, j, :, 0:NS]
                                         ).then_inc(stored[b % 2], 16)
                sp.wait_ge(stored[0], 16 * (NTB // 2 + GS))
                sp.wait_ge(stored[1], 16 * (NTB // 2))


def stage_experts(c):
    nc, A, bank = c.nc, c.A, c.bank
    with ExitStack() as es:
        def sb(name, shape, dt=F32):
            return es.enter_context(nc.sbuf_tensor(name, shape, dt))
        hH, hL = sb("hH", [P, KD, NT], F32R), sb("hL", [P, KD, NT], F32R)
        u, uH, uL = sb("u_raw", [P, 2, KD, P]), sb("uH", [P, 2, KD, P], F32R), sb("uL", [P, 2, KD, P], F32R)
        v, vH, vL = sb("v_raw", [P, 2, D]), sb("vH", [P, GS, D], F32R), sb("vL", [P, GS, D], F32R)
        G = sb("G", [P, 2, GCOL])
        a, wf = sb("acts", [P, 2, NT]), sb("wf", [P, NT])
        wH, wL = sb("wH", [P, GS, NT], F32R), sb("wL", [P, GS, NT], F32R)
        y = c.hT
        h_split, d_own = c.sem("h_split"), c.sem("exp_dve")
        u_in = [c.sem(f"u_in{i}") for i in range(2)]
        v_in = [c.sem(f"v_in{i}") for i in range(2)]
        G_in = [c.sem(f"G_in{i}") for i in range(2)]
        u_split, u_mm, u_act, w_done, v_split, y_added = (c.sem(n) for n in (
            "u_split", "u_mm", "u_act", "w_done", "v_split", "y_added"))
        u_hi, v_hi, v_mm = c.sem("u_hi"), c.sem("v_hi"), c.sem("v_mm")
        R = U_START

        def loop(eng, body):
            with eng.Fori(0, NG // 2 - 1) as r:
                for p in range(2):
                    body(r * 2 + p, p, False)
            for p in range(2):
                body(NG - 2 + p, p, True)

        with nc.Block() as block:
            @block.sync
            def _(sp):
                def body(g, p, last):
                    for j in range(GS):
                        n = g * GS + j
                        sp.wait_ge(u_split, n + 1)
                        src = A["uT"][bass.ds(n, 1)] if not isinstance(n, int) else A["uT"][n:n + 1]
                        sp.dma_start(u[:, j % 2], src.rearrange("a p k n -> p (a k) n")).then_inc(u_in[j % 2], 16)
                loop(sp, body)

            @block.gpsimd
            def _(pool):
                for g in range(2):
                    pool.dma_start(G[:, g], A["gates"][g]).then_inc(G_in[g], 16)

                def body(g, p, last):
                    for j in range(GS):
                        n = g * GS + j
                        pool.wait_ge(v_split, n + 1)
                        src = A["v_rows"][bass.ds(n, 1)] if not isinstance(n, int) else A["v_rows"][n:n + 1]
                        pool.dma_start(v[:, j % 2], src.rearrange("a p n -> p (a n)")).then_inc(v_in[j % 2], 16)
                    if not last:
                        pool.wait_ge(w_done, (g + 1) * GS + R)
                        pool.dma_start(G[:, p], A["gates"][bass.ds(g + 2, 1)].rearrange("a p n -> p (a n)")
                                       ).then_inc(G_in[p], 16)
                loop(pool, body)

            @block.scalar
            def _(act):
                act.sem_inc(u_act, R)

                def high_u(n, j):
                    act.wait_ge(u_in[j % 2], (n - j % 2) * 8 + 16)
                    act.wait_ge(u_mm, n + 1)
                    nc.scalar.activation(uH[:, j % 2], u[:, j % 2], ACT.Copy).then_inc(u_hi, 1)

                high_u(0, 0)

                def body(g, p, last):
                    for j in range(GS):
                        n = g * GS + j
                        if not (last and p == 1 and j == GS - 1):
                            high_u(n + 1, (j + 1) % 2)
                        act.wait_ge(v_in[j % 2], (n - j % 2) * 8 + 16)
                        act.wait_ge(v_mm, g * KD + 1)
                        nc.scalar.activation(vH[:, j], v[:, j % 2], ACT.Copy).then_inc(v_hi, 1)
                        act.wait_ge(u_mm, n + 1 + R)
                        act.wait_ge(w_done, n + 1)
                        nc.scalar.activation(a[:, j % 2, 0:SEQ], bank[j % 2][:], ACT.Gelu_apprx_tanh)
                        nc.scalar.activation(a[:, j % 2, SEQ:NT], bank[2 + j % 2][:, 0:NS],
                                             ACT.Gelu_apprx_tanh).then_inc(u_act, 1)
                loop(act, body)

            @block.vector
            def _(dve):
                V = nc.vector
                for sem in (u_split, v_split, w_done, y_added):
                    dve.sem_inc(sem, R)
                for k in range(KD):
                    V.tensor_copy(hH[:, k], c.hT[:, k]).then_inc(h_split, 1)
                    dve.wait_ge(h_split, 2 * k + 1)
                    V.tensor_tensor(hL[:, k], c.hT[:, k], hH[:, k].bitcast(F32), ALU.subtract).then_inc(h_split, 1)
                dve.wait_ge(h_split, 2 * KD)
                V.memset(y[:], 0.0).then_inc(d_own, 1)
                dve.wait_ge(d_own, 1)
                PER = 3 * GS

                def low_u(n, j):
                    dve.wait_ge(u_hi, n + 1)
                    V.tensor_tensor(uL[:, j % 2], u[:, j % 2], uH[:, j % 2].bitcast(F32),
                                    ALU.subtract).then_inc(u_split, 1)

                low_u(0, 0)

                def body(g, p, last):
                    def own(ins, k):
                        ins.then_inc(d_own, 1)
                        dve.wait_ge(d_own, g * PER + k + 1)
                    for j in range(GS):
                        n = g * GS + j
                        if not (last and p == 1 and j == GS - 1):
                            low_u(n + 1, (j + 1) % 2)
                        dve.wait_ge(v_hi, n + 1)
                        V.tensor_tensor(vL[:, j], v[:, j % 2], vH[:, j].bitcast(F32),
                                        ALU.subtract).then_inc(v_split, 1)
                        if j == 0:
                            dve.wait_ge(G_in[p], (g - p) * 8 + 16)
                        dve.wait_ge(u_act, n + 1 + R)
                        gp = G[:, p, 0:GS * SEQ].rearrange("p (b j t) -> p b j t", b=NTB, j=GS)[:, :, j]
                        own(V.tensor_tensor(wf[:, 0:SEQ].rearrange("p (b t) -> p b t", b=NTB),
                                            a[:, j % 2, 0:SEQ].rearrange("p (b t) -> p b t", b=NTB), gp, ALU.mult),
                            3 * j + 1)
                        own(V.tensor_tensor(wf[:, SEQ:NT], a[:, j % 2, SEQ:NT],
                                            G[:, p, GS * SEQ + j * NS:GS * SEQ + (j + 1) * NS], ALU.mult), 3 * j + 2)
                        own(V.tensor_copy(wH[:, j], wf[:]), 3 * j + 3)
                        V.tensor_tensor(wL[:, j], wf[:], wH[:, j].bitcast(F32), ALU.subtract).then_inc(w_done, 1)
                        dve.wait_ge(w_done, n + 1 + R)
                    for k in range(KD):
                        dve.wait_ge(v_mm, g * KD + k + 2)
                        V.tensor_tensor(y[:, k, 0:SEQ], y[:, k, 0:SEQ], bank[4 + k % 2][:], ALU.add)
                        V.tensor_tensor(y[:, k, SEQ:NT], y[:, k, SEQ:NT], bank[6 + k % 2][:, 0:NS],
                                        ALU.add).then_inc(y_added, 1)
                    dve.wait_ge(y_added, (g + 1) * KD + R)
                loop(dve, body)

            @block.tensor
            def _(pe):
                pe.sem_inc(u_mm, R)
                pe.sem_inc(v_mm, 1)
                pe.wait_ge(h_split, 2 * KD)

                def body(g, p, last):
                    for j in range(GS):
                        n = g * GS + j
                        pe.wait_ge(u_split, n + 1 + R)
                        pe.wait_ge(u_act, n + 1)
                        for dst, cs in ((bank[j % 2][:], slice(0, SEQ)), (bank[2 + j % 2][:, 0:NS], slice(SEQ, NT))):
                            parts = [(w, x, k) for k in range(KD) for w, x in ((uH, hH), (uH, hL), (uL, hH))]
                            for m, (w, x, k) in enumerate(parts):
                                ins = nc.tensor.matmul(dst, w[:, j % 2, k], x[:, k, cs], start=m == 0,
                                                       stop=m == len(parts) - 1)
                        ins.then_inc(u_mm, 1)
                    for k in range(KD):
                        pe.wait_ge(y_added, g * KD + k + 1)
                        if k == 0:
                            pe.wait_ge(v_split, (g + 1) * GS + R)
                            pe.wait_ge(w_done, (g + 1) * GS + R)
                        for dst, cs in ((bank[4 + k % 2][:], slice(0, SEQ)), (bank[6 + k % 2][:, 0:NS], slice(SEQ, NT))):
                            parts = [(w, x, j) for j in range(GS) for w, x in ((vH, wH), (vH, wL), (vL, wH))]
                            for m, (w, x, j) in enumerate(parts):
                                ins = nc.tensor.matmul(dst, w[:, j, k * P:(k + 1) * P], x[:, j, cs], start=m == 0,
                                                       stop=m == len(parts) - 1)
                        ins.then_inc(v_mm, 1)
                loop(pe, body)


def stage_finish(c):
    nc, A, bank = c.nc, c.A, c.bank
    with ExitStack() as es:
        def sb(name, shape, dt=F32):
            return es.enter_context(nc.sbuf_tensor(name, shape, dt))
        r = sb("resid3", [P, D])
        out = sb("yout", [P, NTILE, D])
        st = sb("mv3", [P, 16])
        gb = sb("ln3", [P, 2, D])
        s = {n: c.sem("fin_" + n) for n in ("gb", "mm", "res", "pre", "sqrt", "out", "store")}
        d_own = c.sem("fin_dve")
        with nc.Block() as block:
            @block.tensor
            def _(pe):
                for t in range(NTILE):
                    n = rows(t)
                    if t >= 2:
                        pe.wait_ge(s["res"], t - 1)
                    for k in range(KD):
                        ins = nc.tensor.transpose(bank[2 * (t % 2) + k // 4][0:n, (k % 4) * P:(k % 4 + 1) * P],
                                                  c.hT[:, k, cols(t)], c.ident[:])
                    ins.then_inc(s["mm"], 1)

            @block.scalar
            def _(act):
                for t in range(NTILE):
                    n = rows(t)
                    act.wait_ge(s["pre"], t + 1)
                    nc.scalar.activation(st[0:n, 14:15], st[0:n, 14:15], ACT.Sqrt).then_inc(s["sqrt"], 1)

            @block.vector
            def _(dve):
                link = Link(dve, d_own)
                dve.wait_ge(s["gb"], 16)
                for t in range(NTILE):
                    n = rows(t)
                    dve.wait_ge(s["mm"], t + 1)
                    for q in range(2):
                        cs = slice(q * 512, (q + 1) * 512)
                        link(nc.vector.scalar_tensor_tensor(r[0:n, cs], c.h[0:n, t, cs], ALPHA,
                                                            bank[2 * (t % 2) + q][0:n, :], ALU.mult, ALU.add),
                             s["res"] if q else None)
                    layer_norm(c, link, r, st, n, gb, out[:, t], s["pre"], s["sqrt"], t + 1, s["out"])

            @block.sync
            def _(sp):
                sp.dma_start(gb[:], A["ln3"].to_broadcast([P, 2, D])).then_inc(s["gb"], 16)
                for t in range(NTILE):
                    sp.wait_ge(s["out"], t + 1)
                    dst = A["y_p"][t * P:(t + 1) * P] if t < STILE else A["y_s"]
                    sp.dma_start(dst, out[0:rows(t), t]).then_inc(s["store"], 16)
                sp.wait_ge(s["store"], 16 * NTILE)


def stage_constants(c):
    nc, A = c.nc, c.A
    names = list(c.const)
    const_in = c.sem("const_in")
    with nc.Block() as block:
        @block.sync
        def _(sp):
            for name in names:
                sp.dma_start(c.const[name][:], A["k_" + name]).then_inc(const_in, 16)
            sp.dma_start(c.vecs[:], A["vecs"].to_broadcast([P, NVEC])).then_inc(const_in, 16)
            sp.wait_ge(const_in, 16 * (len(names) + 1))


def build(nc, A, upto=99, dump=None):
    c = Ctx(nc, A)
    with c.stack, ExitStack() as right:
        c.ident = c.keep(c.stack, "ident", [P, P])
        c.iota = c.keep(c.stack, "iota", [P, P])
        c.tri = c.keep(c.stack, "tri", [P, P])
        c.low = c.keep(c.stack, "low", [P, P])
        c.lowneg = c.keep(c.stack, "lowneg", [P, P])
        c.ones = c.keep(c.stack, "ones", [P, P])
        c.triS = c.keep(c.stack, "triS", [NS, NS])
        c.lowS = c.keep(c.stack, "lowS", [NS, NS])
        c.lowSneg = c.keep(c.stack, "lowSneg", [NS, NS])
        c.onesS = c.keep(c.stack, "onesS", [NS, NS])
        c.bsel = c.keep(c.stack, "bsel", [NS, NB])
        c.bcol = c.keep(c.stack, "bcol", [P, NB, NS])
        c.vecs = c.keep(c.stack, "vecs", [P, NVEC])
        c.const = {"ident": c.ident, "iota": c.iota, "tri": c.tri, "low": c.low, "lowneg": c.lowneg, "ones": c.ones, "triS": c.triS, "lowS": c.lowS, "lowSneg": c.lowSneg, "onesS": c.onesS, "bsel": c.bsel, "bcol": c.bcol}
        stage_constants(c)
        with ExitStack() as mid:
            c.mixedT = c.keep(mid, "mixedT", [P, KD, NT])
            with ExitStack() as att:
                c.qT = c.keep(att, "qT", [P, 4, NT])
                c.kT = c.keep(att, "kT", [P, 4, NT])
                c.qiT = c.keep(att, "qiT", [P, 4, NT])
                c.kiT = c.keep(att, "kiT", [P, NT])
                c.v = c.keep(att, "v", [P, NTILE, 512])
                c.small = c.keep(att, "small", [P, NTILE, NSMALL])
                with ExitStack() as ssd:
                    c.convin_p = c.keep(ssd, "convin_p", [P, KD, SEQ + 3])
                    c.convin_s = c.keep(ssd, "convin_s", [P, KD, NB, TS + 3])
                    c.z = c.keep(ssd, "z", [P, NTILE, 512])
                    stage_project(c)
                    if upto >= 2:
                        stage_ssd(c)
                if upto >= 3:
                    stage_dsa_prompt(c)
                if upto >= 4:
                    stage_dsa_sample(c)
            if dump and upto <= 4:
                return dump(c)
            c.reset_semaphores()
            c.h = c.keep(right, "h", [P, NTILE, D], "right")
            c.hT = c.keep(right, "hT", [P, KD, NT], "right")
            stage_mix(c)
        if dump and upto <= 5:
            return dump(c)
        stage_memory(c)
        if dump and upto <= 6:
            return dump(c)
        with ExitStack() as routed:
            c.slots = c.keep(routed, "slots", [P, 3, NT], "right")
            stage_route(c)
            if dump and upto <= 7:
                return dump(c)
            stage_gates(c)
        stage_experts(c)
        stage_finish(c)


def shape_constants():
    f = np.float32
    i, j = np.arange(P)[:, None], np.arange(P)[None, :]
    r, q = np.arange(NS)[:, None], np.arange(NS)[None, :]
    same = r // TS == q // TS
    k = {
        "k_ident": np.eye(P, dtype=f),
        "k_iota": np.broadcast_to(np.arange(P, dtype=f), (P, P)),
        "k_tri": (i <= j).astype(f),
        "k_low": (j <= i).astype(f),
        "k_lowneg": np.where(j <= i, 0.0, NOT_CAUSAL).astype(f),
        "k_ones": np.ones((P, P), f),
        "k_triS": (same & (r <= q)).astype(f),
        "k_lowS": (same & (q <= r)).astype(f),
        "k_lowSneg": np.where(same & (q <= r), 0.0, NOT_CAUSAL).astype(f),
        "k_onesS": same.astype(f),
        "k_bsel": (np.arange(NS)[:, None] // TS == np.arange(NB)[None, :]).astype(f),
        "k_bcol": np.broadcast_to((np.arange(NS)[None, :] // TS == np.arange(NB)[:, None]).astype(f), (P, NB, NS)),
    }

    def bucket(dist):
        n = np.maximum(dist, 0)
        nf = np.maximum(n, 1).astype(f)
        large = 16 + (np.log(nf / f(16)) / f(np.log(128 / 16)) * f(16)).astype(np.int32)
        return np.where(n < 16, n, np.minimum(large, NBUCKET - 1))

    def onehot(dist):
        return (np.arange(NBUCKET).reshape((-1,) + (1,) * np.ndim(dist)) == bucket(dist)[None]).astype(f)

    k["bucket_rev"] = onehot(2 * P - 1 - np.arange(3 * P))
    k["bucket_past"] = onehot(PAST + TS - 1 - np.arange(PAST + TS))
    k["bucket_new"] = onehot(np.arange(TS)[:, None] - (np.arange(NS) % TS)[None, :])
    half = NB // 2
    b4, h, t = (x.ravel() for x in np.meshgrid(np.arange(half), np.arange(H), np.arange(TS), indexing="ij"))
    k["expand_rows"] = np.stack([(np.arange(NS)[:, None] == ((g * half + b4) * TS + t)[None, :]) for g in range(2)],
                                1).astype(f)
    hh, tt = (x.ravel() for x in np.meshgrid(np.arange(H), np.arange(TS), indexing="ij"))
    k["head_mask"] = (HD ** -0.5 * (np.arange(H)[None, None, :] == 2 * np.arange(4)[None, :, None]
                                    + (np.arange(P) // HD)[:, None, None])).astype(f)
    k["out_mask"] = (hh[:, None] == (np.arange(512) // HD)[None, :]).astype(f)
    k["t_sum"] = (tt[:, None] == np.arange(TS)[None, :]).astype(f)
    k["t_sel"] = (np.arange(NS)[:, None] % TS == np.arange(TS)[None, :]).astype(f)
    k["w_mask"] = (np.arange(NB)[None, :, None] * TS + tt[:, None, None] == np.arange(NS)[None, None, :]).astype(f)
    return {n: np.ascontiguousarray(a) for n, a in k.items()}


def layouts(x):
    c = np.ascontiguousarray

    def chunks(w):
        return c(w.reshape(-1, P, w.shape[1]).transpose(1, 0, 2))

    w_in = x["w_in"]
    cut = lambda at, n: w_in[:, at:at + n]
    wt = np.concatenate([cut(OFF_XBC, CONV), cut(OFF_Q, 512), cut(OFF_K, 512), cut(OFF_QI, 512), cut(OFF_KI, HD),
                         cut(OFF_KI, HD)], 1)
    xr = np.concatenate([x["x_prompt"].reshape(SEQ, D), x["x_sample"].reshape(NS, D)], 0)
    vec = {n: x[n].reshape(-1) for n in VEC if n != "bias_far"}
    vec["bias_far"] = x["rel_bias"][NBUCKET - 1]
    out = {
        "xT": chunks(c(xr.T)),
        "x_rows": xr,
        "w_blk": c(chunks(wt).reshape(P, KD, NBLK, P).transpose(2, 0, 1, 3)),
        "w_row": np.stack([chunks(cut(OFF_Z, 512)), chunks(cut(OFF_V, 512))]),
        "w_small": chunks(np.concatenate([cut(OFF_DT, H), cut(OFF_KI, HD), cut(OFF_WI, H)], 1)),
        "vecs": np.concatenate([vec[n] for n in VEC])[None],
        "state_convT": x["state_conv"].reshape(NB, 3, KD, P).transpose(3, 2, 0, 1),
        "conv_w": x["conv_w"].reshape(4, KD, P).transpose(2, 1, 0),
        "conv_b": x["conv_b"].reshape(KD, P).T,
        "state_ssmT": x["state_ssm"].reshape(NB, 512, P).transpose(2, 0, 1),
        "state_ssm": x["state_ssm"].reshape(NB, 4, P, P).transpose(2, 0, 1, 3),
        "rel_bias": x["rel_bias"],
        "ln1": np.stack([x["ln1_g"], x["ln1_b"]])[None],
        "ln2": np.stack([x["ln2_g"], x["ln2_b"]])[None],
        "ln3": np.stack([x["ln3_g"], x["ln3_b"]])[None],
        "page_table": x["page_table"].reshape(1, -1),
        "kidxT": x["cache_kidx"].transpose(0, 2, 1),
        "kT_pages": x["cache_k"].reshape(-1, PAGE, 4, P).transpose(0, 3, 2, 1).reshape(-1, P, 4 * PAGE),
        "v_pages": x["cache_v"].reshape(-1, PAGE, 512),
        "w_out": chunks(x["w_out"]),
        "memT": chunks(c(x["mem_prompt"][0].T)),
        "w_ck": chunks(x["w_ck"]), "w_cv": chunks(x["w_cv"]), "w_cq": chunks(x["w_cq"]), "w_co": chunks(x["w_co"]),
        "cmkT": x["cache_mem_k"].transpose(0, 3, 2, 1),
        "cmv": x["cache_mem_v"].reshape(NB, MEM, 512),
        "wq_blk": chunks(x["peer_wq"]).reshape(P, KD, 2 * PH, P).transpose(2, 0, 1, 3),
        "subkeysT": x["peer_subkeys"].reshape(2 * PH, NKEYS, P).transpose(2, 0, 1),
        "uT": x["peer_u"].reshape(NKEYS, NKEYS, KD, P).transpose(1, 3, 2, 0),
        "v_rows": x["peer_v"].reshape(NKEYS, NKEYS, D).transpose(1, 0, 2),
    }
    out.update(shape_constants())
    return {n: c(a) for n, a in out.items()}


OUTPUTS = {
    "y_p": (SEQ, D), "y_s": (NS, D), "k_p": (SEQ, 512), "v_p": (SEQ, 512), "kidx_p": (SEQ, HD),
    "memk_p": (MEM, 512), "memv_p": (MEM, 512), "ssm_p": (512, P), "conv_p": (1, 3, CONV),
    "k_s": (NS, 512), "v_s": (NS, 512), "kidx_s": (NS, HD), "ssm_s": (NB, 512, P), "conv_s": (NB, 3, CONV),
}
SHAPES = {
    "y_p": (1, SEQ, D), "y_s": (NB, TS, D), "k_p": (1, SEQ, H, HD), "v_p": (1, SEQ, H, HD), "kidx_p": (1, SEQ, HD),
    "memk_p": (1, MEM, MH, MD), "memv_p": (1, MEM, MH, MD), "ssm_p": (1, H, HD, P), "conv_p": (1, 3, CONV),
    "k_s": (NB, TS, H, HD), "v_s": (NB, TS, H, HD), "kidx_s": (NB, TS, HD), "ssm_s": (NB, H, HD, P),
    "conv_s": (NB, 3, CONV),
}


def kernel(**inputs):
    import concourse.bacc as bacc
    from concourse.bass_utils import run_bass_kernel_spmd

    nc = bacc.Bacc("TRN2", target_bir_lowering=False, num_devices=1)
    arrays, A = {}, {}
    for name, a in layouts({k: np.asarray(v) for k, v in inputs.items()}).items():
        arrays[f"in_{name}"] = a
        A[name] = nc.dram_tensor(f"in_{name}", a.shape, mybir.dt.from_np(a.dtype), kind="ExternalInput").ap()
    for name, shape in OUTPUTS.items():
        A[name] = nc.dram_tensor(f"out_{name}", shape, F32, kind="ExternalOutput").ap()
    A["gates"] = nc.dram_tensor("gate_table", [NG, P, GCOL], F32, kind="Internal").ap()
    build(nc, A)
    r = run_bass_kernel_spmd(nc, [arrays], core_ids=[0])
    return tuple(r.results[0][f"out_{name}"].reshape(SHAPES[name]) for name in OUTPUTS)
```

```python
from contextlib import ExitStack

import numpy as np
import concourse.bass as bass
from concourse import mybir

F32 = mybir.dt.float32
F32R = mybir.dt.float32r
I32 = mybir.dt.int32
U32 = mybir.dt.uint32
ALU = mybir.AluOpType
ACT = mybir.ActivationFunctionType
AX_X = mybir.AxisListType.X

P = 128
D = 1024
KD = D // P
SEQ, NB, TS = 512, 8, 4
NS = NB * TS
NT = SEQ + NS
HALF = NT // 2
NTILE = SEQ // P + 1
STILE = NTILE - 1
H, HD = 8, 64
CONV = 1024
NPAGE, PAGE = 16, 128
PAST = NPAGE * PAGE
NKEY = PAST + NS
NBUCKET = 32
KV_RING = 2 + NB // 2
MH, MD, MEM = 4, 128, 256
PH, NKEYS, TOPK = 8, 128, 16
ALPHA = 2.0 ** 0.25
EPS = 1e-5
NOT_SELECTED = -1e30
NOT_CAUSAL = -2e38
PICKED = -3e38

OFF_Z, OFF_XBC, OFF_DT, OFF_Q, OFF_K, OFF_V, OFF_QI, OFF_KI, OFF_WI = (
    0, 512, 1536, 1544, 2056, 2568, 3080, 3592, 3656)
B_XBC, B_Q, B_K, B_QI, B_KI, NBLK = 0, 8, 12, 16, 20, 21
S_DT, S_KI, S_WI, NSMALL = 0, 8, 72, 80
VEC = {}
_at = 0
for _name, _n in (("ssd_norm_w", 512), ("dt_bias", H), ("a_log", H), ("d_skip", H), ("bias_far", H)):
    VEC[_name] = (_at, _n)
    _at += _n
NVEC = _at


def rows(t):
    return P if t < STILE else NS


def cols(t):
    return slice(t * P, t * P + rows(t))


class Link:

    def __init__(self, eng, own):
        self.eng, self.own, self.count = eng, own, {}

    def count_up(self, ins, sem):
        self.count[id(sem)] = self.count.get(id(sem), 0) + 1
        ins.then_inc(sem, 1)

    def __call__(self, ins, sem=None):
        sem = self.own if sem is None else sem
        self.count_up(ins, sem)
        self.eng.wait_ge(sem, self.count[id(sem)])


class Ctx:

    def __init__(self, nc, A):
        self.nc, self.A = nc, A
        self.stack, self.sems = ExitStack(), []
        self.psum = self.stack.enter_context(nc.psum_tensor("psum", [P, 8, 512], F32))
        self.bank = [self.psum[:, i] for i in range(8)]

    def kiS(self, b):
        return self.kvring[HD * (b % 2):HD * (b % 2) + HD, 2 + b // 2]

    def pair(self, i):
        return self.psum[:, 2 * i:2 * i + 2, 0:HALF]

    def keep(self, stack, name, shape, side="left"):
        return stack.enter_context(self.nc.sbuf_tensor(name, shape, F32, side=side))

    def sem(self, name, software_dma=False):
        s = self.nc.alloc_semaphore(name)
        if not software_dma:
            self.sems.append(s)
        return s

    def reset_semaphores(self):
        spans = []
        for num in sorted(s.num for s in self.sems):
            if spans and spans[-1][1] == num:
                spans[-1][1] = num + 1
            else:
                spans.append([num, num + 1])
        with self.nc.Block() as block:
            @block.gpsimd
            def _(pool):
                for lo, hi in spans:
                    pool.sem_clear(range(lo, hi))
        for s in self.sems:
            self.nc.release_semaphore(s)
        self.sems = []


def stage_project(c):
    nc, A, bank = c.nc, c.A, c.bank
    RING = 4
    with ExitStack() as es:
        def sb(name, shape, dt=F32):
            return es.enter_context(nc.sbuf_tensor(name, shape, dt))
        xT = sb("xT", [P, KD, NT])
        wblk = sb("wblk", [P, RING, KD, P])
        wrow = sb("wrow", [P, 2, KD, 512])
        wsmall = sb("wsmall", [P, KD, NSMALL])
        krow = sb("krow", [P, 2, NTILE, P])
        crow = sb("crow", [NS + 3, CONV])
        x_in, small_in, state_in = c.sem("x_in"), c.sem("wsmall_in"), c.sem("state_conv_in")
        blk_in = [c.sem(f"wblk_in{i}") for i in range(RING)]
        row_in = [c.sem(f"wrow_in{i}") for i in range(2)]
        blk_mm, blk_act, blk_dve = c.sem("blk_mm"), c.sem("blk_act"), c.sem("blk_dve")
        k_mm, k_ev = c.sem("krow_mm"), c.sem("krow_ev")
        row_mm, row_ev = c.sem("row_mm"), c.sem("row_ev")
        pad_done, store = c.sem("pad_done"), c.sem("proj_store", True)
        kst = [c.sem(f"krow_store{i}", True) for i in range(2)]
        NROW = 3 * NTILE

        with nc.Block() as block:
            @block.sync
            def _(sp):
                sp.dma_start(xT[:], A["xT"]).then_inc(x_in, 16)
                for j in range(NBLK):
                    if j >= RING:
                        sp.wait_ge(blk_mm, j - RING + 1)
                    sp.dma_start(wblk[:, j % RING], A["w_blk"][j]).then_inc(blk_in[j % RING], 16)
                    if j == 2:
                        sp.dma_start(c.convin_s[:, :, :, 0:3], A["state_convT"]).then_inc(state_in, 16)
                for i in range(2):
                    sp.dma_start(wrow[:, i], A["w_row"][i]).then_inc(row_in[i], 16)
                sp.dma_start(wsmall[:], A["w_small"]).then_inc(small_in, 16)
                sp.wait_ge(state_in, 16)

            @block.tensor
            def _(pe):
                pe.wait_ge(x_in, 16)
                for j in range(NBLK):
                    pe.wait_ge(blk_in[j % RING], 16 * (j // RING + 1))
                    if j >= 2:
                        pe.wait_ge(blk_act, j - 1)
                        pe.wait_ge(blk_dve, min(j - 1, B_Q))
                    for q in range(2):
                        for k in range(KD):
                            last = nc.tensor.matmul(c.pair(j % 2)[:, q], wblk[:, j % RING, k],
                                                    xT[:, k, q * HALF:(q + 1) * HALF],
                                                    start=k == 0, stop=k == KD - 1)
                    if j < B_Q:
                        for k in range(KD):
                            last = nc.tensor.matmul(bank[4 + j % 2][0:NS + 3, 0:P], xT[:, k, SEQ - 3:NT],
                                                    wblk[:, j % RING, k], start=k == 0, stop=k == KD - 1)
                    last.then_inc(blk_mm, 1)
                    if B_K < j <= B_QI:
                        pe.wait_ge(blk_act, j)
                        if j >= B_K + 3:
                            pe.wait_ge(k_ev, j - B_K - 2)
                        for t in range(NTILE):
                            dst = bank[4 + j % 2][:, t * P:(t + 1) * P] if t < STILE else bank[6 + j % 2][0:NS, 0:P]
                            last = nc.tensor.transpose(dst, c.kT[:, j - 1 - B_K, cols(t)], c.ident[:])
                        last.then_inc(k_mm, 1)
                n = 0
                for i in range(3):
                    if i < 2:
                        pe.wait_ge(row_in[i], 16)
                    else:
                        pe.wait_ge(small_in, 16)
                    for t in range(NTILE):
                        if n < 2:
                            pe.wait_ge(blk_act, NBLK)
                        if n >= 4:
                            pe.wait_ge(row_ev, n - 3)
                        w = wrow[:, i] if i < 2 else wsmall
                        width = 512 if i < 2 else NSMALL
                        for k in range(KD):
                            last = nc.tensor.matmul(bank[n % 4][0:rows(t), 0:width], xT[:, k, cols(t)],
                                                    w[:, k, 0:width], start=k == 0, stop=k == KD - 1)
                        last.then_inc(row_mm, 1)
                        n += 1

            @block.scalar
            def _(act):
                for j in range(NBLK):
                    act.wait_ge(blk_mm, j + 1)
                    if j < B_Q:
                        if j == 0:
                            act.wait_ge(state_in, 16)
                        nc.scalar.activation(c.convin_s[:, j, :, 3:3 + TS], c.pair(j % 2)[:, 1, SEQ - HALF:HALF]
                                             .rearrange("p (b t) -> p b t", b=NB), ACT.Copy)
                        nc.scalar.activation(c.convin_p[:, j, 3:3 + HALF], c.pair(j % 2)[:, 0], ACT.Copy)
                        nc.scalar.activation(c.convin_p[:, j, 3 + HALF:3 + SEQ], c.pair(j % 2)[:, 1, 0:SEQ - HALF],
                                             ACT.Copy).then_inc(blk_act, 1)
                        continue
                    if j < B_K:
                        dst = c.qT[:, j - B_Q]
                    elif j < B_QI:
                        dst = c.kT[:, j - B_K]
                    elif j < B_KI:
                        dst = c.qiT[:, j - B_QI]
                    else:
                        dst = c.kiT[:]
                    nc.scalar.activation(dst.rearrange("p (c t) -> p c t", c=2), c.pair(j % 2),
                                         ACT.Copy).then_inc(blk_act, 1)
                n = 0
                for i in range(3):
                    for t in range(NTILE):
                        act.wait_ge(row_mm, n + 1)
                        dst = (c.z, c.v, c.small)[i]
                        nc.scalar.activation(dst[0:rows(t), t], bank[n % 4][0:rows(t), 0:dst.shape[2]],
                                             ACT.Copy).then_inc(row_ev, 1)
                        n += 1

            @block.vector
            def _(dve):
                nc.vector.memset(c.convin_p[:, :, 0:3], 0.0).then_inc(pad_done, 1)
                for j in range(B_Q):
                    dve.wait_ge(blk_mm, j + 1)
                    nc.vector.tensor_copy(crow[:, j * P:(j + 1) * P],
                                          bank[4 + j % 2][0:NS + 3, 0:P]).then_inc(blk_dve, 1)
                for i in range(4):
                    dve.wait_ge(k_mm, i + 1)
                    if i >= 2:
                        dve.wait_ge(kst[i % 2], 32)
                    nc.vector.tensor_copy(krow[:, i % 2, 0:STILE],
                                          bank[4 + (i + 1) % 2][:].rearrange("p (t n) -> p t n", t=STILE))
                    nc.vector.tensor_copy(krow[0:NS, i % 2, STILE],
                                          bank[6 + (i + 1) % 2][0:NS, 0:P]).then_inc(k_ev, 1)
                dve.wait_ge(pad_done, 1)

            @block.gpsimd
            def _(pool):
                pool.wait_ge(blk_dve, B_Q)
                pool.dma_start(A["conv_p"][0], crow[0:3, :]).then_inc(store, 16)
                for b in range(NB):
                    pool.dma_start(A["conv_s"][b], crow[3 + TS * b + 1:3 + TS * (b + 1), :]).then_inc(store, 16)
                for j in range(B_K, B_QI):
                    pool.wait_ge(k_ev, j - B_K + 1)
                    o = (j - B_K) * P
                    pool.dma_start(A["k_p"].rearrange("(t p) n -> p t n", p=P)[:, :, o:o + P],
                                   krow[:, j % 2, 0:STILE]).then_inc(kst[j % 2], 16)
                    pool.dma_start(A["k_s"][:, o:o + P], krow[0:NS, j % 2, STILE]).then_inc(kst[j % 2], 16)
                pool.wait_ge(row_ev, NROW)
                pool.dma_start(A["v_p"].rearrange("(t p) n -> p t n", p=P), c.v[:, 0:STILE]).then_inc(store, 16)
                pool.dma_start(A["v_s"], c.v[0:NS, STILE]).then_inc(store, 16)
                pool.dma_start(A["kidx_p"].rearrange("(t p) n -> p t n", p=P),
                               c.small[:, 0:STILE, S_KI:S_KI + HD]).then_inc(store, 16)
                pool.dma_start(A["kidx_s"], c.small[0:NS, STILE, S_KI:S_KI + HD]).then_inc(store, 16)
                pool.wait_ge(store, 16 * (1 + NB + 4))
                pool.wait_ge(kst[0], 64)
                pool.wait_ge(kst[1], 64)


def stage_ssd(c):
    nc, A, bank = c.nc, c.A, c.bank
    with ExitStack() as es:
        def sb(name, shape, dt=F32):
            return es.enter_context(nc.sbuf_tensor(name, shape, dt))
        convw, convb = sb("convw", [P, KD, 4]), sb("convb", [P, KD])
        acc = sb("conv_acc", [P, 2, NT])
        xbcT = sb("xbcT", [P, KD, NT])
        xsN, BN = sb("xsN", [P, 512]), sb("BN", [P, 256])
        dtN, aN = sb("dtN", [P, NTILE, H]), sb("aN", [P, NTILE, H])
        negA = sb("negA", [P, H])
        u, w1, w2 = sb("sp_u", [P, NTILE, H]), sb("sp_1", [P, NTILE, H]), sb("sp_2", [P, NTILE, H])
        aexp = sb("aexp", [P, H, P])
        seg, M = sb("seg", [P, H, P]), sb("Mdecay", [P, H, P])
        Sm = sb("Smask", [P, 2, P])
        acum, last_, dte, ea, edl = (sb(n, [P, H]) for n in ("acum", "alast", "dte", "ea", "edl"))
        xd, xdd, y, t1 = (sb(n, [P, 512]) for n in ("xd", "xdd", "yssd", "yt"))
        hT = sb("stateT", [P, 512])
        rms = sb("rms", [P, 4])
        CTm = sb("CTm", [P, 2, NB, NS])
        stT = sb("stT", [P, NB, 512])
        stN = sb("stN", [P, NB, 4, P])
        aexp64 = sb("aexp64", [NS, H, HD])
        xddm = sb("xddm", [NS, NB, 512])
        eD = sb("eD", [P, 4, NB])
        ssmo = sb("ssmo", [P, 4, P])

        memT = stT[:, 0:4].rearrange("p a n -> p (a n)").rearrange("p (k m) -> p k m", k=KD)
        mvT, mko = stT[:, 4].rearrange("p (a m) -> p a m", a=2), stT[:, 5:7]
        wkv = stN[:, 0:6].rearrange("p b k n -> p (b k n)").rearrange("p (r k n) -> p r k n", r=3, k=KD)
        mem_in, wkv_in = c.sem("mem_in"), [c.sem(f"wkv_in{i}") for i in range(3)]
        mT_mm, mT_ev, mrow_mm, mrow_ev = (c.sem("mem_" + n) for n in ("T_mm", "T_ev", "row_mm", "row_ev"))
        conv_in, st_in = c.sem("ssd_in"), c.sem("state_in")
        conv_done, xbc_ready = c.sem("conv_done"), c.sem("xbc_ready")
        d_own, a_own = c.sem("ssd_dve"), c.sem("ssd_act")
        names = ("dt_pre", "dt_e", "tr_mm", "tr_ev", "a_ready", "cum_mm", "seg_pre", "decay", "ea_pre", "ea_done",
                 "m_ready", "y_mm", "y_done", "sz_done", "rms_pre", "rms_sqrt", "yn_ready", "ynT_mm", "ynT_ev",
                 "xdd_ready", "st_mm", "h_ready", "ho_mm", "ho_ev", "ns_mm", "ns_ev", "eD_mm", "eD_done", "ctm")
        s = {n: c.sem("ssd_" + n) for n in names}
        store = c.sem("ssd_store")
        vec = lambda name, n=P: c.vecs[0:n, VEC[name][0]:VEC[name][0] + VEC[name][1]]

        def by_head(ap, n, width=HD):
            return ap.unsqueeze(2).to_broadcast([n, H, width])

        with nc.Block() as block:
            @block.sync
            def _(sp):
                sp.dma_start(convw[:], A["conv_w"]).then_inc(conv_in, 16)
                sp.dma_start(convb[:], A["conv_b"]).then_inc(conv_in, 16)
                sp.dma_start(memT[:], A["memT"]).then_inc(mem_in, 16)
                for j in range(2 * MH):
                    if j >= 3:
                        sp.wait_ge(mT_mm, j - 2)
                    src = A["w_ck" if j < MH else "w_cv"][:, :, (j % MH) * P:(j % MH + 1) * P]
                    sp.dma_start(wkv[:, j % 3], src).then_inc(wkv_in[j % 3], 16)
                sp.wait_ge(mrow_ev, 2 * MH)
                sp.dma_start(A["memk_p"].rearrange("(k p) n -> p k n", p=P), mko[:]).then_inc(store, 16)
                sp.dma_start(A["memv_p"].rearrange("(k p) n -> p k n", p=P), c.mv[:]).then_inc(store, 16)
                sp.wait_ge(store, 32)
                sp.dma_start(stT[:], A["state_ssmT"]).then_inc(st_in, 16)
                sp.dma_start(stN[:], A["state_ssm"]).then_inc(st_in, 16)
                sp.wait_ge(s["ho_ev"], 1)
                sp.dma_start(A["ssm_p"].rearrange("(k p) n -> p k n", p=P), ssmo[:]).then_inc(store, 16)
                sp.wait_ge(s["ns_ev"], NB)
                sp.dma_start(A["ssm_s"].rearrange("b (k p) n -> p b k n", p=P), stN[:]).then_inc(store, 16)
                sp.wait_ge(store, 64)

            @block.tensor
            def _(pe):
                pe.wait_ge(mem_in, 16)

                def mem_rows(j):
                    pe.wait_ge(mT_ev, j + 1)
                    if j >= 2:
                        pe.wait_ge(mrow_ev, j - 1)
                    src = c.mkT[:, j] if j < MH else mvT[:, j % 2]
                    for m in range(2):
                        ins = nc.tensor.transpose(bank[2 + j % 2][:, m * P:(m + 1) * P], src[:, m * P:(m + 1) * P],
                                                  c.ident[:])
                    ins.then_inc(mrow_mm, 1)

                for j in range(2 * MH):
                    pe.wait_ge(wkv_in[j % 3], 16 * (j // 3 + 1))
                    if j >= 2:
                        pe.wait_ge(mT_ev, j - 1)
                    for k in range(KD):
                        ins = nc.tensor.matmul(bank[j % 2][:, 0:MEM], wkv[:, j % 3, k], memT[:, k],
                                               start=k == 0, stop=k == KD - 1)
                    ins.then_inc(mT_mm, 1)
                    if j:
                        mem_rows(j - 1)
                mem_rows(2 * MH - 1)

                pe.wait_ge(mrow_ev, 2 * MH)
                pe.wait_ge(xbc_ready, 2 * KD)
                for t in range(NTILE):
                    n = rows(t)
                    sample = t == STILE
                    tri = c.tri if not sample else c.triS
                    if t:
                        pe.wait_ge(s["ynT_ev"], t)
                        pe.wait_ge(s["y_done"], t)
                        pe.wait_ge(s["h_ready"], t)
                    for k in range(6):
                        dst = bank[0][0:n, k * P:(k + 1) * P] if k < 4 else bank[1][0:n, (k - 4) * P:(k - 3) * P]
                        ins = nc.tensor.transpose(dst, xbcT[:, k, cols(t)], c.ident[:])
                    ins.then_inc(s["tr_mm"], 1)
                    pe.wait_ge(s["a_ready"], t + 1)
                    nc.tensor.matmul(bank[2][0:n, 0:H], tri[0:n, 0:n], aN[0:n, t], start=True, stop=True)
                    nc.tensor.matmul(bank[2][0:n, H:2 * H], c.ones[0:n, 0:n] if not sample else c.onesS[:],
                                     aN[0:n, t], start=True, stop=True)
                    for h in range(H):
                        nc.tensor.matmul(bank[3 + h // 4][0:n, (h % 4) * n:(h % 4 + 1) * n], aexp[0:n, h, 0:n],
                                         tri[0:n, 0:n], start=True, stop=True)
                    for g in range(2):
                        ins = nc.tensor.matmul(bank[5][0:n, g * n:(g + 1) * n], xbcT[:, 4 + g, cols(t)],
                                               xbcT[:, 6 + g, cols(t)], start=True, stop=True)
                    ins.then_inc(s["cum_mm"], 1)
                    pe.wait_ge(s["m_ready"], t + 1)
                    for h in range(H):
                        ins = nc.tensor.matmul(bank[6][0:n, h * HD:(h + 1) * HD], M[0:n, h, 0:n],
                                               xd[0:n, h * HD:(h + 1) * HD], start=True, stop=True)
                    if sample:
                        pe.wait_ge(st_in, 32)
                        pe.wait_ge(s["ctm"], 1)
                        for g in range(2):
                            for b in range(NB):
                                ins = nc.tensor.matmul(bank[7][0:n, g * 256:(g + 1) * 256], CTm[:, g, b],
                                                       stT[:, b, g * 256:(g + 1) * 256],
                                                       start=b == 0, stop=b == NB - 1)
                    elif t:
                        for g in range(2):
                            ins = nc.tensor.matmul(bank[7][0:n, g * 256:(g + 1) * 256], xbcT[:, 6 + g, cols(t)],
                                                   hT[:, g * 256:(g + 1) * 256], start=True, stop=True)
                    ins.then_inc(s["y_mm"], 1)
                    if not sample:
                        pe.wait_ge(s["xdd_ready"], t + 1)
                        for g in range(2):
                            ins = nc.tensor.matmul(bank[0][:, g * 256:(g + 1) * 256], BN[:, g * P:(g + 1) * P],
                                                   xdd[:, g * 256:(g + 1) * 256], start=True, stop=True)
                        ins.then_inc(s["st_mm"], 1)
                    pe.wait_ge(s["yn_ready"], t + 1)
                    for k in range(4):
                        ins = nc.tensor.transpose(bank[1][:, k * n:(k + 1) * n], y[0:n, k * P:(k + 1) * P],
                                                  c.ident[0:n, 0:n])
                    ins.then_inc(s["ynT_mm"], 1)
                pe.wait_ge(s["h_ready"], STILE)
                for k in range(4):
                    ins = nc.tensor.transpose(bank[3][:, k * P:(k + 1) * P], hT[:, k * P:(k + 1) * P], c.ident[:])
                ins.then_inc(s["ho_mm"], 1)
                pe.wait_ge(s["xdd_ready"], NTILE)
                for k in range(4):
                    ins = nc.tensor.matmul(bank[2][:, 64 + k * NB:64 + (k + 1) * NB],
                                           aexp64[:].rearrange("p h d -> p (h d)")[:, k * P:(k + 1) * P],
                                           c.bsel[:], start=True, stop=True)
                ins.then_inc(s["eD_mm"], 1)
                for b in range(NB):
                    if b >= 2:
                        pe.wait_ge(s["ns_ev"], b - 1)
                    for k in range(4):
                        ins = nc.tensor.matmul(bank[4 + b % 2][:, k * P:(k + 1) * P], xddm[:, b, k * P:(k + 1) * P],
                                               BN[0:NS, (k // 2) * P:(k // 2 + 1) * P], start=True, stop=True)
                    ins.then_inc(s["ns_mm"], 1)

            @block.scalar
            def _(act):
                link = Link(act, a_own)
                act.wait_ge(s["dt_pre"], 1)
                link(nc.scalar.activation(negA[:], vec("a_log"), ACT.Exp), s["dt_e"])
                link(nc.scalar.activation(u[:], w1[:], ACT.Exp), s["dt_e"])

                def mem_row(j):
                    act.wait_ge(mrow_mm, j + 1)
                    dst = (mko if j < MH else c.mv)[:, :, (j % MH) * P:(j % MH + 1) * P]
                    nc.scalar.activation(dst, bank[2 + j % 2][:, 0:MEM].rearrange("p (m n) -> p m n", m=2),
                                         ACT.Copy).then_inc(mrow_ev, 1)

                for k in range(KD):
                    act.wait_ge(mT_mm, k + 1)
                    if k >= MH + 2:
                        act.wait_ge(mrow_mm, k - 1)
                    nc.scalar.activation(c.mkT[:, k] if k < MH else mvT[:, k % 2], bank[k % 2][:, 0:MEM],
                                         ACT.Copy).then_inc(mT_ev, 1)
                    if k:
                        mem_row(k - 1)
                    act.wait_ge(conv_done, 2 * (k + 1))
                    nc.scalar.activation(xbcT[:, k, 0:SEQ], acc[:, k % 2, 0:SEQ], ACT.Silu,
                                         bias=convb[:, k:k + 1]).then_inc(xbc_ready, 1)
                    nc.scalar.activation(xbcT[:, k, SEQ:NT], acc[:, k % 2, SEQ:NT], ACT.Silu,
                                         bias=convb[:, k:k + 1]).then_inc(xbc_ready, 1)
                mem_row(2 * MH - 1)
                for t in range(NTILE):
                    n = rows(t)
                    nc.scalar.activation(c.z[0:n, t], c.z[0:n, t], ACT.Silu).then_inc(s["sz_done"], 1)
                for t in range(NTILE):
                    n = rows(t)
                    act.wait_ge(s["seg_pre"], t + 1)
                    nc.scalar.activation(seg[0:n, :, 0:n], seg[0:n, :, 0:n], ACT.Exp).then_inc(s["decay"], 1)
                    nc.scalar.activation(ea[0:n, :], acum[0:n, :], ACT.Exp).then_inc(s["ea_done"], 1)
                    nc.scalar.activation(dte[0:n, :], dte[0:n, :], ACT.Exp).then_inc(s["ea_done"], 1)
                    nc.scalar.activation(edl[0:n, :], last_[0:n, :], ACT.Exp).then_inc(s["ea_done"], 1)
                    act.wait_ge(s["rms_pre"], t + 1)
                    nc.scalar.activation(rms[0:n, 1:2], rms[0:n, 1:2], ACT.Sqrt).then_inc(s["rms_sqrt"], 1)
                    act.wait_ge(s["ynT_mm"], t + 1)
                    nc.scalar.activation(c.mixedT[:, 0:4, cols(t)],
                                         bank[1][:, 0:4 * n].rearrange("p (k n) -> p k n", k=4),
                                         ACT.Copy).then_inc(s["ynT_ev"], 1)
                act.wait_ge(s["ho_mm"], 1)
                nc.scalar.activation(ssmo[:], bank[3][:].rearrange("p (k n) -> p k n", k=4),
                                     ACT.Copy).then_inc(s["ho_ev"], 1)
                act.wait_ge(s["eD_mm"], 1)
                nc.scalar.activation(eD[:], bank[2][:, 64:64 + 4 * NB].rearrange("p (k b) -> p k b", k=4),
                                     ACT.Exp).then_inc(s["eD_done"], 1)

            @block.vector
            def _(dve):
                V = nc.vector
                link = Link(dve, d_own)
                link(V.memset(aN[:], 0.0))
                for t in range(NTILE):
                    link(V.tensor_tensor(dtN[0:rows(t), t], c.small[0:rows(t), t, S_DT:S_DT + H],
                                         vec("dt_bias", rows(t)), ALU.add))
                link(V.memset(w1[:], 0.0))
                for t in range(NTILE):
                    n = rows(t)
                    link(V.tensor_scalar(w1[0:n, t], dtN[0:n, t], -1.0, None, ALU.mult))
                    link(V.tensor_tensor(w1[0:n, t], w1[0:n, t], dtN[0:n, t], ALU.min),
                         s["dt_pre"] if t == STILE else None)
                dve.wait_ge(s["dt_e"], 2)
                link(V.tensor_scalar(negA[:], negA[:], -1.0, None, ALU.mult))
                link(V.tensor_scalar(w1[:], u[:], 2.0, None, ALU.add))
                link(V.reciprocal(w1[:], w1[:]))
                link(V.tensor_tensor(u[:], u[:], w1[:], ALU.mult))
                link(V.tensor_tensor(w1[:], u[:], u[:], ALU.mult))
                link(V.tensor_scalar(w2[:], w1[:], 1 / 19, 1 / 17, ALU.mult, ALU.add))
                for q in (15, 13, 11, 9, 7, 5, 3, 1):
                    link(V.tensor_tensor(w2[:], w2[:], w1[:], ALU.mult))
                    link(V.tensor_scalar(w2[:], w2[:], 1 / q, None, ALU.add))
                link(V.tensor_tensor(w2[:], w2[:], u[:], ALU.mult))
                for t in range(NTILE):
                    n = rows(t)
                    link(V.tensor_scalar(dtN[0:n, t], dtN[0:n, t], 0.0, None, ALU.max))
                    link(V.scalar_tensor_tensor(dtN[0:n, t], w2[0:n, t], 2.0, dtN[0:n, t], ALU.mult, ALU.add))
                    link(V.tensor_tensor(aN[0:n, t], dtN[0:n, t], negA[0:n, :], ALU.mult))
                dve.wait_ge(conv_in, 32)
                for k in range(KD):
                    if k >= 2:
                        dve.wait_ge(xbc_ready, 2 * (k - 1))
                    ap = acc[:, k % 2, 0:SEQ]
                    as_ = acc[:, k % 2, SEQ:NT].rearrange("p (b t) -> p b t", b=NB)
                    for tap in range(4):
                        w = convw[:, k, tap:tap + 1]
                        sem = conv_done if tap == 3 else None
                        xp, xs = c.convin_p[:, k, tap:tap + SEQ], c.convin_s[:, k, :, tap:tap + TS]
                        if tap == 0:
                            link(V.tensor_scalar(ap, xp, w, None, ALU.mult))
                            link(V.tensor_scalar(as_, xs, w, None, ALU.mult))
                        else:
                            link(V.scalar_tensor_tensor(ap, xp, w, ap, ALU.mult, ALU.add), sem)
                            link(V.scalar_tensor_tensor(as_, xs, w, as_, ALU.mult, ALU.add), sem)
                dve.wait_ge(xbc_ready, 2 * KD)
                for g in range(2):
                    link(V.tensor_tensor(CTm[:, g], xbcT[:, 6 + g, SEQ:NT].unsqueeze(1).to_broadcast([P, NB, NS]),
                                         c.bcol[:], ALU.mult), s["ctm"] if g else None)
                for t in range(NTILE):
                    n = rows(t)
                    sample = t == STILE
                    hd = lambda ap: ap[0:n, :].rearrange("p (h d) -> p h d", h=H)
                    if t:
                        dve.wait_ge(s["cum_mm"], t)
                        dve.wait_ge(s["st_mm"], t)
                    link(V.tensor_copy(aexp[0:n, :, 0:n], by_head(aN[0:n, t], n, n)), s["a_ready"])
                    dve.wait_ge(s["tr_mm"], t + 1)
                    link(V.tensor_copy(xsN[0:n, :], bank[0][0:n, :]))
                    link(V.tensor_copy(BN[0:n, :], bank[1][0:n, 0:256]))
                    if t:
                        dve.wait_ge(s["y_mm"], t)
                    link(V.tensor_tensor(hd(xd), hd(xsN), by_head(dtN[0:n, t], n), ALU.mult))
                    dve.wait_ge(s["cum_mm"], t + 1)
                    link(V.tensor_copy(acum[0:n, :], bank[2][0:n, 0:H]))
                    link(V.tensor_copy(last_[0:n, :], bank[2][0:n, H:2 * H]))
                    link(V.tensor_tensor(dte[0:n, :], last_[0:n, :], acum[0:n, :], ALU.subtract))
                    for q in range(2):
                        link(V.tensor_tensor(seg[0:n, 4 * q:4 * q + 4, 0:n],
                                             bank[3 + q][0:n, 0:4 * n].rearrange("p (h i) -> p h i", h=4),
                                             acum[0:n, 4 * q:4 * q + 4].unsqueeze(2).to_broadcast([n, 4, n]),
                                             ALU.subtract))
                    link(V.tensor_scalar(seg[0:n, :, 0:n], seg[0:n, :, 0:n], 0.0, None, ALU.min), s["seg_pre"])
                    tri = c.tri[0:n, 0:n] if not sample else c.triS[:]
                    link(V.tensor_tensor(Sm[0:n, :, 0:n], bank[5][0:n, 0:2 * n].rearrange("p (g i) -> p g i", g=2),
                                         tri.unsqueeze(1).to_broadcast([n, 2, n]), ALU.mult))
                    dve.wait_ge(s["decay"], t + 1)
                    for g in range(2):
                        link(V.tensor_tensor(M[0:n, 4 * g:4 * g + 4, 0:n], seg[0:n, 4 * g:4 * g + 4, 0:n],
                                             Sm[0:n, g, 0:n].unsqueeze(1).to_broadcast([n, 4, n]), ALU.mult),
                             s["m_ready"] if g else None)
                    dve.wait_ge(s["ea_done"], 3 * (t + 1))
                    link(V.tensor_tensor(hd(xdd), hd(xd), by_head(dte[0:n, :], n), ALU.mult),
                         s["xdd_ready"] if not sample else None)
                    if t:
                        dve.wait_ge(s["ynT_mm"], t)
                    link(V.tensor_tensor(hd(y), hd(xsN), by_head(vec("d_skip", n), n), ALU.mult))
                    dve.wait_ge(s["y_mm"], t + 1)
                    if t:
                        link(V.tensor_tensor(hd(t1), hd(bank[7]), by_head(ea[0:n, :], n), ALU.mult))
                        link(V.tensor_tensor(y[0:n, :], y[0:n, :], t1[0:n, :], ALU.add))
                    link(V.tensor_tensor(y[0:n, :], y[0:n, :], bank[6][0:n, :], ALU.add), s["y_done"])
                    if not sample:
                        dve.wait_ge(s["st_mm"], t + 1)
                        if t:
                            link(V.tensor_tensor(hd(hT), hd(hT), by_head(edl[:], P), ALU.mult))
                            link(V.tensor_tensor(hT[:], hT[:], bank[0][:], ALU.add), s["h_ready"])
                        else:
                            link(V.tensor_copy(hT[:], bank[0][:]), s["h_ready"])
                    dve.wait_ge(s["sz_done"], t + 1)
                    link(V.tensor_tensor(y[0:n, :], y[0:n, :], c.z[0:n, t], ALU.mult))
                    link(V.tensor_tensor_reduce(out=t1[0:n, :], in0=y[0:n, :], in1=y[0:n, :], scale=1.0, scalar=0.0,
                                                op0=ALU.mult, op1=ALU.add, accum_out=rms[0:n, 0:1]))
                    link(V.tensor_scalar(rms[0:n, 1:2], rms[0:n, 0:1], 1 / 512, EPS, ALU.mult, ALU.add), s["rms_pre"])
                    dve.wait_ge(s["rms_sqrt"], t + 1)
                    link(V.reciprocal(rms[0:n, 2:3], rms[0:n, 1:2]))
                    link(V.scalar_tensor_tensor(y[0:n, :], y[0:n, :], rms[0:n, 2:3], vec("ssd_norm_w", n),
                                                ALU.mult, ALU.mult), s["yn_ready"])
                link(V.tensor_copy(aexp64[:], by_head(aN[0:NS, STILE], NS)))
                for b in range(NB):
                    link(V.tensor_scalar(xddm[:, b], xdd[0:NS, :], c.bsel[:, b:b + 1], None, ALU.mult),
                         s["xdd_ready"] if b == NB - 1 else None)
                dve.wait_ge(s["eD_done"], 1)
                for b in range(NB):
                    dve.wait_ge(s["ns_mm"], b + 1)
                    for k in range(4):
                        link(V.scalar_tensor_tensor(stN[:, b, k], stN[:, b, k], eD[:, k, b:b + 1],
                                                    bank[4 + b % 2][:, k * P:(k + 1) * P], ALU.mult, ALU.add),
                             s["ns_ev"] if k == 3 else None)


def stage_dsa_prompt(c):
    nc, A, bank = c.nc, c.A, c.bank
    NTP = SEQ // P
    BW = 2 * P
    topk = min(256, SEQ // 4)
    with ExitStack() as es:
        def sb(name, shape, dt=F32):
            return es.enter_context(nc.sbuf_tensor(name, shape, dt))
        relb = sb("relb", [NBUCKET, H])
        relx = sb("relx", [NBUCKET, H, P])
        onehot = sb("onehot", [NBUCKET, 3 * P])
        spread = sb("spread", [P, H, 3 * P])
        T = sb("Tbias", [P, H, BW])
        relu = sb("relu", [P, 2, SEQ])
        sc = sb("scores", [P, SEQ])
        wi = sb("wi", [P, H])
        m8 = sb("max8", [P, 8])
        msk = sb("mask", [P, 2, SEQ])
        L = sb("logits", [P, 2, SEQ])
        E = sb("probs", [P, 2, SEQ])
        PT = sb("probsT", [P, 2, NTP, P])
        mx, den, rden = sb("mx", [P, H]), sb("den", [P, H]), sb("rden", [P, H])
        o = sb("att", [P, 512])
        scratch = nc.dram_tensor("bias_scratch", [P, H * 3 * P], F32, kind="Internal").ap()

        pt = c.ptab
        names = ("in", "relx", "sp_mm", "sp_ev", "sp_st", "T_in", "idx_mm", "relu", "relu_used", "mask",
                 "qk_mm", "logit", "exp", "tr_mm", "pt", "pv_mm", "att", "attT_mm", "attT")
        s = {n: c.sem("dsap_" + n) for n in names}
        d_own = c.sem("dsap_dve")

        with nc.Block() as block:
            @block.sync
            def _(sp):
                sp.dma_start(relb[:], A["rel_bias"]).then_inc(s["in"], 16)
                sp.dma_start(onehot[:], A["bucket_rev"]).then_inc(s["in"], 16)
                sp.wait_ge(s["sp_ev"], H)
                sp.dma_start(scratch[:, :], spread[:].rearrange("p h m -> p (h m)")).then_inc(s["sp_st"], 16)
                sp.wait_ge(s["sp_st"], 16)
                skew = bass.AP(scratch.tensor, P - 1, [[H * 3 * P - 1, P], [3 * P, H], [1, BW]])
                sp.dma_start(T[:], skew).then_inc(s["T_in"], 16)
                sp.dma_start(pt[:], A["page_table"]).then_inc(c.pt_in, 16)
                sp.wait_ge(c.pt_in, 16)
                for b in range(NB):
                    for j in range(NPAGE):
                        page = sp.value_load(pt[0:1, b * NPAGE + j:b * NPAGE + j + 1], min_val=0,
                                             max_val=A["kidxT"].shape[0] - 1)
                        sp.dma_start(c.kiS(b)[:, j * PAGE:(j + 1) * PAGE],
                                     A["kidxT"][bass.ds(page, 1)].rearrange("a d n -> d (a n)")
                                     ).then_inc(c.ki_in, 16)
                sp.wait_ge(s["T_in"], 16)
                sp.wait_ge(c.ki_in, 16 * NB * NPAGE)

            @block.tensor
            def _(pe):
                pe.wait_ge(s["in"], 32)
                pe.wait_ge(s["relx"], 1)
                for h in range(H):
                    if h >= 2:
                        pe.wait_ge(s["sp_ev"], h - 1)
                    nc.tensor.matmul(bank[h % 2][:, 0:3 * P], relx[:, h], onehot[:], start=True,
                                     stop=True).then_inc(s["sp_mm"], 1)
                pe.wait_ge(s["sp_ev"], H)

                def scores(t):
                    nk = (t + 1) * P
                    for h in range(H):
                        n = t * H + h
                        if n >= 2:
                            pe.wait_ge(s["relu"], n - 1)
                        lo = HD * (h % 2)
                        nc.tensor.matmul(bank[h % 2][:, 0:nk], c.qiT[lo:lo + HD, h // 2, cols(t)],
                                         c.kiT[lo:lo + HD, 0:nk], start=True, stop=True).then_inc(s["idx_mm"], 1)

                def attend(t):
                    nk = (t + 1) * P

                    def tail(h):
                        n = t * H + h
                        pe.wait_ge(s["exp"], n + 1)
                        if n >= 2:
                            pe.wait_ge(s["pt"], n - 1)
                        for k in range(t + 1):
                            ins = nc.tensor.transpose(bank[4 + h % 2][:, k * P:(k + 1) * P],
                                                      E[:, h % 2, k * P:(k + 1) * P], c.ident[:])
                        ins.then_inc(s["tr_mm"], 1)
                        pe.wait_ge(s["pt"], n + 1)
                        for k in range(t + 1):
                            ins = nc.tensor.matmul(bank[6][:, h * HD:(h + 1) * HD], PT[:, h % 2, k],
                                                   c.v[:, k, h * HD:(h + 1) * HD], start=k == 0, stop=k == t)
                        ins.then_inc(s["pv_mm"], 1)

                    for h in range(H):
                        n = t * H + h
                        if n >= 2:
                            pe.wait_ge(s["logit"], n - 1)
                        lo = HD * (h % 2)
                        nc.tensor.matmul(bank[2 + h % 2][:, 0:nk], c.qT[lo:lo + HD, h // 2, cols(t)],
                                         c.kT[lo:lo + HD, h // 2, 0:nk], start=True, stop=True).then_inc(s["qk_mm"], 1)
                        if h == 0 and t:
                            pe.wait_ge(s["att"], t)
                        if h:
                            tail(h - 1)
                    tail(H - 1)
                    pe.wait_ge(s["att"], t + 1)
                    if t:
                        pe.wait_ge(s["attT"], t)
                    for k in range(4):
                        ins = nc.tensor.transpose(bank[7][:, k * P:(k + 1) * P], o[:, k * P:(k + 1) * P], c.ident[:])
                    ins.then_inc(s["attT_mm"], 1)

                scores(0)
                for t in range(NTP):
                    if t + 1 < NTP:
                        scores(t + 1)
                    attend(t)

            @block.scalar
            def _(act):
                def relus(t):
                    nk = (t + 1) * P
                    for h in range(H):
                        n = t * H + h
                        act.wait_ge(s["idx_mm"], n + 1)
                        if n >= 2:
                            act.wait_ge(s["relu_used"], n - 1)
                        nc.scalar.activation(relu[:, h % 2, 0:nk], bank[h % 2][:, 0:nk], ACT.Relu,
                                             scale=HD ** -0.5).then_inc(s["relu"], 1)

                def attend(t):
                    nk = (t + 1) * P
                    for h in range(H):
                        n = t * H + h
                        act.wait_ge(s["logit"], n + 1)
                        if n >= 2:
                            act.wait_ge(s["tr_mm"], n - 1)
                        nc.scalar.activation(E[:, h % 2, 0:nk], L[:, h % 2, 0:nk], ACT.Exp, bias=mx[:, h:h + 1],
                                             accum_out=den[:, h:h + 1]).then_inc(s["exp"], 1)
                        act.wait_ge(s["tr_mm"], n + 1)
                        if n >= 2:
                            act.wait_ge(s["pv_mm"], n - 1)
                        nc.scalar.activation(PT[:, h % 2, 0:t + 1], bank[4 + h % 2][:, 0:nk].rearrange(
                            "p (k q) -> p k q", q=P), ACT.Copy).then_inc(s["pt"], 1)
                    act.wait_ge(s["attT_mm"], t + 1)
                    nc.scalar.activation(c.mixedT[:, 4:8, cols(t)], bank[7][:].rearrange("p (k q) -> p k q", k=4),
                                         ACT.Copy).then_inc(s["attT"], 1)

                relus(0)
                for t in range(NTP):
                    if t + 1 < NTP:
                        relus(t + 1)
                    attend(t)

            @block.vector
            def _(dve):
                V = nc.vector
                link = Link(dve, d_own)
                dve.wait_ge(s["in"], 32)
                link(V.tensor_copy(relx[:], relb[:].unsqueeze(2).to_broadcast([NBUCKET, H, P])), s["relx"])
                for h in range(H):
                    dve.wait_ge(s["sp_mm"], h + 1)
                    link(V.tensor_copy(spread[:, h], bank[h % 2][:, 0:3 * P]), s["sp_ev"])

                def select(t):
                    nk = (t + 1) * P
                    link(V.tensor_scalar(wi[:], c.small[:, t, S_WI:S_WI + H], H ** -0.5, None, ALU.mult))
                    for h in range(H):
                        dve.wait_ge(s["relu"], t * H + h + 1)
                        if h == 0:
                            link(V.tensor_scalar(sc[:, 0:nk], relu[:, 0, 0:nk], wi[:, 0:1], None, ALU.mult),
                                 s["relu_used"])
                        else:
                            link(V.scalar_tensor_tensor(sc[:, 0:nk], relu[:, h % 2, 0:nk], wi[:, h:h + 1],
                                                        sc[:, 0:nk], ALU.mult, ALU.add), s["relu_used"])
                    own = sc[:, t * P:nk]
                    link(V.tensor_tensor(own, own, c.low[:], ALU.mult))
                    link(V.tensor_tensor(own, own, c.lowneg[:], ALU.add))
                    if nk > topk:
                        for _ in range(topk // 8):
                            link(V.max(m8[:], sc[:, 0:nk]))
                            link(V.match_replace(sc[:, 0:nk], m8[:], sc[:, 0:nk], PICKED))
                        link(V.tensor_scalar(msk[:, t % 2, 0:nk], sc[:, 0:nk], -2.9e38, NOT_SELECTED, ALU.is_gt,
                                             ALU.mult))
                    else:
                        link(V.tensor_scalar(msk[:, t % 2, 0:nk], sc[:, 0:nk], -1.9e38, NOT_SELECTED, ALU.is_lt,
                                             ALU.mult))

                def attend(t):
                    nk = (t + 1) * P
                    far = max(0, nk - BW)
                    for h in range(H):
                        n = t * H + h
                        dve.wait_ge(s["qk_mm"], n + 1)
                        if n >= 2:
                            dve.wait_ge(s["exp"], n - 1)
                        ps, l = bank[2 + h % 2], L[:, h % 2]
                        a = VEC["bias_far"][0] + h
                        if far:
                            link(V.tensor_scalar(l[:, 0:far], ps[:, 0:far], HD ** -0.5, c.vecs[:, a:a + 1],
                                                 ALU.mult, ALU.add))
                        link(V.scalar_tensor_tensor(l[:, far:nk], ps[:, far:nk], HD ** -0.5,
                                                    T[:, h, BW - (nk - far):BW], ALU.mult, ALU.add))
                        link(V.tensor_tensor(l[:, 0:nk], l[:, 0:nk], msk[:, t % 2, 0:nk], ALU.add))
                        if t:
                            dve.wait_ge(s["exp"], t * H)
                        link(V.reduce_max(mx[:, h:h + 1], l[:, 0:nk], AX_X))
                        link(V.tensor_scalar(mx[:, h:h + 1], mx[:, h:h + 1], -1.0, None, ALU.mult), s["logit"])
                    dve.wait_ge(s["exp"], (t + 1) * H)
                    link(V.reciprocal(rden[:], den[:]))
                    dve.wait_ge(s["pv_mm"], (t + 1) * H)
                    if t:
                        dve.wait_ge(s["attT_mm"], t)
                    link(V.tensor_tensor(o[:].rearrange("p (h d) -> p h d", h=H),
                                         bank[6][:].rearrange("p (h d) -> p h d", h=H),
                                         rden[:].unsqueeze(2).to_broadcast([P, H, HD]), ALU.mult), s["att"])

                select(0)
                dve.wait_ge(s["T_in"], 16)
                for t in range(NTP):
                    if t + 1 < NTP:
                        select(t + 1)
                    attend(t)


def stage_dsa_sample(c):
    nc, A, bank = c.nc, c.A, c.bank
    HT = H * TS
    HB = NB // 2
    NKC = PAST // 512
    topk = min(256, (PAST + TS) // 4)
    UP = 512 // PAGE
    RING = KV_RING
    pt, ring = c.ptab, c.kvring
    with ExitStack() as es:
        def sb(name, shape, dt=F32):
            return es.enter_context(nc.sbuf_tensor(name, shape, dt))
        qiS = sb("qiS", [P, NB, H, TS])
        swapped = sb("qi_swapped", [P, 4, NS])
        L = sb("logitsS", [P, 2, NKEY])
        wv = sb("wv", [HT, NB])
        wx = sb("wx", [NS, H, TS])
        tsel = sb("tsel", [NS, TS])
        Wsel = sb("Wsel", [HT, NB, NS])
        rS = sb("reluS", [HT, NKEY])
        sc = sb("scS", [NS, NKEY])
        m8 = sb("m8S", [NS, 8])
        msk = sb("mskS", [NS, NKEY])
        relb = sb("relbS", [NBUCKET, H])
        RB = sb("RB", [NBUCKET, TS, HB, H, TS])
        oh = sb("ohS", [NBUCKET, PAST + TS])
        ohn = sb("ohn", [NBUCKET, TS, NS])
        exp_rows = sb("exp_rows", [NS, 2, P])
        hmask = sb("hmask", [P, 4, H])
        omask = sb("omask", [HT, 512])
        tsum = sb("tsum", [HT, TS])
        wmask = sb("wmask", [HT, NB, NS])
        Q = sb("Qblk", [P, 2, HB, 4, P])
        Qall = sb("Qall", [P, 2, 4, P])
        PT = sb("PTS", [P, NPAGE + 1, P])
        mx, ngm, den = sb("mxS", [P, 2, NKC + 1]), sb("ngm", [P, 2]), sb("denS", [P, 2, NKC + 1])
        dsum, rden = sb("dsum", [P, 2]), sb("rdenS", [P, 2])
        Om = rS[:, 0:1024].rearrange("r (a n) -> r a n", a=2)

        names = ("c_in", "swap_in", "wx", "wv_mm", "q_ready", "w_ready", "idx_mm", "relu",
                 "sel_mm", "sc_ready", "mask", "rb", "qblk", "log_mm", "logit", "mask_mm", "masked", "max", "exp",
                 "prob", "tr_mm", "pt", "pv_mm", "om", "ot_mm", "ot")
        s = {n: c.sem("dsas_" + n, n == "swap_in") for n in names}
        kv_in = [c.sem(f"kv_in{i}") for i in range(RING)]
        kv_used = c.sem("kv_used")
        d_own, a_own = c.sem("dsas_dve"), c.sem("dsas_act")

        def unit(g, kind, b, q):
            return (kind * 2 + g) * HB * NKC + (b * NKC + q if kind else q * HB + b)

        with nc.Block() as block:
            @block.sync
            def _(sp):
                for dst, src in ((relb, "rel_bias"), (oh, "bucket_past"), (ohn, "bucket_new"),
                                 (exp_rows, "expand_rows"), (hmask, "head_mask"), (omask, "out_mask"),
                                 (tsel, "t_sel"), (tsum, "t_sum"), (wmask, "w_mask")):
                    sp.dma_start(dst[:], A[src]).then_inc(s["c_in"], 16)
                for kind, src in enumerate((A["kT_pages"], A["v_pages"])):
                    for g in range(2):
                        for m in range(HB * NKC):
                            n = unit(g, kind, 0, 0) + m
                            b, q = (m // NKC, m % NKC) if kind else (m % HB, m // HB)
                            if n == 2:
                                sp.wait_ge(s["sel_mm"], NB)
                            if n >= RING:
                                sp.wait_ge(kv_used, n - RING + 1)
                            for j in range(UP):
                                at = (g * HB + b) * NPAGE + q * UP + j
                                page = sp.value_load(pt[0:1, at:at + 1], min_val=0, max_val=src.shape[0] - 1)
                                sp.dma_start(ring[:, n % RING, j * 512:(j + 1) * 512],
                                             src[bass.ds(page, 1)].rearrange("a p n -> p (a n)")
                                             ).then_inc(kv_in[n % RING], 16)

            @block.gpsimd
            def _(pool):
                for lo in (0, HD):
                    pool.dma_start(swapped[lo:lo + HD], c.qiT[HD - lo:P - lo, :, SEQ:NT]).then_inc(s["swap_in"], 16)
                pool.wait_ge(s["swap_in"], 32)

            @block.scalar
            def _(act):
                for b in range(NB):
                    for q in range(NKC + 1):
                        n = b * (NKC + 1) + q
                        act.wait_ge(s["idx_mm"], n + 1)
                        if b and q == 0:
                            act.wait_ge(s["sel_mm"], b)
                        w = 512 if q < NKC else NS
                        nc.scalar.activation(rS[:, q * 512:q * 512 + w], bank[4 + q % 3][0:HT, 0:w],
                                             ACT.Relu, scale=HD ** -0.5).then_inc(s["relu"], 1)
                for q in range(NKC + 1):
                    w = 512 if q < NKC else NS
                    src = bank[q] if q < NKC else bank[7]
                    if q == 0:
                        act.wait_ge(s["sel_mm"], NB)
                    nc.scalar.activation(sc[:, q * 512:q * 512 + w], src[0:NS, 0:w], ACT.Copy
                                         ).then_inc(s["sc_ready"], 1)
                for g in range(2):
                    for q in range(NKC + 1):
                        act.wait_ge(s["log_mm"], g * (NKC + 1) + q + 1)
                        w = 512 if q < NKC else NS
                        nc.scalar.activation(L[:, g, q * 512:q * 512 + w], bank[q][:, 0:w], ACT.Copy
                                             ).then_inc(s["logit"], 1)
                for g in range(2):
                    act.wait_ge(s["max"], g + 1)
                    for q in range(NKC + 1):
                        part = L[:, g, q * 512:q * 512 + (512 if q < NKC else NS)]
                        nc.scalar.activation(part, part, ACT.Exp, bias=ngm[:, g:g + 1],
                                             accum_out=den[:, g, q:q + 1]).then_inc(s["exp"], 1)
                for g in range(2):
                    for q in range(5):
                        act.wait_ge(s["tr_mm"], 5 * g + q + 1)
                        if g and q == 0:
                            act.wait_ge(s["pv_mm"], HB * g)
                        if q < 4:
                            nc.scalar.activation(PT[:, 4 * q:4 * q + 4],
                                                 bank[3 + q % 2][:].rearrange("p (k r) -> p k r", k=4),
                                                 ACT.Copy).then_inc(s["pt"], 1)
                        else:
                            nc.scalar.activation(PT[0:NS, NPAGE], bank[3 + q % 2][0:NS, 0:P], ACT.Copy
                                                 ).then_inc(s["pt"], 1)
                    act.wait_ge(s["ot_mm"], HB * (g + 1))
                    nc.scalar.activation(c.mixedT[:, 4:8, SEQ + HB * TS * g:SEQ + HB * TS * (g + 1)],
                                         bank[7][:, 128:128 + 4 * HB * TS].rearrange("p (k r) -> p k r", k=4),
                                         ACT.Copy).then_inc(s["ot"], 1)

            @block.tensor
            def _(pe):
                pe.wait_ge(s["wx"], 1)
                nc.tensor.matmul(bank[7][0:HT, 0:NB], wx[:].rearrange("r h t -> r (h t)"), c.bsel[:], start=True,
                                 stop=True).then_inc(s["wv_mm"], 1)
                pe.wait_ge(s["q_ready"], 1)
                pe.wait_ge(s["w_ready"], 1)
                for b in range(NB):
                    lo = HD * (b % 2)
                    lhsT = qiS[lo:lo + HD, b].rearrange("d h t -> d (h t)")
                    for q in range(NKC + 1):
                        n = b * (NKC + 1) + q
                        if q >= 3:
                            pe.wait_ge(s["relu"], n - 2)
                        elif b:
                            pe.wait_ge(s["relu"], b * (NKC + 1))
                        w, rhs = (512, c.kiS(b)[:, q * 512:(q + 1) * 512]) if q < NKC else (
                            NS, c.kiT[lo:lo + HD, SEQ:NT])
                        nc.tensor.matmul(bank[4 + q % 3][0:HT, 0:w], lhsT, rhs, start=True,
                                         stop=True).then_inc(s["idx_mm"], 1)
                    for q in range(NKC + 1):
                        pe.wait_ge(s["relu"], b * (NKC + 1) + q + 1)
                        w = 512 if q < NKC else NS
                        ins = nc.tensor.matmul(bank[q if q < NKC else 7][0:NS, 0:w], Wsel[:, b],
                                               rS[:, q * 512:q * 512 + w], start=b == 0, stop=b == NB - 1)
                    ins.then_inc(s["sel_mm"], 1)

                pe.wait_ge(s["rb"], 1)
                pe.wait_ge(s["qblk"], 3)
                for g in range(2):
                    for q in range(NKC + 1):
                        if g:
                            pe.wait_ge(s["logit"], q + 1)
                        elif q == 0:
                            pe.wait_ge(s["sc_ready"], NKC + 1)
                        w = 512 if q < NKC else NS
                        for b in range(HB if q < NKC else 0):
                            n = unit(g, 0, b, q)
                            pe.wait_ge(kv_in[n % RING], 16 * UP * (n // RING + 1))
                            kk = ring[:, n % RING].rearrange("p (j k n) -> p k j n", j=UP, k=4)
                            for k in range(4):
                                ins = nc.tensor.matmul(bank[q][:], Q[:, g, b, k], kk[:, k],
                                                       start=b == 0 and k == 0, stop=False)
                            ins.then_inc(kv_used, 1)
                        if q == NKC:
                            for k in range(4):
                                nc.tensor.matmul(bank[NKC][:, 0:NS], Qall[:, g, k], c.kT[:, k, SEQ:NT],
                                                 start=k == 0, stop=False)
                        for t in range(TS):
                            rhs = oh[:, q * 512 + TS - 1 - t:q * 512 + TS - 1 - t + 512] if q < NKC else ohn[:, t]
                            ins = nc.tensor.matmul(bank[q][:, 0:w], RB[:, t].rearrange("k b h t -> k (b h t)"), rhs,
                                                   start=False, stop=t == TS - 1)
                        ins.then_inc(s["log_mm"], 1)

                def masks(g):
                    for q in range(NKC + 1):
                        n = g * (NKC + 1) + q
                        if n >= 2:
                            pe.wait_ge(s["masked"], n - 1)
                        w = 512 if q < NKC else NS
                        nc.tensor.matmul(bank[1 + n % 2][:, 0:w], exp_rows[:, g], msk[:, q * 512:q * 512 + w],
                                         start=True, stop=True).then_inc(s["mask_mm"], 1)

                pe.wait_ge(s["mask"], 1)
                pe.wait_ge(s["logit"], 2 * (NKC + 1))
                masks(0)
                masks(1)
                for g in range(2):
                    pe.wait_ge(s["prob"], g + 1)
                    for q in range(5):
                        if q >= 2:
                            pe.wait_ge(s["pt"], 5 * g + q - 1)
                        for k in range(4 * q, min(4 * q + 4, NPAGE + 1)):
                            m = P if k < NPAGE else NS
                            ins = nc.tensor.transpose(bank[3 + q % 2][0:m, (k % 4) * P:(k % 4 + 1) * P],
                                                      L[:, g, k * P:k * P + m], c.ident[:])
                        ins.then_inc(s["tr_mm"], 1)
                    pe.wait_ge(s["pt"], 5 * (g + 1))

                    def out_T(b):
                        pe.wait_ge(s["om"], g * HB + b + 1)
                        for k in range(4):
                            at = 128 + k * HB * TS + b * TS
                            ins = nc.tensor.matmul(bank[7][:, at:at + TS], Om[:, b % 2, k * P:(k + 1) * P], tsum[:],
                                                   start=True, stop=True)
                        ins.then_inc(s["ot_mm"], 1)

                    for b in range(HB):
                        n0 = g * HB + b
                        if n0 >= 2:
                            pe.wait_ge(s["om"], n0 - 1)
                        for q in range(NKC):
                            n = unit(g, 1, b, q)
                            pe.wait_ge(kv_in[n % RING], 16 * UP * (n // RING + 1))
                            for j in range(UP):
                                ins = nc.tensor.matmul(bank[5 + b % 2][0:HT, :],
                                                       PT[:, q * UP + j, b * HT:(b + 1) * HT],
                                                       ring[:, n % RING, j * 512:(j + 1) * 512],
                                                       start=q == 0 and j == 0, stop=False)
                            ins.then_inc(kv_used, 1)
                        nc.tensor.matmul(bank[5 + b % 2][0:HT, :], PT[0:NS, NPAGE, b * HT:(b + 1) * HT],
                                         c.v[0:NS, STILE], start=False, stop=True).then_inc(s["pv_mm"], 1)
                        if b == 0 and g:
                            pe.wait_ge(s["ot"], g)
                        if b:
                            out_T(b - 1)
                    out_T(HB - 1)

            @block.vector
            def _(dve):
                V = nc.vector
                link = Link(dve, d_own)
                dve.wait_ge(s["c_in"], 16 * 9)
                dve.wait_ge(s["swap_in"], 32)
                qi = qiS[:].rearrange("d b (k two) t -> d two k b t", two=2)
                for k in range(4):
                    for half in range(2):
                        for lo in (0, HD):
                            src = (c.qiT[:, :, SEQ:NT] if lo == HD * half else swapped[:])[lo:lo + HD, k]
                            link(V.tensor_copy(qi[lo:lo + HD, half, k], src.rearrange("d (b t) -> d b t", b=NB)),
                                 s["q_ready"] if (k, half, lo) == (3, 1, HD) else None)
                link(V.tensor_tensor(wx[:], c.small[0:NS, STILE, S_WI:S_WI + H].unsqueeze(2).to_broadcast([NS, H, TS]),
                                     tsel[:].unsqueeze(1).to_broadcast([NS, H, TS]), ALU.mult), s["wx"])
                dve.wait_ge(s["wv_mm"], 1)
                link(V.tensor_scalar(wv[:], bank[7][0:HT, 0:NB], H ** -0.5, None, ALU.mult))
                link(V.tensor_tensor(Wsel[:], wmask[:], wv[:].unsqueeze(2).to_broadcast([HT, NB, NS]), ALU.mult),
                     s["w_ready"])
                link(V.memset(RB[:], 0.0))
                for t in range(TS):
                    link(V.tensor_copy(RB[:, t, :, :, t], relb[:].unsqueeze(1).to_broadcast([NBUCKET, HB, H])),
                         s["rb"] if t == TS - 1 else None)
                link(V.memset(Q[:], 0.0))
                for g in range(2):
                    for b in range(HB):
                        own = Q[:, g, b, :, b * HT:(b + 1) * HT].rearrange("p k (h t) -> p k h t", t=TS)
                        at = SEQ + (g * HB + b) * TS
                        for k in range(4):
                            link(V.tensor_tensor(own[:, k],
                                                 c.qT[:, k, at:at + TS].unsqueeze(1).to_broadcast([P, H, TS]),
                                                 hmask[:, k].unsqueeze(2).to_broadcast([P, H, TS]), ALU.mult),
                                 s["qblk"] if g and b == HB - 1 and k == 3 else None)
                for g in range(2):
                    link(V.reduce_sum(Qall[:, g], Q[:, g].rearrange("p b k n -> p k n b"), AX_X), s["qblk"])
                dve.wait_ge(s["sc_ready"], NKC + 1)
                new = sc[:, PAST:NKEY]
                link(V.tensor_tensor(new, new, c.lowS[:], ALU.mult))
                link(V.tensor_tensor(new, new, c.lowSneg[:], ALU.add))
                for _ in range(topk // 8):
                    link(V.max(m8[:], sc[:]))
                    link(V.match_replace(sc[:], m8[:], sc[:], PICKED))
                link(V.tensor_scalar(msk[:], sc[:], -2.9e38, NOT_SELECTED, ALU.is_gt, ALU.mult), s["mask"])
                dve.wait_ge(s["logit"], 2 * (NKC + 1))
                for g in range(2):
                    for q in range(NKC + 1):
                        n = g * (NKC + 1) + q
                        dve.wait_ge(s["mask_mm"], n + 1)
                        w = 512 if q < NKC else NS
                        part = L[:, g, q * 512:q * 512 + w]
                        link(V.tensor_tensor(part, part, bank[1 + n % 2][:, 0:w], ALU.add), s["masked"])
                        link(V.reduce_max(mx[:, g, q:q + 1], part, AX_X))
                    link(V.reduce_max(ngm[:, g:g + 1], mx[:, g], AX_X))
                    link(V.tensor_scalar(ngm[:, g:g + 1], ngm[:, g:g + 1], -1.0, None, ALU.mult), s["max"])
                for g in range(2):
                    dve.wait_ge(s["exp"], 5 * (g + 1))
                    link(V.reduce_sum(dsum[:, g:g + 1], den[:, g], AX_X))
                    link(V.reciprocal(rden[:, g:g + 1], dsum[:, g:g + 1]))
                    link(V.tensor_scalar(L[:, g], L[:, g], rden[:, g:g + 1], None, ALU.mult), s["prob"])
                for g in range(2):
                    for b in range(HB):
                        n0 = g * HB + b
                        dve.wait_ge(s["pv_mm"], n0 + 1)
                        if n0 >= 2:
                            dve.wait_ge(s["ot_mm"], n0 - 1)
                        link(V.tensor_tensor(Om[:, b % 2], bank[5 + b % 2][0:HT, :], omask[:], ALU.mult), s["om"])


def layer_norm(c, link, r, mv, n, gb, out, pre, sqrt_done, count, done):
    V = c.nc.vector
    for q in range(2):
        link(V.bn_stats(mv[0:n, 6 * q:6 * q + 6], r[0:n, q * 512:(q + 1) * 512]))
    link(V.bn_aggr(mv[0:n, 12:14], mv[0:n, 0:12]))
    link(V.tensor_scalar(mv[0:n, 14:15], mv[0:n, 13:14], EPS, None, ALU.add), pre)
    link.eng.wait_ge(sqrt_done, count)
    link(V.reciprocal(mv[0:n, 15:16], mv[0:n, 14:15]))
    link(V.tensor_scalar(r[0:n, :], r[0:n, :], mv[0:n, 12:13], mv[0:n, 15:16], ALU.subtract, ALU.mult))
    link(V.tensor_tensor(r[0:n, :], r[0:n, :], gb[0:n, 0], ALU.mult))
    link(V.tensor_tensor(out[0:n, :], r[0:n, :], gb[0:n, 1], ALU.add), done)


def stage_mix(c):
    nc, A, bank = c.nc, c.A, c.bank
    with ExitStack() as es:
        def sb(name, shape, dt=F32):
            return es.enter_context(nc.sbuf_tensor(name, shape, dt))
        w = sb("w_out", [P, KD, D])
        x = sb("x_rows", [P, NTILE, D])
        r = sb("resid", [P, 2, D])
        mv = sb("mv", [P, 16])
        gb = sb("ln1", [P, 2, D])
        s = {n: c.sem("mix_" + n) for n in ("in", "mm", "res", "pre", "sqrt", "h", "tr_mm", "tr")}
        d_own = c.sem("mix_dve")
        with nc.Block() as block:
            @block.sync
            def _(sp):
                sp.dma_start(w[:], A["w_out"]).then_inc(s["in"], 16)
                sp.dma_start(x[:, 0:STILE], A["x_rows"][0:SEQ].rearrange("(t p) n -> p t n", p=P)).then_inc(s["in"], 16)
                sp.dma_start(x[0:NS, STILE], A["x_rows"][SEQ:NT]).then_inc(s["in"], 16)
                sp.dma_start(gb[:], A["ln1"].to_broadcast([P, 2, D])).then_inc(s["in"], 16)

            @block.tensor
            def _(pe):
                pe.wait_ge(s["in"], 64)

                def trans(t):
                    n = rows(t)
                    pe.wait_ge(s["h"], t + 1)
                    if t:
                        pe.wait_ge(s["tr"], t)
                    for k in range(KD):
                        ins = nc.tensor.transpose(bank[4 + k // 4][:, (k % 4) * n:(k % 4 + 1) * n],
                                                  c.h[0:n, t, k * P:(k + 1) * P], c.ident[0:n, 0:n])
                    ins.then_inc(s["tr_mm"], 1)

                for t in range(NTILE):
                    if t >= 2:
                        pe.wait_ge(s["res"], t - 1)
                    for q in range(2):
                        for k in range(KD):
                            ins = nc.tensor.matmul(bank[2 * (t % 2) + q][0:rows(t), :], c.mixedT[:, k, cols(t)],
                                                   w[:, k, q * 512:(q + 1) * 512], start=k == 0, stop=k == KD - 1)
                    ins.then_inc(s["mm"], 1)
                    if t:
                        trans(t - 1)
                trans(STILE)

            @block.scalar
            def _(act):
                for t in range(NTILE):
                    n = rows(t)
                    act.wait_ge(s["pre"], t + 1)
                    nc.scalar.activation(mv[0:n, 14:15], mv[0:n, 14:15], ACT.Sqrt).then_inc(s["sqrt"], 1)
                    act.wait_ge(s["tr_mm"], t + 1)
                    nc.scalar.activation(c.hT[:, 0:4, cols(t)], bank[4][:, 0:4 * n].rearrange("p (k n) -> p k n", k=4),
                                         ACT.Copy)
                    nc.scalar.activation(c.hT[:, 4:8, cols(t)], bank[5][:, 0:4 * n].rearrange("p (k n) -> p k n", k=4),
                                         ACT.Copy).then_inc(s["tr"], 1)

            @block.vector
            def _(dve):
                V = nc.vector
                link = Link(dve, d_own)
                dve.wait_ge(s["in"], 64)
                for t in range(NTILE):
                    n = rows(t)
                    dve.wait_ge(s["mm"], t + 1)
                    for q in range(2):
                        cs = slice(q * 512, (q + 1) * 512)
                        link(V.scalar_tensor_tensor(r[0:n, t % 2, cs], x[0:n, t, cs], ALPHA,
                                                    bank[2 * (t % 2) + q][0:n, :], ALU.mult, ALU.add),
                             s["res"] if q else None)
                    layer_norm(c, link, r[:, t % 2], mv, n, gb, c.h[:, t], s["pre"], s["sqrt"], t + 1,
                               s["h"])


def stage_memory(c):
    nc, A, bank = c.nc, c.A, c.bank
    mkT, mv_ = c.mkT, c.mv
    with ExitStack() as es:
        def sb(name, shape, dt=F32):
            return es.enter_context(nc.sbuf_tensor(name, shape, dt))
        wcq = sb("w_cq", [P, KD, 512])
        wco = sb("w_co", [P, MH, D])
        mkS, mvS = sb("mkS", [P, 2, MH, MEM]), sb("mvS", [P, 2, 2, 512])
        q = sb("q_mem", [P, MH, NT])
        qm = sb("qm", [P, MH, NB, NS])
        Pm = sb("p_mem", [P, 2, MH, MEM])
        PT = sb("pT_mem", [P, MH, 2, P])
        oT = sb("oT_mem", [P, MH, P])
        mx, den, rden = sb("mx_m", [P, 2, MH]), sb("den_m", [P, 2, MH]), sb("rden_m", [P, MH])
        r = sb("resid2", [P, D])
        st = sb("mv2", [P, 16])
        gb = sb("ln2", [P, 2, D])
        names = ("wco", "q_mm", "q_ev", "qm", "log_mm", "max", "exp", "prob", "trp_mm", "pt",
                 "o_mm", "oT", "co_mm", "res", "pre", "sqrt", "h", "tr_mm", "tr", "ks0", "ks1", "vs0", "vs1", "vs_used",
                 "ks_used", "gb")
        s = {n: c.sem("mem_" + n) for n in names}
        wcq_in = [c.sem(f"wcq_in{h}") for h in range(MH)]
        d_own = c.sem("mem_dve")
        SCALE = MD ** -0.5
        ORDER = [0, STILE] + list(range(1, STILE))

        def logit_bank(t, h):
            if t < STILE:
                return bank[h // 2][:, (h % 2) * MEM:(h % 2 + 1) * MEM]
            return bank[h if h < 2 else h + 4][0:NS, 0:MEM]

        with nc.Block() as block:
            @block.sync
            def _(sp):
                for h in range(MH):
                    sp.dma_start(wcq[:, :, h * P:(h + 1) * P], A["w_cq"][:, :, h * P:(h + 1) * P]).then_inc(wcq_in[h], 16)
                sp.dma_start(wco[:], A["w_co"]).then_inc(s["wco"], 16)
                sp.dma_start(gb[:], A["ln2"].to_broadcast([P, 2, D])).then_inc(s["gb"], 16)
                for b in range(NB):
                    if b >= 2:
                        sp.wait_ge(s["ks_used"], b - 1)
                    sp.dma_start(mkS[:, b % 2], A["cmkT"][b]).then_inc(s[f"ks{b % 2}"], 16)
                for b in range(NB):
                    if b >= 2:
                        sp.wait_ge(s["vs_used"], b - 1)
                    sp.dma_start(mvS[:, b % 2], A["cmv"][b].rearrange("(k p) n -> p k n", p=P)).then_inc(s[f"vs{b % 2}"], 16)

            @block.tensor
            def _(pe):
                for h in range(MH):
                    pe.wait_ge(wcq_in[h], 16)
                    if h >= 2:
                        pe.wait_ge(s["q_ev"], h - 1)
                    for half in range(2):
                        for k in range(KD):
                            ins = nc.tensor.matmul(c.pair(h % 2)[:, half], wcq[:, k, h * P:(h + 1) * P],
                                                   c.hT[:, k, half * HALF:(half + 1) * HALF],
                                                   start=k == 0, stop=k == KD - 1)
                    ins.then_inc(s["q_mm"], 1)
                pe.wait_ge(s["q_ev"], MH)

                def logits(i):
                    t = ORDER[i]
                    if i:
                        pe.wait_ge(s["exp"], MH * i)
                    if t < STILE:
                        for h in range(MH):
                            ins = nc.tensor.matmul(logit_bank(t, h), q[:, h, cols(t)], mkT[:, h],
                                                   start=True, stop=True)
                    else:
                        pe.wait_ge(s["qm"], 1)
                        for b in range(NB):
                            pe.wait_ge(s[f"ks{b % 2}"], 16 * (b // 2 + 1))
                            for h in range(MH):
                                ins = nc.tensor.matmul(logit_bank(t, h), qm[:, h, b], mkS[:, b % 2, h],
                                                       start=b == 0, stop=b == NB - 1)
                            if b < NB - 1:
                                ins.then_inc(s["ks_used"], 1)
                    ins.then_inc(s["log_mm"], 1)

                def transposes(i):
                    t = ORDER[i]
                    n = rows(t)
                    pe.wait_ge(s["h"], i + 1)
                    if i == 0:
                        pe.wait_ge(s["exp"], 2 * MH)
                    for k in range(KD):
                        ins = nc.tensor.transpose(bank[(4, 7)[k // 4]][:, (k % 4) * n:(k % 4 + 1) * n],
                                                  c.h[0:n, t, k * P:(k + 1) * P], c.ident[0:n, 0:n])
                    ins.then_inc(s["tr_mm"], 1)

                logits(0)
                for i, t in enumerate(ORDER):
                    n = rows(t)
                    if i + 1 < NTILE:
                        logits(i + 1)
                    pe.wait_ge(s["prob"], i + 1)
                    if i:
                        pe.wait_ge(s["pt"], 2 * i)
                    for h in range(MH):
                        for m in range(2):
                            ins = nc.tensor.transpose(bank[2 + m][:, h * n:(h + 1) * n],
                                                      Pm[0:n, i % 2, h, m * P:(m + 1) * P], c.ident[0:n, 0:n])
                    ins.then_inc(s["trp_mm"], 1)
                    pe.wait_ge(s["pt"], 2 * (i + 1))
                    if i >= 2:
                        pe.wait_ge(s["tr"], i - 1)
                    if t < STILE:
                        for h in range(MH):
                            for m in range(2):
                                ins = nc.tensor.matmul(bank[4][:, h * P:(h + 1) * P], mv_[:, m, h * P:(h + 1) * P],
                                                       PT[:, h, m, 0:n], start=m == 0, stop=m == 1)
                    else:
                        for b in range(NB):
                            pe.wait_ge(s[f"vs{b % 2}"], 16 * (b // 2 + 1))
                            for h in range(MH):
                                for m in range(2):
                                    ins = nc.tensor.matmul(bank[4][:, h * n + b * TS:h * n + (b + 1) * TS],
                                                           mvS[:, b % 2, m, h * P:(h + 1) * P],
                                                           PT[:, h, m, b * TS:(b + 1) * TS], start=m == 0, stop=m == 1)
                            if b < NB - 1:
                                ins.then_inc(s["vs_used"], 1)
                    ins.then_inc(s["o_mm"], 1)
                    pe.wait_ge(s["oT"], i + 1)
                    if i == 0:
                        pe.wait_ge(s["wco"], 16)
                        pe.wait_ge(s["exp"], 2 * MH)
                    else:
                        pe.wait_ge(s["res"], i)
                    for half in range(2):
                        for h in range(MH):
                            ins = nc.tensor.matmul(bank[5 + half][0:n, :], oT[:, h, 0:n],
                                                   wco[:, h, half * 512:(half + 1) * 512], start=h == 0, stop=h == MH - 1)
                    ins.then_inc(s["co_mm"], 1)
                    if i:
                        transposes(i - 1)
                pe.wait_ge(s["tr"], NTILE - 1)
                transposes(NTILE - 1)

            @block.scalar
            def _(act):
                for h in range(MH):
                    act.wait_ge(s["q_mm"], h + 1)
                    nc.scalar.activation(q[:, h].rearrange("p (c t) -> p c t", c=2), c.pair(h % 2),
                                         ACT.Copy).then_inc(s["q_ev"], 1)

                def exps(i):
                    n = rows(ORDER[i])
                    act.wait_ge(s["max"], i + 1)
                    if i >= 2:
                        act.wait_ge(s["trp_mm"], i - 1)
                    for h in range(MH):
                        nc.scalar.activation(Pm[0:n, i % 2, h], logit_bank(ORDER[i], h), ACT.Exp,
                                             bias=mx[0:n, i % 2, h:h + 1], scale=SCALE,
                                             accum_out=den[0:n, i % 2, h:h + 1]).then_inc(s["exp"], 1)

                def store_hT(i):
                    n = rows(ORDER[i])
                    act.wait_ge(s["tr_mm"], i + 1)
                    for half in range(2):
                        ins = nc.scalar.activation(c.hT[:, 4 * half:4 * half + 4, cols(ORDER[i])],
                                                   bank[(4, 7)[half]][:, 0:4 * n].rearrange("p (k n) -> p k n", k=4),
                                                   ACT.Copy)
                    ins.then_inc(s["tr"], 1)

                exps(0)
                for i, t in enumerate(ORDER):
                    n = rows(t)
                    if i + 1 < NTILE:
                        exps(i + 1)
                    act.wait_ge(s["trp_mm"], i + 1)
                    if i:
                        act.wait_ge(s["o_mm"], i)
                    for m in range(2):
                        nc.scalar.activation(PT[:, :, m, 0:n], bank[2 + m][:, 0:MH * n].rearrange(
                            "p (h n) -> p h n", h=MH), ACT.Copy).then_inc(s["pt"], 1)
                    act.wait_ge(s["o_mm"], i + 1)
                    if i:
                        act.wait_ge(s["co_mm"], i)
                    nc.scalar.activation(oT[:, :, 0:n], bank[4][:, 0:MH * n].rearrange("p (h n) -> p h n", h=MH),
                                         ACT.Copy).then_inc(s["oT"], 1)
                    if i:
                        store_hT(i - 1)
                    act.wait_ge(s["pre"], i + 1)
                    nc.scalar.activation(st[0:n, 14:15], st[0:n, 14:15], ACT.Sqrt).then_inc(s["sqrt"], 1)
                store_hT(NTILE - 1)

            @block.vector
            def _(dve):
                V = nc.vector
                link = Link(dve, d_own)
                dve.wait_ge(s["q_ev"], MH)

                def softmax(i):
                    t = ORDER[i]
                    n, m, Pt = rows(t), mx[:, i % 2], Pm[:, i % 2]
                    dve.wait_ge(s["log_mm"], i + 1)
                    if t < STILE:
                        for half in range(2):
                            link(V.reduce_max(m[:, 2 * half:2 * half + 2],
                                              bank[half][:].rearrange("p (h m) -> p h m", h=2), AX_X))
                    else:
                        for h in range(MH):
                            link(V.reduce_max(m[0:n, h:h + 1], logit_bank(t, h), AX_X))
                    link(V.tensor_scalar(m[0:n, :], m[0:n, :], -SCALE, None, ALU.mult), s["max"])
                    dve.wait_ge(s["exp"], MH * (i + 1))
                    link(V.reciprocal(rden[0:n, :], den[0:n, i % 2]))
                    link(V.tensor_tensor(Pt[0:n], Pt[0:n], rden[0:n, :].unsqueeze(2).to_broadcast([n, MH, MEM]),
                                         ALU.mult), s["prob"])

                softmax(0)
                for h in range(MH):
                    link(V.tensor_tensor(qm[:, h], q[:, h, SEQ:NT].unsqueeze(1).to_broadcast([P, NB, NS]), c.bcol[:],
                                         ALU.mult), s["qm"] if h == MH - 1 else None)
                dve.wait_ge(s["gb"], 16)
                for i, t in enumerate(ORDER):
                    n = rows(t)
                    if i + 1 < NTILE:
                        softmax(i + 1)
                    dve.wait_ge(s["co_mm"], i + 1)
                    for half in range(2):
                        cs = slice(half * 512, (half + 1) * 512)
                        link(V.scalar_tensor_tensor(r[0:n, cs], c.h[0:n, t, cs], ALPHA, bank[5 + half][0:n, :],
                                                    ALU.mult, ALU.add), s["res"] if half else None)
                    layer_norm(c, link, r, st, n, gb, c.h[:, t], s["pre"], s["sqrt"], i + 1, s["h"])


def stage_route(c):
    nc, A, bank = c.nc, c.A, c.bank
    NJ = 2 * PH
    RING = 3
    with ExitStack() as es:
        def sb(name, shape, dt=F32):
            return es.enter_context(nc.sbuf_tensor(name, shape, dt))
        wq = sb("wq", [P, RING, KD, P])
        sk = sb("subkeys", [P, NJ, NKEYS])
        qp = sb("qp", [P, 2, NT])
        S = sb("S", [P, NTILE, NJ * NKEYS])
        work = sb("work", [P, NJ, NKEYS])
        v16 = sb("v16", [P, NJ, TOPK])
        i16 = sb("i16", [P, NJ, TOPK], U32)
        i16f = sb("i16f", [P, NJ, TOPK])
        cand = sb("cand", [P, PH, TOPK * TOPK])
        gs, gi = sb("gs", [P, PH, TOPK]), sb("gi", [P, PH, TOPK], U32)
        ab = sb("ab", [P, 2, PH * TOPK], U32)
        abf = sb("abf", [P, 2, PH * TOPK])
        eq = sb("eq", [P, PH * TOPK, TOPK])
        gm, gsum = sb("gm", [P, PH, TOPK]), sb("gsum", [P, PH])
        res = sb("res", [P, 3, P])
        sk_in, q_mm, q_ev = c.sem("sk_in"), c.sem("rq_mm"), c.sem("rq_ev")
        wq_in = [c.sem(f"wq_in{i}") for i in range(RING)]
        s_mm, s_ev, zero = c.sem("rs_mm"), c.sem("rs_ev"), c.sem("r_zero")
        g_pre, g_exp, res_ready, res_mm, res_ev = (c.sem("r_" + n) for n in
                                                   ("g_pre", "g_exp", "res", "res_mm", "res_ev"))
        d_own = c.sem("route_dve")

        with nc.Block() as block:
            @block.sync
            def _(sp):
                sp.dma_start(sk[:], A["subkeysT"]).then_inc(sk_in, 16)
                for j in range(NJ):
                    if j >= RING:
                        sp.wait_ge(q_mm, j - RING + 1)
                    sp.dma_start(wq[:, j % RING], A["wq_blk"][j]).then_inc(wq_in[j % RING], 16)

            @block.tensor
            def _(pe):
                pe.sem_inc(res_mm, 1)
                pe.wait_ge(sk_in, 16)

                def scores(j):
                    pe.wait_ge(q_ev, j + 1)
                    if j >= 2:
                        pe.wait_ge(s_ev, 2 * (j - 1))
                    for t in range(NTILE):
                        dst = bank[4 + j % 2][:, t * P:(t + 1) * P] if t < STILE else bank[6 + j % 2][0:NS, 0:P]
                        ins = nc.tensor.matmul(dst, qp[:, j % 2, cols(t)], sk[:, j], start=True, stop=True)
                    ins.then_inc(s_mm, 1)

                for j in range(NJ):
                    pe.wait_ge(wq_in[j % RING], 16 * (j // RING + 1))
                    if j >= 2:
                        pe.wait_ge(q_ev, j - 1)
                    for q in range(2):
                        for k in range(KD):
                            ins = nc.tensor.matmul(c.pair(j % 2)[:, q], wq[:, j % RING, k],
                                                   c.hT[:, k, q * HALF:(q + 1) * HALF],
                                                   start=k == 0, stop=k == KD - 1)
                    ins.then_inc(q_mm, 1)
                    if j:
                        scores(j - 1)
                scores(NJ - 1)
                for t in range(NTILE):
                    pe.wait_ge(res_ready, t + 1)
                    if t == 0:
                        pe.wait_ge(q_ev, NJ)
                    else:
                        pe.wait_ge(res_ev, t)
                    for q in range(3):
                        ins = nc.tensor.transpose(bank[0][:, q * P:(q + 1) * P], res[:, q], c.ident[:])
                    ins.then_inc(res_mm, 1)

            @block.scalar
            def _(act):
                def scores(j):
                    act.wait_ge(s_mm, j + 1)
                    if j == 0:
                        act.wait_ge(zero, 1)
                    nc.scalar.activation(S[:, 0:STILE, j * NKEYS:(j + 1) * NKEYS],
                                         bank[4 + j % 2][:].rearrange("p (t n) -> p t n", t=STILE),
                                         ACT.Copy).then_inc(s_ev, 1)
                    nc.scalar.activation(S[0:NS, STILE, j * NKEYS:(j + 1) * NKEYS], bank[6 + j % 2][0:NS, 0:P],
                                         ACT.Copy).then_inc(s_ev, 1)

                for j in range(NJ):
                    act.wait_ge(q_mm, j + 1)
                    if j >= 2:
                        act.wait_ge(s_mm, j - 1)
                    nc.scalar.activation(qp[:, j % 2].rearrange("p (c t) -> p c t", c=2), c.pair(j % 2),
                                         ACT.Copy).then_inc(q_ev, 1)
                    if j:
                        scores(j - 1)
                scores(NJ - 1)
                for t in range(NTILE):
                    act.wait_ge(g_pre, t + 1)
                    nc.scalar.activation(gm[:], gm[:], ACT.Exp).then_inc(g_exp, 1)
                    act.wait_ge(res_mm, t + 2)
                    n = rows(t)
                    nc.scalar.activation(c.slots[:, :, cols(t)],
                                         bank[0][:, 0:3 * P].rearrange("p (q n) -> p q n", q=3)[:, :, 0:n],
                                         ACT.Copy).then_inc(res_ev, 1)

            @block.vector
            def _(dve):
                V = nc.vector
                V.memset(S[:, STILE], 0.0).then_inc(zero, 1)
                dve.wait_ge(s_ev, 2 * NJ)
                with dve.Fori(0, NTILE) as ti:
                    dve.sem_clear(d_own)
                    link = Link(dve, d_own)

                    def top16(val, idx, x):
                        link(V.max(val[:, 0:8], x))
                        link(V.max_index(idx[:, 0:8], val[:, 0:8], x))
                        link(V.match_replace(x, val[:, 0:8], x, PICKED))
                        link(V.max(val[:, 8:16], x))
                        link(V.max_index(idx[:, 8:16], val[:, 8:16], x))

                    link(V.tensor_copy(work[:].rearrange("p j n -> p (j n)").unsqueeze(1), S[:, bass.ds(ti, 1)]))
                    for j in range(NJ):
                        top16(v16[:, j], i16[:, j], work[:, j])
                    v = v16[:].rearrange("p (h two) a -> p two h a", two=2)
                    c4 = cand[:].rearrange("p h (a b) -> p h a b", a=TOPK)
                    link(V.tensor_tensor(c4, v[:, 0].unsqueeze(3).to_broadcast([P, PH, TOPK, TOPK]),
                                         v[:, 1].unsqueeze(2).to_broadcast([P, PH, TOPK, TOPK]), ALU.add))
                    for h in range(PH):
                        top16(gs[:, h], gi[:, h], cand[:, h])
                    flat = gi[:].rearrange("p h a -> p (h a)")
                    link(V.tensor_scalar(ab[:, 0], flat, 4, None, ALU.logical_shift_right))
                    link(V.tensor_scalar(ab[:, 1], flat, TOPK - 1, None, ALU.bitwise_and))
                    link(V.tensor_copy(abf[:], ab[:]))
                    link(V.tensor_copy(i16f[:], i16[:]))
                    V.tensor_tensor(gm[:], gs[:], gs[:, :, 0:1].to_broadcast([P, PH, TOPK]),
                                    ALU.subtract).then_inc(g_pre, 1)
                    if16 = i16f[:].rearrange("p (h two) a -> p two h a", two=2)
                    dve.wait_ge(res_mm, ti + 1)
                    for q in range(2):
                        e3 = eq[:]
                        link(V.tensor_tensor(e3, abf[:, q].unsqueeze(2).to_broadcast([P, PH * TOPK, TOPK]),
                                             c.iota[:, 0:TOPK].unsqueeze(1).to_broadcast([P, PH * TOPK, TOPK]),
                                             ALU.is_equal))
                        e4 = eq[:].rearrange("p (h s) a -> p h s a", h=PH)
                        link(V.tensor_tensor(e4, e4, if16[:, q].unsqueeze(2).to_broadcast([P, PH, TOPK, TOPK]),
                                             ALU.mult))
                        link(V.reduce_sum(res[:, q], e3, AX_X))
                    dve.wait_ge(g_exp, ti + 1)
                    link(V.reduce_sum(gsum[:], gm[:], AX_X))
                    link(V.reciprocal(gsum[:], gsum[:]))
                    V.tensor_tensor(res[:, 2].rearrange("p (h s) -> p h s", h=PH), gm[:],
                                    gsum[:].unsqueeze(2).to_broadcast([P, PH, TOPK]), ALU.mult).then_inc(res_ready, 1)
                    dve.wait_ge(res_ready, ti + 1)


GS = 4
NG = NKEYS // GS
TB = 64
NTB = SEQ // TB
GCOL = GS * NT
U_START = 2


def stage_gates(c):
    nc, A, bank = c.nc, c.A, c.bank
    with ExitStack() as es:
        def sb(name, shape, dt=F32):
            return es.enter_context(nc.sbuf_tensor(name, shape, dt))
        hot_i, hot_j, raw_j = (sb(n, [P, 2, 4, P]) for n in ("hot_i", "hot_j", "raw_j"))
        G = sb("Gtile", [P, 2, NKEYS, TB])
        hi_ready, hj_ready, rj_ready = c.sem("hot_i"), c.sem("hot_j"), c.sem("raw_j")
        g_mm, g_ev = c.sem("g_mm"), c.sem("g_ev")
        stored = [c.sem(f"g_stored{i}") for i in range(2)]
        blocks = [(b * TB, TB // 8) for b in range(NTB)] + [(SEQ, NS // 8)]

        def rounds(eng, body):
            first = 0
            for b, (tok0, count) in enumerate(blocks):
                with eng.Fori(0, count) as r:
                    for u in range(2):
                        body(r * 8 + (tok0 + 4 * u), r * 2 + (2 * first + u), r * 8 + 4 * u, b, u)
                first += count
                yield b, 2 * first

        with nc.Block() as block:
            @block.vector
            def _(dve):
                def body(tok, n, at, b, u):
                    dve.wait_ge(g_mm, n + 1)
                    for q, (hot, ready) in enumerate(((raw_j, rj_ready), (hot_i, hi_ready))):
                        nc.vector.tensor_tensor(hot[:, u], c.iota[:].unsqueeze(1).to_broadcast([P, 4, P]),
                                                c.slots[:, 1 - q, bass.ds(tok, 4)].unsqueeze(2).to_broadcast([P, 4, P]),
                                                ALU.is_equal).then_inc(ready, 1)
                for _ in rounds(dve, body):
                    pass

            @block.gpsimd
            def _(pool):
                def body(tok, n, at, b, u):
                    pool.wait_ge(rj_ready, n + 1)
                    nc.gpsimd.tensor_tensor(hot_j[:, u], raw_j[:, u],
                                            c.slots[:, 2, bass.ds(tok, 4)].unsqueeze(2).to_broadcast([P, 4, P]),
                                            ALU.mult).then_inc(hj_ready, 1)
                for _ in rounds(pool, body):
                    pass

            @block.tensor
            def _(pe):
                pe.sem_inc(g_mm, 2)
                def body(tok, n, at, b, u):
                    pe.wait_ge(hi_ready, n + 1)
                    pe.wait_ge(hj_ready, n + 1)
                    pe.wait_ge(g_ev, n + 1)
                    for q in range(4):
                        ins = nc.tensor.matmul(bank[u][:, q * P:(q + 1) * P], hot_i[:, u, q], hot_j[:, u, q],
                                               start=True, stop=True)
                    ins.then_inc(g_mm, 1)
                for _ in rounds(pe, body):
                    pass

            @block.scalar
            def _(act):
                act.sem_inc(g_ev, 2)
                def body(tok, n, at, b, u):
                    act.wait_ge(g_mm, n + 3)
                    nc.scalar.activation(G[:, b % 2, :, bass.ds(at, 4)].rearrange("p j t -> p t j"),
                                         bank[u][:].rearrange("p (t j) -> p t j", t=4), ACT.Copy).then_inc(g_ev, 1)
                for b, _ in rounds(act, body):
                    if b + 1 < len(blocks) and b >= 1:
                        act.wait_ge(stored[(b + 1) % 2], 16 * ((b - 1) // 2 + 1))

            @block.sync
            def _(sp):
                first = 0
                for b, (tok0, count) in enumerate(blocks):
                    first += count
                    w = TB if b < NTB else NS
                    sp.wait_ge(g_ev, 2 * first + 2)
                    dst = A["gates"][:, :, b * GS * TB:b * GS * TB + GS * w]
                    if b < NTB:
                        sp.dma_start(dst.rearrange("g p n -> p g n"),
                                     G[:, b % 2].rearrange("p (g j) t -> p g (j t)", j=GS)).then_inc(stored[b % 2], 16)
                    else:
                        for j in range(GS):
                            sp.dma_start(dst[:, :, j * NS:(j + 1) * NS].rearrange("g p t -> p g t"),
                                         G[:, b % 2].rearrange("p (g j) t -> p j g t", j=GS)[:, j, :, 0:NS]
                                         ).then_inc(stored[b % 2], 16)
                sp.wait_ge(stored[0], 16 * (NTB // 2 + GS))
                sp.wait_ge(stored[1], 16 * (NTB // 2))


def stage_experts(c):
    nc, A, bank = c.nc, c.A, c.bank
    with ExitStack() as es:
        def sb(name, shape, dt=F32):
            return es.enter_context(nc.sbuf_tensor(name, shape, dt))
        hH, hL = sb("hH", [P, KD, NT], F32R), sb("hL", [P, KD, NT], F32R)
        u, uH, uL = sb("u_raw", [P, 2, KD, P]), sb("uH", [P, 2, KD, P], F32R), sb("uL", [P, 2, KD, P], F32R)
        v, vH, vL = sb("v_raw", [P, 2, D]), sb("vH", [P, GS, D], F32R), sb("vL", [P, GS, D], F32R)
        G = sb("G", [P, 2, GCOL])
        a, wf = sb("acts", [P, 2, NT]), sb("wf", [P, NT])
        wH, wL = sb("wH", [P, GS, NT], F32R), sb("wL", [P, GS, NT], F32R)
        y = c.hT
        h_split, d_own = c.sem("h_split"), c.sem("exp_dve")
        u_in = [c.sem(f"u_in{i}") for i in range(2)]
        v_in = [c.sem(f"v_in{i}") for i in range(2)]
        G_in = [c.sem(f"G_in{i}") for i in range(2)]
        u_split, u_mm, u_act, w_done, v_split, y_added = (c.sem(n) for n in (
            "u_split", "u_mm", "u_act", "w_done", "v_split", "y_added"))
        u_hi, v_hi, v_mm = c.sem("u_hi"), c.sem("v_hi"), c.sem("v_mm")
        R = U_START

        def loop(eng, body):
            with eng.Fori(0, NG // 2 - 1) as r:
                for p in range(2):
                    body(r * 2 + p, p, False)
            for p in range(2):
                body(NG - 2 + p, p, True)

        with nc.Block() as block:
            @block.sync
            def _(sp):
                def body(g, p, last):
                    for j in range(GS):
                        n = g * GS + j
                        sp.wait_ge(u_split, n + 1)
                        src = A["uT"][bass.ds(n, 1)] if not isinstance(n, int) else A["uT"][n:n + 1]
                        sp.dma_start(u[:, j % 2], src.rearrange("a p k n -> p (a k) n")).then_inc(u_in[j % 2], 16)
                loop(sp, body)

            @block.gpsimd
            def _(pool):
                for g in range(2):
                    pool.dma_start(G[:, g], A["gates"][g]).then_inc(G_in[g], 16)

                def body(g, p, last):
                    for j in range(GS):
                        n = g * GS + j
                        pool.wait_ge(v_split, n + 1)
                        src = A["v_rows"][bass.ds(n, 1)] if not isinstance(n, int) else A["v_rows"][n:n + 1]
                        pool.dma_start(v[:, j % 2], src.rearrange("a p n -> p (a n)")).then_inc(v_in[j % 2], 16)
                    if not last:
                        pool.wait_ge(w_done, (g + 1) * GS + R)
                        pool.dma_start(G[:, p], A["gates"][bass.ds(g + 2, 1)].rearrange("a p n -> p (a n)")
                                       ).then_inc(G_in[p], 16)
                loop(pool, body)

            @block.scalar
            def _(act):
                act.sem_inc(u_act, R)

                def high_u(n, j):
                    act.wait_ge(u_in[j % 2], (n - j % 2) * 8 + 16)
                    act.wait_ge(u_mm, n + 1)
                    nc.scalar.activation(uH[:, j % 2], u[:, j % 2], ACT.Copy).then_inc(u_hi, 1)

                high_u(0, 0)

                def body(g, p, last):
                    for j in range(GS):
                        n = g * GS + j
                        if not (last and p == 1 and j == GS - 1):
                            high_u(n + 1, (j + 1) % 2)
                        act.wait_ge(v_in[j % 2], (n - j % 2) * 8 + 16)
                        act.wait_ge(v_mm, g * KD + 1)
                        nc.scalar.activation(vH[:, j], v[:, j % 2], ACT.Copy).then_inc(v_hi, 1)
                        act.wait_ge(u_mm, n + 1 + R)
                        act.wait_ge(w_done, n + 1)
                        nc.scalar.activation(a[:, j % 2].rearrange("p (c t) -> p c t", c=2), c.pair(j % 2),
                                             ACT.Gelu_apprx_tanh).then_inc(u_act, 1)
                loop(act, body)

            @block.vector
            def _(dve):
                V = nc.vector
                for sem in (u_split, v_split, w_done, y_added):
                    dve.sem_inc(sem, R)
                for k in range(KD):
                    V.tensor_copy(hH[:, k], c.hT[:, k]).then_inc(h_split, 1)
                    dve.wait_ge(h_split, 2 * k + 1)
                    V.tensor_tensor(hL[:, k], c.hT[:, k], hH[:, k].bitcast(F32), ALU.subtract).then_inc(h_split, 1)
                dve.wait_ge(h_split, 2 * KD)
                V.memset(y[:], 0.0).then_inc(d_own, 1)
                dve.wait_ge(d_own, 1)
                PER = 3 * GS

                def low_u(n, j):
                    dve.wait_ge(u_hi, n + 1)
                    V.tensor_tensor(uL[:, j % 2], u[:, j % 2], uH[:, j % 2].bitcast(F32),
                                    ALU.subtract).then_inc(u_split, 1)

                low_u(0, 0)

                def body(g, p, last):
                    def own(ins, k):
                        ins.then_inc(d_own, 1)
                        dve.wait_ge(d_own, g * PER + k + 1)
                    for j in range(GS):
                        n = g * GS + j
                        if not (last and p == 1 and j == GS - 1):
                            low_u(n + 1, (j + 1) % 2)
                        dve.wait_ge(v_hi, n + 1)
                        V.tensor_tensor(vL[:, j], v[:, j % 2], vH[:, j].bitcast(F32),
                                        ALU.subtract).then_inc(v_split, 1)
                        if j == 0:
                            dve.wait_ge(G_in[p], (g - p) * 8 + 16)
                        dve.wait_ge(u_act, n + 1 + R)
                        gp = G[:, p, 0:GS * SEQ].rearrange("p (b j t) -> p b j t", b=NTB, j=GS)[:, :, j]
                        own(V.tensor_tensor(wf[:, 0:SEQ].rearrange("p (b t) -> p b t", b=NTB),
                                            a[:, j % 2, 0:SEQ].rearrange("p (b t) -> p b t", b=NTB), gp, ALU.mult),
                            3 * j + 1)
                        own(V.tensor_tensor(wf[:, SEQ:NT], a[:, j % 2, SEQ:NT],
                                            G[:, p, GS * SEQ + j * NS:GS * SEQ + (j + 1) * NS], ALU.mult), 3 * j + 2)
                        own(V.tensor_copy(wH[:, j], wf[:]), 3 * j + 3)
                        V.tensor_tensor(wL[:, j], wf[:], wH[:, j].bitcast(F32), ALU.subtract).then_inc(w_done, 1)
                        dve.wait_ge(w_done, n + 1 + R)
                    for k in range(KD):
                        dve.wait_ge(v_mm, g * KD + k + 2)
                        yk = y[:, k].rearrange("p (c t) -> p c t", c=2)
                        V.tensor_tensor(yk, yk, c.pair(2 + k % 2), ALU.add).then_inc(y_added, 1)
                    dve.wait_ge(y_added, (g + 1) * KD + R)
                loop(dve, body)

            @block.tensor
            def _(pe):
                pe.sem_inc(u_mm, R)
                pe.sem_inc(v_mm, 1)
                pe.wait_ge(h_split, 2 * KD)

                def body(g, p, last):
                    for j in range(GS):
                        n = g * GS + j
                        pe.wait_ge(u_split, n + 1 + R)
                        pe.wait_ge(u_act, n + 1)
                        for q in range(2):
                            dst, cs = c.pair(j % 2)[:, q], slice(q * HALF, (q + 1) * HALF)
                            parts = [(w, x, k) for k in range(KD) for w, x in ((uH, hH), (uH, hL), (uL, hH))]
                            for m, (w, x, k) in enumerate(parts):
                                ins = nc.tensor.matmul(dst, w[:, j % 2, k], x[:, k, cs], start=m == 0,
                                                       stop=m == len(parts) - 1)
                        ins.then_inc(u_mm, 1)
                    for k in range(KD):
                        pe.wait_ge(y_added, g * KD + k + 1)
                        for q in range(2):
                            dst, cs = c.pair(2 + k % 2)[:, q], slice(q * HALF, (q + 1) * HALF)
                            parts = [(w, x, j) for j in range(GS) for w, x in ((vH, wH), (vH, wL), (vL, wH))]
                            for m, (w, x, j) in enumerate(parts):
                                if k == 0 and q == 0 and m % 3 == 0:
                                    pe.wait_ge(v_split, g * GS + j + 1 + R)
                                    pe.wait_ge(w_done, g * GS + j + 1 + R)
                                ins = nc.tensor.matmul(dst, w[:, j, k * P:(k + 1) * P], x[:, j, cs], start=m == 0,
                                                       stop=m == len(parts) - 1)
                        ins.then_inc(v_mm, 1)
                loop(pe, body)


def stage_finish(c):
    nc, A, bank = c.nc, c.A, c.bank
    with ExitStack() as es:
        def sb(name, shape, dt=F32):
            return es.enter_context(nc.sbuf_tensor(name, shape, dt))
        r = sb("resid3", [P, D])
        out = sb("yout", [P, NTILE, D])
        st = sb("mv3", [P, 16])
        gb = sb("ln3", [P, 2, D])
        s = {n: c.sem("fin_" + n) for n in ("gb", "mm", "res", "pre", "sqrt", "out", "store")}
        d_own = c.sem("fin_dve")
        with nc.Block() as block:
            @block.tensor
            def _(pe):
                for t in range(NTILE):
                    n = rows(t)
                    if t >= 2:
                        pe.wait_ge(s["res"], t - 1)
                    for k in range(KD):
                        ins = nc.tensor.transpose(bank[2 * (t % 2) + k // 4][0:n, (k % 4) * P:(k % 4 + 1) * P],
                                                  c.hT[:, k, cols(t)], c.ident[:])
                    ins.then_inc(s["mm"], 1)

            @block.scalar
            def _(act):
                for t in range(NTILE):
                    n = rows(t)
                    act.wait_ge(s["pre"], t + 1)
                    nc.scalar.activation(st[0:n, 14:15], st[0:n, 14:15], ACT.Sqrt).then_inc(s["sqrt"], 1)

            @block.vector
            def _(dve):
                link = Link(dve, d_own)
                dve.wait_ge(s["gb"], 16)
                for t in range(NTILE):
                    n = rows(t)
                    dve.wait_ge(s["mm"], t + 1)
                    for q in range(2):
                        cs = slice(q * 512, (q + 1) * 512)
                        link(nc.vector.scalar_tensor_tensor(r[0:n, cs], c.h[0:n, t, cs], ALPHA,
                                                            bank[2 * (t % 2) + q][0:n, :], ALU.mult, ALU.add),
                             s["res"] if q else None)
                    layer_norm(c, link, r, st, n, gb, out[:, t], s["pre"], s["sqrt"], t + 1, s["out"])

            @block.sync
            def _(sp):
                sp.dma_start(gb[:], A["ln3"].to_broadcast([P, 2, D])).then_inc(s["gb"], 16)
                for t in range(NTILE):
                    sp.wait_ge(s["out"], t + 1)
                    dst = A["y_p"][t * P:(t + 1) * P] if t < STILE else A["y_s"]
                    sp.dma_start(dst, out[0:rows(t), t]).then_inc(s["store"], 16)
                sp.wait_ge(s["store"], 16 * NTILE)


def stage_constants(c):
    nc, A = c.nc, c.A
    names = list(c.const)
    const_in = c.sem("const_in")
    with nc.Block() as block:
        @block.sync
        def _(sp):
            for name in names:
                sp.dma_start(c.const[name][:], A["k_" + name]).then_inc(const_in, 16)
            sp.dma_start(c.vecs[:], A["vecs"].to_broadcast([P, NVEC])).then_inc(const_in, 16)
            sp.wait_ge(const_in, 16 * (len(names) + 1))


def build(nc, A, upto=99, dump=None):
    c = Ctx(nc, A)
    with c.stack, ExitStack() as right:
        c.ident = c.keep(c.stack, "ident", [P, P])
        c.iota = c.keep(c.stack, "iota", [P, P])
        c.tri = c.keep(c.stack, "tri", [P, P])
        c.low = c.keep(c.stack, "low", [P, P])
        c.lowneg = c.keep(c.stack, "lowneg", [P, P])
        c.ones = c.keep(c.stack, "ones", [P, P])
        c.triS = c.keep(c.stack, "triS", [NS, NS])
        c.lowS = c.keep(c.stack, "lowS", [NS, NS])
        c.lowSneg = c.keep(c.stack, "lowSneg", [NS, NS])
        c.onesS = c.keep(c.stack, "onesS", [NS, NS])
        c.bsel = c.keep(c.stack, "bsel", [NS, NB])
        c.bcol = c.keep(c.stack, "bcol", [P, NB, NS])
        c.vecs = c.keep(c.stack, "vecs", [P, NVEC])
        c.const = {"ident": c.ident, "iota": c.iota, "tri": c.tri, "low": c.low, "lowneg": c.lowneg, "ones": c.ones, "triS": c.triS, "lowS": c.lowS, "lowSneg": c.lowSneg, "onesS": c.onesS, "bsel": c.bsel, "bcol": c.bcol}
        stage_constants(c)
        memory = ExitStack()
        c.stack.enter_context(memory)
        c.mkT, c.mv = c.keep(memory, "mkT", [P, MH, MEM]), c.keep(memory, "mv_rows", [P, 2, 512])
        with ExitStack() as mid:
            c.mixedT = c.keep(mid, "mixedT", [P, KD, NT])
            with ExitStack() as att:
                c.qT = c.keep(att, "qT", [P, 4, NT])
                c.kT = c.keep(att, "kT", [P, 4, NT])
                c.qiT = c.keep(att, "qiT", [P, 4, NT])
                c.kiT = c.keep(att, "kiT", [P, NT])
                c.v = c.keep(att, "v", [P, NTILE, 512])
                c.small = c.keep(att, "small", [P, NTILE, NSMALL])
                with ExitStack() as ssd:
                    c.convin_p = c.keep(ssd, "convin_p", [P, KD, SEQ + 3])
                    c.convin_s = c.keep(ssd, "convin_s", [P, KD, NB, TS + 3])
                    c.z = c.keep(ssd, "z", [P, NTILE, 512])
                    stage_project(c)
                    if upto >= 2:
                        stage_ssd(c)
                c.pt_in, c.ki_in = c.sem("page_table_in"), c.sem("ki_in")
                c.ptab = att.enter_context(nc.sbuf_tensor("ptab", [1, NB * NPAGE], I32))
                c.kvring = c.keep(att, "kvring", [P, KV_RING, 4 * 512])
                if upto >= 3:
                    stage_dsa_prompt(c)
                if upto >= 4:
                    stage_dsa_sample(c)
            if dump and upto <= 4:
                return dump(c)
            c.reset_semaphores()
            c.h = c.keep(right, "h", [P, NTILE, D], "right")
            c.hT = c.keep(right, "hT", [P, KD, NT], "right")
            stage_mix(c)
        if dump and upto <= 5:
            return dump(c)
        stage_memory(c)
        memory.close()
        if dump and upto <= 6:
            return dump(c)
        with ExitStack() as routed:
            c.slots = c.keep(routed, "slots", [P, 3, NT], "right")
            stage_route(c)
            if dump and upto <= 7:
                return dump(c)
            stage_gates(c)
        stage_experts(c)
        stage_finish(c)


def shape_constants():
    f = np.float32
    i, j = np.arange(P)[:, None], np.arange(P)[None, :]
    r, q = np.arange(NS)[:, None], np.arange(NS)[None, :]
    same = r // TS == q // TS
    k = {
        "k_ident": np.eye(P, dtype=f),
        "k_iota": np.broadcast_to(np.arange(P, dtype=f), (P, P)),
        "k_tri": (i <= j).astype(f),
        "k_low": (j <= i).astype(f),
        "k_lowneg": np.where(j <= i, 0.0, NOT_CAUSAL).astype(f),
        "k_ones": np.ones((P, P), f),
        "k_triS": (same & (r <= q)).astype(f),
        "k_lowS": (same & (q <= r)).astype(f),
        "k_lowSneg": np.where(same & (q <= r), 0.0, NOT_CAUSAL).astype(f),
        "k_onesS": same.astype(f),
        "k_bsel": (np.arange(NS)[:, None] // TS == np.arange(NB)[None, :]).astype(f),
        "k_bcol": np.broadcast_to((np.arange(NS)[None, :] // TS == np.arange(NB)[:, None]).astype(f), (P, NB, NS)),
    }

    def bucket(dist):
        n = np.maximum(dist, 0)
        nf = np.maximum(n, 1).astype(f)
        large = 16 + (np.log(nf / f(16)) / f(np.log(128 / 16)) * f(16)).astype(np.int32)
        return np.where(n < 16, n, np.minimum(large, NBUCKET - 1))

    def onehot(dist):
        return (np.arange(NBUCKET).reshape((-1,) + (1,) * np.ndim(dist)) == bucket(dist)[None]).astype(f)

    k["bucket_rev"] = onehot(2 * P - 1 - np.arange(3 * P))
    k["bucket_past"] = onehot(PAST + TS - 1 - np.arange(PAST + TS))
    k["bucket_new"] = onehot(np.arange(TS)[:, None] - (np.arange(NS) % TS)[None, :])
    half = NB // 2
    b4, h, t = (x.ravel() for x in np.meshgrid(np.arange(half), np.arange(H), np.arange(TS), indexing="ij"))
    k["expand_rows"] = np.stack([(np.arange(NS)[:, None] == ((g * half + b4) * TS + t)[None, :]) for g in range(2)],
                                1).astype(f)
    hh, tt = (x.ravel() for x in np.meshgrid(np.arange(H), np.arange(TS), indexing="ij"))
    k["head_mask"] = (HD ** -0.5 * (np.arange(H)[None, None, :] == 2 * np.arange(4)[None, :, None]
                                    + (np.arange(P) // HD)[:, None, None])).astype(f)
    k["out_mask"] = (hh[:, None] == (np.arange(512) // HD)[None, :]).astype(f)
    k["t_sum"] = (tt[:, None] == np.arange(TS)[None, :]).astype(f)
    k["t_sel"] = (np.arange(NS)[:, None] % TS == np.arange(TS)[None, :]).astype(f)
    k["w_mask"] = (np.arange(NB)[None, :, None] * TS + tt[:, None, None] == np.arange(NS)[None, None, :]).astype(f)
    return {n: np.ascontiguousarray(a) for n, a in k.items()}


def layouts(x):
    c = np.ascontiguousarray

    def chunks(w):
        return c(w.reshape(-1, P, w.shape[1]).transpose(1, 0, 2))

    w_in = x["w_in"]
    cut = lambda at, n: w_in[:, at:at + n]
    wt = np.concatenate([cut(OFF_XBC, CONV), cut(OFF_Q, 512), cut(OFF_K, 512), cut(OFF_QI, 512), cut(OFF_KI, HD),
                         cut(OFF_KI, HD)], 1)
    xr = np.concatenate([x["x_prompt"].reshape(SEQ, D), x["x_sample"].reshape(NS, D)], 0)
    vec = {n: x[n].reshape(-1) for n in VEC if n != "bias_far"}
    vec["bias_far"] = x["rel_bias"][NBUCKET - 1]
    out = {
        "xT": chunks(c(xr.T)),
        "x_rows": xr,
        "w_blk": c(chunks(wt).reshape(P, KD, NBLK, P).transpose(2, 0, 1, 3)),
        "w_row": np.stack([chunks(cut(OFF_Z, 512)), chunks(cut(OFF_V, 512))]),
        "w_small": chunks(np.concatenate([cut(OFF_DT, H), cut(OFF_KI, HD), cut(OFF_WI, H)], 1)),
        "vecs": np.concatenate([vec[n] for n in VEC])[None],
        "state_convT": x["state_conv"].reshape(NB, 3, KD, P).transpose(3, 2, 0, 1),
        "conv_w": x["conv_w"].reshape(4, KD, P).transpose(2, 1, 0),
        "conv_b": x["conv_b"].reshape(KD, P).T,
        "state_ssmT": x["state_ssm"].reshape(NB, 512, P).transpose(2, 0, 1),
        "state_ssm": x["state_ssm"].reshape(NB, 4, P, P).transpose(2, 0, 1, 3),
        "rel_bias": x["rel_bias"],
        "ln1": np.stack([x["ln1_g"], x["ln1_b"]])[None],
        "ln2": np.stack([x["ln2_g"], x["ln2_b"]])[None],
        "ln3": np.stack([x["ln3_g"], x["ln3_b"]])[None],
        "page_table": x["page_table"].reshape(1, -1),
        "kidxT": x["cache_kidx"].transpose(0, 2, 1),
        "kT_pages": x["cache_k"].reshape(-1, PAGE, 4, P).transpose(0, 3, 2, 1).reshape(-1, P, 4 * PAGE),
        "v_pages": x["cache_v"].reshape(-1, PAGE, 512),
        "w_out": chunks(x["w_out"]),
        "memT": chunks(c(x["mem_prompt"][0].T)),
        "w_ck": chunks(x["w_ck"]), "w_cv": chunks(x["w_cv"]), "w_cq": chunks(x["w_cq"]), "w_co": chunks(x["w_co"]),
        "cmkT": x["cache_mem_k"].transpose(0, 3, 2, 1),
        "cmv": x["cache_mem_v"].reshape(NB, MEM, 512),
        "wq_blk": chunks(x["peer_wq"]).reshape(P, KD, 2 * PH, P).transpose(2, 0, 1, 3),
        "subkeysT": x["peer_subkeys"].reshape(2 * PH, NKEYS, P).transpose(2, 0, 1),
        "uT": x["peer_u"].reshape(NKEYS, NKEYS, KD, P).transpose(1, 3, 2, 0),
        "v_rows": x["peer_v"].reshape(NKEYS, NKEYS, D).transpose(1, 0, 2),
    }
    out.update(shape_constants())
    return {n: c(a) for n, a in out.items()}


OUTPUTS = {
    "y_p": (SEQ, D), "y_s": (NS, D), "k_p": (SEQ, 512), "v_p": (SEQ, 512), "kidx_p": (SEQ, HD),
    "memk_p": (MEM, 512), "memv_p": (MEM, 512), "ssm_p": (512, P), "conv_p": (1, 3, CONV),
    "k_s": (NS, 512), "v_s": (NS, 512), "kidx_s": (NS, HD), "ssm_s": (NB, 512, P), "conv_s": (NB, 3, CONV),
}
SHAPES = {
    "y_p": (1, SEQ, D), "y_s": (NB, TS, D), "k_p": (1, SEQ, H, HD), "v_p": (1, SEQ, H, HD), "kidx_p": (1, SEQ, HD),
    "memk_p": (1, MEM, MH, MD), "memv_p": (1, MEM, MH, MD), "ssm_p": (1, H, HD, P), "conv_p": (1, 3, CONV),
    "k_s": (NB, TS, H, HD), "v_s": (NB, TS, H, HD), "kidx_s": (NB, TS, HD), "ssm_s": (NB, H, HD, P),
    "conv_s": (NB, 3, CONV),
}


def kernel(**inputs):
    import concourse.bacc as bacc
    from concourse.bass_utils import run_bass_kernel_spmd

    nc = bacc.Bacc("TRN2", target_bir_lowering=False, num_devices=1)
    arrays, A = {}, {}
    for name, a in layouts({k: np.asarray(v) for k, v in inputs.items()}).items():
        arrays[f"in_{name}"] = a
        A[name] = nc.dram_tensor(f"in_{name}", a.shape, mybir.dt.from_np(a.dtype), kind="ExternalInput").ap()
    for name, shape in OUTPUTS.items():
        A[name] = nc.dram_tensor(f"out_{name}", shape, F32, kind="ExternalOutput").ap()
    A["gates"] = nc.dram_tensor("gate_table", [NG, P, GCOL], F32, kind="Internal").ap()
    build(nc, A)
    r = run_bass_kernel_spmd(nc, [arrays], core_ids=[0])
    return tuple(r.results[0][f"out_{name}"].reshape(SHAPES[name]) for name in OUTPUTS)
```

```python
from contextlib import ExitStack

import numpy as np
import concourse.bass as bass
from concourse import mybir

F32 = mybir.dt.float32
F32R = mybir.dt.float32r
I32 = mybir.dt.int32
U32 = mybir.dt.uint32
ALU = mybir.AluOpType
ACT = mybir.ActivationFunctionType
AX_X = mybir.AxisListType.X

P = 128
D = 1024
KD = D // P
SEQ, NB, TS = 512, 8, 4
NS = NB * TS
NT = SEQ + NS
HALF = NT // 2
NTILE = SEQ // P + 1
STILE = NTILE - 1
H, HD = 8, 64
CONV = 1024
NPAGE, PAGE = 16, 128
PAST = NPAGE * PAGE
NKEY = PAST + NS
NBUCKET = 32
KV_RING = 2 + NB // 2
MH, MD, MEM = 4, 128, 256
PH, NKEYS, TOPK = 8, 128, 16
ALPHA = 2.0 ** 0.25
EPS = 1e-5
NOT_SELECTED = -1e30
NOT_CAUSAL = -2e38
PICKED = -3e38

OFF_Z, OFF_XBC, OFF_DT, OFF_Q, OFF_K, OFF_V, OFF_QI, OFF_KI, OFF_WI = (
    0, 512, 1536, 1544, 2056, 2568, 3080, 3592, 3656)
B_XBC, B_Q, B_K, B_QI, B_KI, NBLK = 0, 8, 12, 16, 20, 21
S_DT, S_KI, S_WI, NSMALL = 0, 8, 72, 80
VEC = {}
_at = 0
for _name, _n in (("ssd_norm_w", 512), ("dt_bias", H), ("a_log", H), ("d_skip", H), ("bias_far", H)):
    VEC[_name] = (_at, _n)
    _at += _n
NVEC = _at


def rows(t):
    return P if t < STILE else NS


def cols(t):
    return slice(t * P, t * P + rows(t))


class Link:

    def __init__(self, eng, own):
        self.eng, self.own, self.count = eng, own, {}

    def count_up(self, ins, sem):
        self.count[id(sem)] = self.count.get(id(sem), 0) + 1
        ins.then_inc(sem, 1)

    def __call__(self, ins, sem=None):
        sem = self.own if sem is None else sem
        self.count_up(ins, sem)
        self.eng.wait_ge(sem, self.count[id(sem)])


class Ctx:

    def __init__(self, nc, A):
        self.nc, self.A = nc, A
        self.stack, self.sems = ExitStack(), []
        self.psum = self.stack.enter_context(nc.psum_tensor("psum", [P, 8, 512], F32))
        self.bank = [self.psum[:, i] for i in range(8)]

    def kiS(self, b):
        return self.kvring[HD * (b % 2):HD * (b % 2) + HD, 2 + b // 2]

    def pair(self, i):
        return self.psum[:, 2 * i:2 * i + 2, 0:HALF]

    def keep(self, stack, name, shape, side="left"):
        return stack.enter_context(self.nc.sbuf_tensor(name, shape, F32, side=side))

    def sem(self, name, software_dma=False):
        s = self.nc.alloc_semaphore(name)
        if not software_dma:
            self.sems.append(s)
        return s

    def reset_semaphores(self):
        spans = []
        for num in sorted(s.num for s in self.sems):
            if spans and spans[-1][1] == num:
                spans[-1][1] = num + 1
            else:
                spans.append([num, num + 1])
        with self.nc.Block() as block:
            @block.gpsimd
            def _(pool):
                for lo, hi in spans:
                    pool.sem_clear(range(lo, hi))
        for s in self.sems:
            self.nc.release_semaphore(s)
        self.sems = []


def stage_project(c):
    nc, A, bank = c.nc, c.A, c.bank
    RING = 4
    with ExitStack() as es:
        def sb(name, shape, dt=F32):
            return es.enter_context(nc.sbuf_tensor(name, shape, dt))
        xT = sb("xT", [P, KD, NT])
        wblk = sb("wblk", [P, RING, KD, P])
        wrow = sb("wrow", [P, 2, KD, 512])
        wsmall = sb("wsmall", [P, KD, NSMALL])
        krow = sb("krow", [P, 2, NTILE, P])
        crow = sb("crow", [NS + 3, CONV])
        x_in = [c.sem(f"x_in{k}") for k in range(KD)]
        small_in, state_in = c.sem("wsmall_in"), c.sem("state_conv_in")
        blk_in = [c.sem(f"wblk_in{i}") for i in range(RING)]
        row_in = [c.sem(f"wrow_in{i}") for i in range(2)]
        blk_mm, blk_act, blk_dve = c.sem("blk_mm"), c.sem("blk_act"), c.sem("blk_dve")
        k_mm, k_ev = c.sem("krow_mm"), c.sem("krow_ev")
        row_mm, row_ev = c.sem("row_mm"), c.sem("row_ev")
        pad_done, store = c.sem("pad_done"), c.sem("proj_store", True)
        kst = [c.sem(f"krow_store{i}", True) for i in range(2)]
        NROW = 3 * NTILE

        with nc.Block() as block:
            @block.sync
            def _(sp):
                sp.dma_start(wblk[:, 0], A["w_blk"][0]).then_inc(blk_in[0], 16)
                for k in range(KD):
                    sp.dma_start(xT[:, k], A["xT"][:, k]).then_inc(x_in[k], 16)
                for j in range(1, NBLK):
                    if j >= RING:
                        sp.wait_ge(blk_mm, j - RING + 1)
                    sp.dma_start(wblk[:, j % RING], A["w_blk"][j]).then_inc(blk_in[j % RING], 16)
                    if j == 2:
                        sp.dma_start(c.convin_s[:, :, :, 0:3], A["state_convT"]).then_inc(state_in, 16)
                for i in range(2):
                    sp.dma_start(wrow[:, i], A["w_row"][i]).then_inc(row_in[i], 16)
                sp.dma_start(wsmall[:], A["w_small"]).then_inc(small_in, 16)
                sp.wait_ge(state_in, 16)

            @block.tensor
            def _(pe):
                for j in range(NBLK):
                    pe.wait_ge(blk_in[j % RING], 16 * (j // RING + 1))
                    if j >= 2:
                        pe.wait_ge(blk_act, j - 1)
                        pe.wait_ge(blk_dve, min(j - 1, B_Q))
                    for q in range(2):
                        for k in range(KD):
                            if j == 0 and q == 0:
                                pe.wait_ge(x_in[k], 16)
                            last = nc.tensor.matmul(c.pair(j % 2)[:, q], wblk[:, j % RING, k],
                                                    xT[:, k, q * HALF:(q + 1) * HALF],
                                                    start=k == 0, stop=k == KD - 1)
                    if j < B_Q:
                        for k in range(KD):
                            last = nc.tensor.matmul(bank[4 + j % 2][0:NS + 3, 0:P], xT[:, k, SEQ - 3:NT],
                                                    wblk[:, j % RING, k], start=k == 0, stop=k == KD - 1)
                    last.then_inc(blk_mm, 1)
                    if B_K < j <= B_QI:
                        pe.wait_ge(blk_act, j)
                        if j >= B_K + 3:
                            pe.wait_ge(k_ev, j - B_K - 2)
                        for t in range(NTILE):
                            dst = bank[4 + j % 2][:, t * P:(t + 1) * P] if t < STILE else bank[6 + j % 2][0:NS, 0:P]
                            last = nc.tensor.transpose(dst, c.kT[:, j - 1 - B_K, cols(t)], c.ident[:])
                        last.then_inc(k_mm, 1)
                n = 0
                for i in range(3):
                    if i < 2:
                        pe.wait_ge(row_in[i], 16)
                    else:
                        pe.wait_ge(small_in, 16)
                    for t in range(NTILE):
                        if n < 2:
                            pe.wait_ge(blk_act, NBLK)
                        if n >= 4:
                            pe.wait_ge(row_ev, n - 3)
                        w = wrow[:, i] if i < 2 else wsmall
                        width = 512 if i < 2 else NSMALL
                        for k in range(KD):
                            last = nc.tensor.matmul(bank[n % 4][0:rows(t), 0:width], xT[:, k, cols(t)],
                                                    w[:, k, 0:width], start=k == 0, stop=k == KD - 1)
                        last.then_inc(row_mm, 1)
                        n += 1

            @block.scalar
            def _(act):
                for j in range(NBLK):
                    act.wait_ge(blk_mm, j + 1)
                    if j < B_Q:
                        if j == 0:
                            act.wait_ge(state_in, 16)
                        nc.scalar.activation(c.convin_s[:, j, :, 3:3 + TS], c.pair(j % 2)[:, 1, SEQ - HALF:HALF]
                                             .rearrange("p (b t) -> p b t", b=NB), ACT.Copy)
                        nc.scalar.activation(c.convin_p[:, j, 3:3 + HALF], c.pair(j % 2)[:, 0], ACT.Copy)
                        nc.scalar.activation(c.convin_p[:, j, 3 + HALF:3 + SEQ], c.pair(j % 2)[:, 1, 0:SEQ - HALF],
                                             ACT.Copy).then_inc(blk_act, 1)
                        continue
                    if j < B_K:
                        dst = c.qT[:, j - B_Q]
                    elif j < B_QI:
                        dst = c.kT[:, j - B_K]
                    elif j < B_KI:
                        dst = c.qiT[:, j - B_QI]
                    else:
                        dst = c.kiT[:]
                    nc.scalar.activation(dst.rearrange("p (c t) -> p c t", c=2), c.pair(j % 2),
                                         ACT.Copy).then_inc(blk_act, 1)
                n = 0
                for i in range(3):
                    for t in range(NTILE):
                        act.wait_ge(row_mm, n + 1)
                        dst = (c.z, c.v, c.small)[i]
                        nc.scalar.activation(dst[0:rows(t), t], bank[n % 4][0:rows(t), 0:dst.shape[2]],
                                             ACT.Copy).then_inc(row_ev, 1)
                        n += 1

            @block.vector
            def _(dve):
                nc.vector.memset(c.convin_p[:, :, 0:3], 0.0).then_inc(pad_done, 1)
                for j in range(B_Q):
                    dve.wait_ge(blk_mm, j + 1)
                    nc.vector.tensor_copy(crow[:, j * P:(j + 1) * P],
                                          bank[4 + j % 2][0:NS + 3, 0:P]).then_inc(blk_dve, 1)
                for i in range(4):
                    dve.wait_ge(k_mm, i + 1)
                    if i >= 2:
                        dve.wait_ge(kst[i % 2], 32)
                    nc.vector.tensor_copy(krow[:, i % 2, 0:STILE],
                                          bank[4 + (i + 1) % 2][:].rearrange("p (t n) -> p t n", t=STILE))
                    nc.vector.tensor_copy(krow[0:NS, i % 2, STILE],
                                          bank[6 + (i + 1) % 2][0:NS, 0:P]).then_inc(k_ev, 1)
                dve.wait_ge(pad_done, 1)

            @block.gpsimd
            def _(pool):
                pool.wait_ge(blk_dve, B_Q)
                pool.dma_start(A["conv_p"][0], crow[0:3, :]).then_inc(store, 16)
                for b in range(NB):
                    pool.dma_start(A["conv_s"][b], crow[3 + TS * b + 1:3 + TS * (b + 1), :]).then_inc(store, 16)
                for j in range(B_K, B_QI):
                    pool.wait_ge(k_ev, j - B_K + 1)
                    o = (j - B_K) * P
                    pool.dma_start(A["k_p"].rearrange("(t p) n -> p t n", p=P)[:, :, o:o + P],
                                   krow[:, j % 2, 0:STILE]).then_inc(kst[j % 2], 16)
                    pool.dma_start(A["k_s"][:, o:o + P], krow[0:NS, j % 2, STILE]).then_inc(kst[j % 2], 16)
                pool.wait_ge(row_ev, NROW)
                pool.dma_start(A["v_p"].rearrange("(t p) n -> p t n", p=P), c.v[:, 0:STILE]).then_inc(store, 16)
                pool.dma_start(A["v_s"], c.v[0:NS, STILE]).then_inc(store, 16)
                pool.dma_start(A["kidx_p"].rearrange("(t p) n -> p t n", p=P),
                               c.small[:, 0:STILE, S_KI:S_KI + HD]).then_inc(store, 16)
                pool.dma_start(A["kidx_s"], c.small[0:NS, STILE, S_KI:S_KI + HD]).then_inc(store, 16)
                pool.wait_ge(store, 16 * (1 + NB + 4))
                pool.wait_ge(kst[0], 64)
                pool.wait_ge(kst[1], 64)


def stage_ssd(c):
    nc, A, bank = c.nc, c.A, c.bank
    with ExitStack() as es:
        def sb(name, shape, dt=F32):
            return es.enter_context(nc.sbuf_tensor(name, shape, dt))
        convw, convb = sb("convw", [P, KD, 4]), sb("convb", [P, KD])
        acc = sb("conv_acc", [P, 2, NT])
        xbcT = sb("xbcT", [P, KD, NT])
        xsN, BN = sb("xsN", [P, 512]), sb("BN", [P, 256])
        dtN, aN = sb("dtN", [P, NTILE, H]), sb("aN", [P, NTILE, H])
        negA = sb("negA", [P, H])
        u, w1, w2 = sb("sp_u", [P, NTILE, H]), sb("sp_1", [P, NTILE, H]), sb("sp_2", [P, NTILE, H])
        aexp = sb("aexp", [P, H, P])
        seg, M = sb("seg", [P, H, P]), sb("Mdecay", [P, H, P])
        Sm = sb("Smask", [P, 2, P])
        acum, last_, dte, ea, edl = (sb(n, [P, H]) for n in ("acum", "alast", "dte", "ea", "edl"))
        xd, xdd, y, t1 = (sb(n, [P, 512]) for n in ("xd", "xdd", "yssd", "yt"))
        hT = sb("stateT", [P, 512])
        rms = sb("rms", [P, 4])
        CTm = sb("CTm", [P, 2, NB, NS])
        stT = sb("stT", [P, NB, 512])
        stN = sb("stN", [P, NB, 4, P])
        aexp64 = sb("aexp64", [NS, H, HD])
        xddm = sb("xddm", [NS, NB, 512])
        eD = sb("eD", [P, 4, NB])
        ssmo = sb("ssmo", [P, 4, P])

        memT = stT[:, 0:4].rearrange("p a n -> p (a n)").rearrange("p (k m) -> p k m", k=KD)
        mvT, mko = stT[:, 4].rearrange("p (a m) -> p a m", a=2), stT[:, 5:7]
        wkv = stN[:, 0:6].rearrange("p b k n -> p (b k n)").rearrange("p (r k n) -> p r k n", r=3, k=KD)
        mem_in, wkv_in = c.sem("mem_in"), [c.sem(f"wkv_in{i}") for i in range(3)]
        mT_mm, mT_ev, mrow_mm, mrow_ev = (c.sem("mem_" + n) for n in ("T_mm", "T_ev", "row_mm", "row_ev"))
        conv_in, st_in = c.sem("ssd_in"), c.sem("state_in")
        conv_done, xbc_ready = c.sem("conv_done"), c.sem("xbc_ready")
        d_own, a_own = c.sem("ssd_dve"), c.sem("ssd_act")
        names = ("dt_pre", "dt_e", "tr_mm", "tr_ev", "a_ready", "cum_mm", "seg_pre", "decay", "ea_pre", "ea_done",
                 "m_ready", "y_mm", "y_done", "sz_done", "rms_pre", "rms_sqrt", "yn_ready", "ynT_mm", "ynT_ev",
                 "xdd_ready", "st_mm", "h_ready", "ho_mm", "ho_ev", "ns_mm", "ns_ev", "eD_mm", "eD_done", "ctm")
        s = {n: c.sem("ssd_" + n) for n in names}
        store = c.sem("ssd_store")
        vec = lambda name, n=P: c.vecs[0:n, VEC[name][0]:VEC[name][0] + VEC[name][1]]

        def by_head(ap, n, width=HD):
            return ap.unsqueeze(2).to_broadcast([n, H, width])

        with nc.Block() as block:
            @block.sync
            def _(sp):
                sp.dma_start(convw[:], A["conv_w"]).then_inc(conv_in, 16)
                sp.dma_start(convb[:], A["conv_b"]).then_inc(conv_in, 16)
                sp.dma_start(memT[:], A["memT"]).then_inc(mem_in, 16)
                for j in range(2 * MH):
                    if j >= 3:
                        sp.wait_ge(mT_mm, j - 2)
                    src = A["w_ck" if j < MH else "w_cv"][:, :, (j % MH) * P:(j % MH + 1) * P]
                    sp.dma_start(wkv[:, j % 3], src).then_inc(wkv_in[j % 3], 16)
                sp.wait_ge(mrow_ev, 2 * MH)
                sp.dma_start(A["memk_p"].rearrange("(k p) n -> p k n", p=P), mko[:]).then_inc(store, 16)
                sp.dma_start(A["memv_p"].rearrange("(k p) n -> p k n", p=P), c.mv[:]).then_inc(store, 16)
                sp.wait_ge(store, 32)
                sp.dma_start(stT[:], A["state_ssmT"]).then_inc(st_in, 16)
                sp.dma_start(stN[:], A["state_ssm"]).then_inc(st_in, 16)
                sp.wait_ge(s["ho_ev"], 1)
                sp.dma_start(A["ssm_p"].rearrange("(k p) n -> p k n", p=P), ssmo[:]).then_inc(store, 16)
                sp.wait_ge(s["ns_ev"], NB)
                sp.dma_start(A["ssm_s"].rearrange("b (k p) n -> p b k n", p=P), stN[:]).then_inc(store, 16)
                sp.wait_ge(store, 64)

            @block.tensor
            def _(pe):
                pe.wait_ge(mem_in, 16)

                def mem_rows(j):
                    pe.wait_ge(mT_ev, j + 1)
                    if j >= 2:
                        pe.wait_ge(mrow_ev, j - 1)
                    src = c.mkT[:, j] if j < MH else mvT[:, j % 2]
                    for m in range(2):
                        ins = nc.tensor.transpose(bank[2 + j % 2][:, m * P:(m + 1) * P], src[:, m * P:(m + 1) * P],
                                                  c.ident[:])
                    ins.then_inc(mrow_mm, 1)

                for j in range(2 * MH):
                    pe.wait_ge(wkv_in[j % 3], 16 * (j // 3 + 1))
                    if j >= 2:
                        pe.wait_ge(mT_ev, j - 1)
                    for k in range(KD):
                        ins = nc.tensor.matmul(bank[j % 2][:, 0:MEM], wkv[:, j % 3, k], memT[:, k],
                                               start=k == 0, stop=k == KD - 1)
                    ins.then_inc(mT_mm, 1)
                    if j:
                        mem_rows(j - 1)
                mem_rows(2 * MH - 1)

                pe.wait_ge(mrow_ev, 2 * MH)
                pe.wait_ge(xbc_ready, 2 * KD)

                def turn(t):
                    if t:
                        pe.wait_ge(s["h_ready"], t)
                    for k in range(6):
                        dst = bank[0][0:rows(t), k * P:(k + 1) * P] if k < 4 else \
                            bank[1][0:rows(t), (k - 4) * P:(k - 3) * P]
                        ins = nc.tensor.transpose(dst, xbcT[:, k, cols(t)], c.ident[:])
                    ins.then_inc(s["tr_mm"], 1)

                def sums(t):
                    n = rows(t)
                    tri, ones = (c.tri, c.ones) if t < STILE else (c.triS, c.onesS)
                    pe.wait_ge(s["a_ready"], t + 1)
                    nc.tensor.matmul(bank[2][0:n, 0:H], tri[0:n, 0:n], aN[0:n, t], start=True, stop=True)
                    nc.tensor.matmul(bank[2][0:n, H:2 * H], ones[0:n, 0:n], aN[0:n, t], start=True, stop=True)
                    for h in range(H):
                        nc.tensor.matmul(bank[3 + h // 4][0:n, (h % 4) * n:(h % 4 + 1) * n], aexp[0:n, h, 0:n],
                                         tri[0:n, 0:n], start=True, stop=True)
                    for g in range(2):
                        ins = nc.tensor.matmul(bank[5][0:n, g * n:(g + 1) * n], xbcT[:, 4 + g, cols(t)],
                                               xbcT[:, 6 + g, cols(t)], start=True, stop=True)
                    ins.then_inc(s["cum_mm"], 1)

                turn(0)
                sums(0)
                for t in range(NTILE):
                    n = rows(t)
                    sample = t == STILE
                    if t:
                        pe.wait_ge(s["ynT_ev"], t)
                    pe.wait_ge(s["m_ready"], t + 1)
                    for h in range(H):
                        ins = nc.tensor.matmul(bank[6][0:n, h * HD:(h + 1) * HD], M[0:n, h, 0:n],
                                               xd[0:n, h * HD:(h + 1) * HD], start=True, stop=True)
                    if sample:
                        pe.wait_ge(st_in, 32)
                        pe.wait_ge(s["ctm"], 1)
                        for g in range(2):
                            for b in range(NB):
                                ins = nc.tensor.matmul(bank[7][0:n, g * 256:(g + 1) * 256], CTm[:, g, b],
                                                       stT[:, b, g * 256:(g + 1) * 256],
                                                       start=b == 0, stop=b == NB - 1)
                    elif t:
                        for g in range(2):
                            ins = nc.tensor.matmul(bank[7][0:n, g * 256:(g + 1) * 256], xbcT[:, 6 + g, cols(t)],
                                                   hT[:, g * 256:(g + 1) * 256], start=True, stop=True)
                    ins.then_inc(s["y_mm"], 1)
                    if not sample:
                        pe.wait_ge(s["xdd_ready"], t + 1)
                        for g in range(2):
                            ins = nc.tensor.matmul(bank[0][:, g * 256:(g + 1) * 256], BN[:, g * P:(g + 1) * P],
                                                   xdd[:, g * 256:(g + 1) * 256], start=True, stop=True)
                        ins.then_inc(s["st_mm"], 1)
                        turn(t + 1)
                        sums(t + 1)
                    pe.wait_ge(s["yn_ready"], t + 1)
                    for k in range(4):
                        ins = nc.tensor.transpose(bank[6][:, k * n:(k + 1) * n], y[0:n, k * P:(k + 1) * P],
                                                  c.ident[0:n, 0:n])
                    ins.then_inc(s["ynT_mm"], 1)
                pe.wait_ge(s["h_ready"], STILE)
                for k in range(4):
                    ins = nc.tensor.transpose(bank[3][:, k * P:(k + 1) * P], hT[:, k * P:(k + 1) * P], c.ident[:])
                ins.then_inc(s["ho_mm"], 1)
                pe.wait_ge(s["xdd_ready"], NTILE)
                for k in range(4):
                    ins = nc.tensor.matmul(bank[2][:, 64 + k * NB:64 + (k + 1) * NB],
                                           aexp64[:].rearrange("p h d -> p (h d)")[:, k * P:(k + 1) * P],
                                           c.bsel[:], start=True, stop=True)
                ins.then_inc(s["eD_mm"], 1)
                for b in range(NB):
                    if b >= 2:
                        pe.wait_ge(s["ns_ev"], b - 1)
                    for k in range(4):
                        ins = nc.tensor.matmul(bank[4 + b % 2][:, k * P:(k + 1) * P], xddm[:, b, k * P:(k + 1) * P],
                                               BN[0:NS, (k // 2) * P:(k // 2 + 1) * P], start=True, stop=True)
                    ins.then_inc(s["ns_mm"], 1)

            @block.scalar
            def _(act):
                link = Link(act, a_own)
                act.wait_ge(s["dt_pre"], 1)
                link(nc.scalar.activation(negA[:], vec("a_log"), ACT.Exp), s["dt_e"])
                link(nc.scalar.activation(u[:], w1[:], ACT.Exp), s["dt_e"])

                def mem_row(j):
                    act.wait_ge(mrow_mm, j + 1)
                    dst = (mko if j < MH else c.mv)[:, :, (j % MH) * P:(j % MH + 1) * P]
                    nc.scalar.activation(dst, bank[2 + j % 2][:, 0:MEM].rearrange("p (m n) -> p m n", m=2),
                                         ACT.Copy).then_inc(mrow_ev, 1)

                for k in range(KD):
                    act.wait_ge(mT_mm, k + 1)
                    if k >= MH + 2:
                        act.wait_ge(mrow_mm, k - 1)
                    nc.scalar.activation(c.mkT[:, k] if k < MH else mvT[:, k % 2], bank[k % 2][:, 0:MEM],
                                         ACT.Copy).then_inc(mT_ev, 1)
                    if k:
                        mem_row(k - 1)
                    act.wait_ge(conv_done, 2 * (k + 1))
                    nc.scalar.activation(xbcT[:, k, 0:SEQ], acc[:, k % 2, 0:SEQ], ACT.Silu,
                                         bias=convb[:, k:k + 1]).then_inc(xbc_ready, 1)
                    nc.scalar.activation(xbcT[:, k, SEQ:NT], acc[:, k % 2, SEQ:NT], ACT.Silu,
                                         bias=convb[:, k:k + 1]).then_inc(xbc_ready, 1)
                mem_row(2 * MH - 1)
                for t in range(NTILE):
                    n = rows(t)
                    nc.scalar.activation(c.z[0:n, t], c.z[0:n, t], ACT.Silu).then_inc(s["sz_done"], 1)
                for t in range(NTILE):
                    n = rows(t)
                    act.wait_ge(s["seg_pre"], t + 1)
                    nc.scalar.activation(seg[0:n, :, 0:n], seg[0:n, :, 0:n], ACT.Exp).then_inc(s["decay"], 1)
                    nc.scalar.activation(ea[0:n, :], acum[0:n, :], ACT.Exp).then_inc(s["ea_done"], 1)
                    nc.scalar.activation(dte[0:n, :], dte[0:n, :], ACT.Exp).then_inc(s["ea_done"], 1)
                    nc.scalar.activation(edl[0:n, :], last_[0:n, :], ACT.Exp).then_inc(s["ea_done"], 1)
                    act.wait_ge(s["rms_pre"], t + 1)
                    nc.scalar.activation(rms[0:n, 1:2], rms[0:n, 1:2], ACT.Sqrt).then_inc(s["rms_sqrt"], 1)
                    act.wait_ge(s["ynT_mm"], t + 1)
                    nc.scalar.activation(c.mixedT[:, 0:4, cols(t)],
                                         bank[6][:, 0:4 * n].rearrange("p (k n) -> p k n", k=4),
                                         ACT.Copy).then_inc(s["ynT_ev"], 1)
                act.wait_ge(s["ho_mm"], 1)
                nc.scalar.activation(ssmo[:], bank[3][:].rearrange("p (k n) -> p k n", k=4),
                                     ACT.Copy).then_inc(s["ho_ev"], 1)
                act.wait_ge(s["eD_mm"], 1)
                nc.scalar.activation(eD[:], bank[2][:, 64:64 + 4 * NB].rearrange("p (k b) -> p k b", k=4),
                                     ACT.Exp).then_inc(s["eD_done"], 1)

            @block.vector
            def _(dve):
                V = nc.vector
                link = Link(dve, d_own)
                link(V.memset(aN[:], 0.0))
                for t in range(NTILE):
                    link(V.tensor_tensor(dtN[0:rows(t), t], c.small[0:rows(t), t, S_DT:S_DT + H],
                                         vec("dt_bias", rows(t)), ALU.add))
                link(V.memset(w1[:], 0.0))
                for t in range(NTILE):
                    n = rows(t)
                    link(V.tensor_scalar(w1[0:n, t], dtN[0:n, t], -1.0, None, ALU.mult))
                    link(V.tensor_tensor(w1[0:n, t], w1[0:n, t], dtN[0:n, t], ALU.min),
                         s["dt_pre"] if t == STILE else None)
                dve.wait_ge(s["dt_e"], 2)
                link(V.tensor_scalar(negA[:], negA[:], -1.0, None, ALU.mult))
                link(V.tensor_scalar(w1[:], u[:], 2.0, None, ALU.add))
                link(V.reciprocal(w1[:], w1[:]))
                link(V.tensor_tensor(u[:], u[:], w1[:], ALU.mult))
                link(V.tensor_tensor(w1[:], u[:], u[:], ALU.mult))
                link(V.tensor_scalar(w2[:], w1[:], 1 / 19, 1 / 17, ALU.mult, ALU.add))
                for q in (15, 13, 11, 9, 7, 5, 3, 1):
                    link(V.tensor_tensor(w2[:], w2[:], w1[:], ALU.mult))
                    link(V.tensor_scalar(w2[:], w2[:], 1 / q, None, ALU.add))
                link(V.tensor_tensor(w2[:], w2[:], u[:], ALU.mult))
                for t in range(NTILE):
                    n = rows(t)
                    link(V.tensor_scalar(dtN[0:n, t], dtN[0:n, t], 0.0, None, ALU.max))
                    link(V.scalar_tensor_tensor(dtN[0:n, t], w2[0:n, t], 2.0, dtN[0:n, t], ALU.mult, ALU.add))
                    link(V.tensor_tensor(aN[0:n, t], dtN[0:n, t], negA[0:n, :], ALU.mult))
                dve.wait_ge(conv_in, 32)
                for k in range(KD):
                    if k >= 2:
                        dve.wait_ge(xbc_ready, 2 * (k - 1))
                    ap = acc[:, k % 2, 0:SEQ]
                    as_ = acc[:, k % 2, SEQ:NT].rearrange("p (b t) -> p b t", b=NB)
                    for tap in range(4):
                        w = convw[:, k, tap:tap + 1]
                        sem = conv_done if tap == 3 else None
                        xp, xs = c.convin_p[:, k, tap:tap + SEQ], c.convin_s[:, k, :, tap:tap + TS]
                        if tap == 0:
                            link(V.tensor_scalar(ap, xp, w, None, ALU.mult))
                            link(V.tensor_scalar(as_, xs, w, None, ALU.mult))
                        else:
                            link(V.scalar_tensor_tensor(ap, xp, w, ap, ALU.mult, ALU.add), sem)
                            link(V.scalar_tensor_tensor(as_, xs, w, as_, ALU.mult, ALU.add), sem)
                dve.wait_ge(xbc_ready, 2 * KD)
                for g in range(2):
                    link(V.tensor_tensor(CTm[:, g], xbcT[:, 6 + g, SEQ:NT].unsqueeze(1).to_broadcast([P, NB, NS]),
                                         c.bcol[:], ALU.mult), s["ctm"] if g else None)
                def spread(t):
                    n = rows(t)
                    link(V.tensor_copy(aexp[0:n, :, 0:n], by_head(aN[0:n, t], n, n)), s["a_ready"])

                spread(0)
                for t in range(NTILE):
                    n = rows(t)
                    sample = t == STILE
                    hd = lambda ap: ap[0:n, :].rearrange("p (h d) -> p h d", h=H)
                    if t:
                        dve.wait_ge(s["st_mm"], t)
                    dve.wait_ge(s["tr_mm"], t + 1)
                    link(V.tensor_copy(xsN[0:n, :], bank[0][0:n, :]))
                    link(V.tensor_copy(BN[0:n, :], bank[1][0:n, 0:256]))
                    if t:
                        dve.wait_ge(s["y_mm"], t)
                    link(V.tensor_tensor(hd(xd), hd(xsN), by_head(dtN[0:n, t], n), ALU.mult))
                    dve.wait_ge(s["cum_mm"], t + 1)
                    link(V.tensor_copy(acum[0:n, :], bank[2][0:n, 0:H]))
                    link(V.tensor_copy(last_[0:n, :], bank[2][0:n, H:2 * H]))
                    link(V.tensor_tensor(dte[0:n, :], last_[0:n, :], acum[0:n, :], ALU.subtract))
                    for q in range(2):
                        link(V.tensor_tensor(seg[0:n, 4 * q:4 * q + 4, 0:n],
                                             bank[3 + q][0:n, 0:4 * n].rearrange("p (h i) -> p h i", h=4),
                                             acum[0:n, 4 * q:4 * q + 4].unsqueeze(2).to_broadcast([n, 4, n]),
                                             ALU.subtract))
                    link(V.tensor_scalar(seg[0:n, :, 0:n], seg[0:n, :, 0:n], 0.0, None, ALU.min), s["seg_pre"])
                    tri = c.tri[0:n, 0:n] if not sample else c.triS[:]
                    link(V.tensor_tensor(Sm[0:n, :, 0:n], bank[5][0:n, 0:2 * n].rearrange("p (g i) -> p g i", g=2),
                                         tri.unsqueeze(1).to_broadcast([n, 2, n]), ALU.mult))
                    if not sample:
                        spread(t + 1)
                    dve.wait_ge(s["decay"], t + 1)
                    for g in range(2):
                        link(V.tensor_tensor(M[0:n, 4 * g:4 * g + 4, 0:n], seg[0:n, 4 * g:4 * g + 4, 0:n],
                                             Sm[0:n, g, 0:n].unsqueeze(1).to_broadcast([n, 4, n]), ALU.mult),
                             s["m_ready"] if g else None)
                    dve.wait_ge(s["ea_done"], 3 * (t + 1))
                    link(V.tensor_tensor(hd(xdd), hd(xd), by_head(dte[0:n, :], n), ALU.mult),
                         s["xdd_ready"] if not sample else None)
                    if t:
                        dve.wait_ge(s["ynT_mm"], t)
                    link(V.tensor_tensor(hd(y), hd(xsN), by_head(vec("d_skip", n), n), ALU.mult))
                    dve.wait_ge(s["y_mm"], t + 1)
                    if t:
                        link(V.tensor_tensor(hd(t1), hd(bank[7]), by_head(ea[0:n, :], n), ALU.mult))
                        link(V.tensor_tensor(y[0:n, :], y[0:n, :], t1[0:n, :], ALU.add))
                    link(V.tensor_tensor(y[0:n, :], y[0:n, :], bank[6][0:n, :], ALU.add), s["y_done"])
                    if not sample:
                        dve.wait_ge(s["st_mm"], t + 1)
                        if t:
                            link(V.tensor_tensor(hd(hT), hd(hT), by_head(edl[:], P), ALU.mult))
                            link(V.tensor_tensor(hT[:], hT[:], bank[0][:], ALU.add), s["h_ready"])
                        else:
                            link(V.tensor_copy(hT[:], bank[0][:]), s["h_ready"])
                    dve.wait_ge(s["sz_done"], t + 1)
                    link(V.tensor_tensor(y[0:n, :], y[0:n, :], c.z[0:n, t], ALU.mult))
                    link(V.tensor_tensor_reduce(out=t1[0:n, :], in0=y[0:n, :], in1=y[0:n, :], scale=1.0, scalar=0.0,
                                                op0=ALU.mult, op1=ALU.add, accum_out=rms[0:n, 0:1]))
                    link(V.tensor_scalar(rms[0:n, 1:2], rms[0:n, 0:1], 1 / 512, EPS, ALU.mult, ALU.add), s["rms_pre"])
                    dve.wait_ge(s["rms_sqrt"], t + 1)
                    link(V.reciprocal(rms[0:n, 2:3], rms[0:n, 1:2]))
                    link(V.scalar_tensor_tensor(y[0:n, :], y[0:n, :], rms[0:n, 2:3], vec("ssd_norm_w", n),
                                                ALU.mult, ALU.mult), s["yn_ready"])
                link(V.tensor_copy(aexp64[:], by_head(aN[0:NS, STILE], NS)))
                for b in range(NB):
                    link(V.tensor_scalar(xddm[:, b], xdd[0:NS, :], c.bsel[:, b:b + 1], None, ALU.mult),
                         s["xdd_ready"] if b == NB - 1 else None)
                dve.wait_ge(s["eD_done"], 1)
                for b in range(NB):
                    dve.wait_ge(s["ns_mm"], b + 1)
                    for k in range(4):
                        link(V.scalar_tensor_tensor(stN[:, b, k], stN[:, b, k], eD[:, k, b:b + 1],
                                                    bank[4 + b % 2][:, k * P:(k + 1) * P], ALU.mult, ALU.add),
                             s["ns_ev"] if k == 3 else None)


def stage_dsa_prompt(c):
    nc, A, bank = c.nc, c.A, c.bank
    NTP = SEQ // P
    BW = 2 * P
    topk = min(256, SEQ // 4)
    with ExitStack() as es:
        def sb(name, shape, dt=F32):
            return es.enter_context(nc.sbuf_tensor(name, shape, dt))
        relb = sb("relb", [NBUCKET, H])
        relx = sb("relx", [NBUCKET, H, P])
        onehot = sb("onehot", [NBUCKET, 3 * P])
        spread = sb("spread", [P, H, 3 * P])
        T = sb("Tbias", [P, H, BW])
        relu = sb("relu", [P, 2, SEQ])
        sc = sb("scores", [P, SEQ])
        wi = sb("wi", [P, H])
        m8 = sb("max8", [P, 8])
        msk = sb("mask", [P, 2, SEQ])
        L = sb("logits", [P, 2, SEQ])
        E = sb("probs", [P, 2, SEQ])
        PT = sb("probsT", [P, 2, NTP, P])
        mx, den, rden = sb("mx", [P, H]), sb("den", [P, H]), sb("rden", [P, H])
        o = sb("att", [P, 512])
        scratch = nc.dram_tensor("bias_scratch", [P, H * 3 * P], F32, kind="Internal").ap()

        kiZ, kZ = sb("ki_halves", [P, 2, SEQ]), sb("k_halves", [P, 2, 4, SEQ])
        pt = c.ptab
        names = ("in", "halves", "relx", "sp_mm", "sp_ev", "sp_st", "T_in", "idx_mm", "relu", "relu_used", "mask",
                 "qk_mm", "logit", "exp", "tr_mm", "pt", "pv_mm", "att", "attT_mm", "attT")
        s = {n: c.sem("dsap_" + n) for n in names}
        d_own = c.sem("dsap_dve")

        with nc.Block() as block:
            @block.sync
            def _(sp):
                sp.dma_start(relb[:], A["rel_bias"]).then_inc(s["in"], 16)
                sp.dma_start(onehot[:], A["bucket_rev"]).then_inc(s["in"], 16)
                sp.wait_ge(s["sp_ev"], H)
                sp.dma_start(scratch[:, :], spread[:].rearrange("p h m -> p (h m)")).then_inc(s["sp_st"], 16)
                sp.wait_ge(s["sp_st"], 16)
                skew = bass.AP(scratch.tensor, P - 1, [[H * 3 * P - 1, P], [3 * P, H], [1, BW]])
                sp.dma_start(T[:], skew).then_inc(s["T_in"], 16)
                sp.dma_start(pt[:], A["page_table"]).then_inc(c.pt_in, 16)
                sp.wait_ge(c.pt_in, 16)
                for b in range(NB):
                    for j in range(NPAGE):
                        page = sp.value_load(pt[0:1, b * NPAGE + j:b * NPAGE + j + 1], min_val=0,
                                             max_val=A["kidxT"].shape[0] - 1)
                        sp.dma_start(c.kiS(b)[:, j * PAGE:(j + 1) * PAGE],
                                     A["kidxT"][bass.ds(page, 1)].rearrange("a d n -> d (a n)")
                                     ).then_inc(c.ki_in, 16)
                sp.wait_ge(s["T_in"], 16)
                sp.wait_ge(c.ki_in, 16 * NB * NPAGE)

            @block.tensor
            def _(pe):
                pe.wait_ge(s["in"], 32)
                pe.wait_ge(s["relx"], 1)
                for h in range(H):
                    if h >= 2:
                        pe.wait_ge(s["sp_ev"], h - 1)
                    nc.tensor.matmul(bank[h % 2][:, 0:3 * P], relx[:, h], onehot[:], start=True,
                                     stop=True).then_inc(s["sp_mm"], 1)
                pe.wait_ge(s["sp_ev"], H)

                def scores(t):
                    nk = (t + 1) * P
                    for h in range(H):
                        n = t * H + h
                        if n >= 2:
                            pe.wait_ge(s["relu"], n - 1)
                        if h == 0 and t >= 2:
                            pe.wait_ge(s["logit"], (t - 1) * H)
                        nc.tensor.matmul(bank[h % 2][:, 0:nk], c.qiT[:, h // 2, cols(t)], kiZ[:, h % 2, 0:nk],
                                         start=True, stop=True).then_inc(s["idx_mm"], 1)

                def attend(t):
                    nk = (t + 1) * P

                    def tail(h):
                        n = t * H + h
                        pe.wait_ge(s["exp"], n + 1)
                        if n >= 2:
                            pe.wait_ge(s["pt"], n - 1)
                        for k in range(t + 1):
                            ins = nc.tensor.transpose(bank[4 + h % 2][:, k * P:(k + 1) * P],
                                                      E[:, h % 2, k * P:(k + 1) * P], c.ident[:])
                        ins.then_inc(s["tr_mm"], 1)
                        pe.wait_ge(s["pt"], n + 1)
                        for k in range(t + 1):
                            ins = nc.tensor.matmul(bank[6][:, h * HD:(h + 1) * HD], PT[:, h % 2, k],
                                                   c.v[:, k, h * HD:(h + 1) * HD], start=k == 0, stop=k == t)
                        ins.then_inc(s["pv_mm"], 1)

                    def qk(h):
                        n = t * H + h
                        if n >= 4:
                            pe.wait_ge(s["logit"], n - 3)
                        nc.tensor.matmul(bank[h % 4][:, 0:nk], c.qT[:, h // 2, cols(t)],
                                         kZ[:, h % 2, h // 2, 0:nk], start=True, stop=True).then_inc(s["qk_mm"], 1)

                    pe.wait_ge(s["relu"], min(t + 2, NTP) * H)
                    for h in range(3):
                        qk(h)
                    if t:
                        pe.wait_ge(s["att"], t)
                    for h in range(H):
                        tail(h)
                        if h + 3 < H:
                            qk(h + 3)
                    pe.wait_ge(s["att"], t + 1)
                    if t:
                        pe.wait_ge(s["attT"], t)
                    for k in range(4):
                        ins = nc.tensor.transpose(bank[7][:, k * P:(k + 1) * P], o[:, k * P:(k + 1) * P], c.ident[:])
                    ins.then_inc(s["attT_mm"], 1)

                pe.wait_ge(s["halves"], 1)
                scores(0)
                for t in range(NTP):
                    if t + 1 < NTP:
                        scores(t + 1)
                    attend(t)

            @block.scalar
            def _(act):
                def relus(t):
                    nk = (t + 1) * P
                    for h in range(H):
                        n = t * H + h
                        act.wait_ge(s["idx_mm"], n + 1)
                        if n >= 2:
                            act.wait_ge(s["relu_used"], n - 1)
                        nc.scalar.activation(relu[:, h % 2, 0:nk], bank[h % 2][:, 0:nk], ACT.Relu,
                                             scale=HD ** -0.5).then_inc(s["relu"], 1)

                def attend(t):
                    nk = (t + 1) * P
                    for h in range(H):
                        n = t * H + h
                        act.wait_ge(s["logit"], n + 1)
                        if n >= 2:
                            act.wait_ge(s["tr_mm"], n - 1)
                        nc.scalar.activation(E[:, h % 2, 0:nk], L[:, h % 2, 0:nk], ACT.Exp, bias=mx[:, h:h + 1],
                                             accum_out=den[:, h:h + 1]).then_inc(s["exp"], 1)
                        act.wait_ge(s["tr_mm"], n + 1)
                        if n >= 2:
                            act.wait_ge(s["pv_mm"], n - 1)
                        nc.scalar.activation(PT[:, h % 2, 0:t + 1], bank[4 + h % 2][:, 0:nk].rearrange(
                            "p (k q) -> p k q", q=P), ACT.Copy).then_inc(s["pt"], 1)
                    act.wait_ge(s["attT_mm"], t + 1)
                    nc.scalar.activation(c.mixedT[:, 4:8, cols(t)], bank[7][:].rearrange("p (k q) -> p k q", k=4),
                                         ACT.Copy).then_inc(s["attT"], 1)

                relus(0)
                for t in range(NTP):
                    if t + 1 < NTP:
                        relus(t + 1)
                    attend(t)

            @block.vector
            def _(dve):
                V = nc.vector
                link = Link(dve, d_own)
                link(V.memset(kiZ[:], 0.0))
                link(V.memset(kZ[:], 0.0))
                for i in range(2):
                    half = slice(HD * i, HD * (i + 1))
                    link(V.tensor_copy(kiZ[half, i], c.kiT[half, 0:SEQ]))
                    link(V.tensor_copy(kZ[half, i], c.kT[half, :, 0:SEQ]), s["halves"] if i else None)
                dve.wait_ge(s["in"], 32)
                link(V.tensor_copy(relx[:], relb[:].unsqueeze(2).to_broadcast([NBUCKET, H, P])), s["relx"])
                for h in range(H):
                    dve.wait_ge(s["sp_mm"], h + 1)
                    link(V.tensor_copy(spread[:, h], bank[h % 2][:, 0:3 * P]), s["sp_ev"])

                def select(t):
                    nk = (t + 1) * P
                    link(V.tensor_scalar(wi[:], c.small[:, t, S_WI:S_WI + H], H ** -0.5, None, ALU.mult))
                    for h in range(H):
                        dve.wait_ge(s["relu"], t * H + h + 1)
                        if h == 0:
                            link(V.tensor_scalar(sc[:, 0:nk], relu[:, 0, 0:nk], wi[:, 0:1], None, ALU.mult),
                                 s["relu_used"])
                        else:
                            link(V.scalar_tensor_tensor(sc[:, 0:nk], relu[:, h % 2, 0:nk], wi[:, h:h + 1],
                                                        sc[:, 0:nk], ALU.mult, ALU.add), s["relu_used"])
                    own = sc[:, t * P:nk]
                    link(V.tensor_tensor(own, own, c.low[:], ALU.mult))
                    link(V.tensor_tensor(own, own, c.lowneg[:], ALU.add))
                    if nk > topk:
                        for _ in range(topk // 8):
                            link(V.max(m8[:], sc[:, 0:nk]))
                            link(V.match_replace(sc[:, 0:nk], m8[:], sc[:, 0:nk], PICKED))
                        link(V.tensor_scalar(msk[:, t % 2, 0:nk], sc[:, 0:nk], -2.9e38, NOT_SELECTED, ALU.is_gt,
                                             ALU.mult))
                    else:
                        link(V.tensor_scalar(msk[:, t % 2, 0:nk], sc[:, 0:nk], -1.9e38, NOT_SELECTED, ALU.is_lt,
                                             ALU.mult))

                def attend(t):
                    nk = (t + 1) * P
                    far = max(0, nk - BW)
                    for h in range(H):
                        n = t * H + h
                        dve.wait_ge(s["qk_mm"], n + 1)
                        if n >= 2:
                            dve.wait_ge(s["exp"], n - 1)
                        ps, l = bank[h % 4], L[:, h % 2]
                        a = VEC["bias_far"][0] + h
                        if far:
                            link(V.tensor_scalar(l[:, 0:far], ps[:, 0:far], HD ** -0.5, c.vecs[:, a:a + 1],
                                                 ALU.mult, ALU.add))
                        link(V.scalar_tensor_tensor(l[:, far:nk], ps[:, far:nk], HD ** -0.5,
                                                    T[:, h, BW - (nk - far):BW], ALU.mult, ALU.add))
                        link(V.tensor_tensor(l[:, 0:nk], l[:, 0:nk], msk[:, t % 2, 0:nk], ALU.add))
                        if t:
                            dve.wait_ge(s["exp"], t * H)
                        link(V.reduce_max(mx[:, h:h + 1], l[:, 0:nk], AX_X))
                        link(V.tensor_scalar(mx[:, h:h + 1], mx[:, h:h + 1], -1.0, None, ALU.mult), s["logit"])
                    dve.wait_ge(s["exp"], (t + 1) * H)
                    link(V.reciprocal(rden[:], den[:]))
                    dve.wait_ge(s["pv_mm"], (t + 1) * H)
                    if t:
                        dve.wait_ge(s["attT_mm"], t)
                    link(V.tensor_tensor(o[:].rearrange("p (h d) -> p h d", h=H),
                                         bank[6][:].rearrange("p (h d) -> p h d", h=H),
                                         rden[:].unsqueeze(2).to_broadcast([P, H, HD]), ALU.mult), s["att"])

                select(0)
                dve.wait_ge(s["T_in"], 16)
                for t in range(NTP):
                    if t + 1 < NTP:
                        select(t + 1)
                    attend(t)


def stage_dsa_sample(c):
    nc, A, bank = c.nc, c.A, c.bank
    HT = H * TS
    HB = NB // 2
    NKC = PAST // 512
    topk = min(256, (PAST + TS) // 4)
    UP = 512 // PAGE
    RING = KV_RING
    pt, ring = c.ptab, c.kvring
    with ExitStack() as es:
        def sb(name, shape, dt=F32):
            return es.enter_context(nc.sbuf_tensor(name, shape, dt))
        qiS = sb("qiS", [P, NB // 2, 2, H, TS])
        swapped = sb("qi_swapped", [P, 4, NS])
        L = sb("logitsS", [P, 2, NKEY])
        wv = sb("wv", [P, 2])
        wx = sb("wx", [NS, H, TS])
        tsel = sb("tsel", [NS, TS])
        Wsel = sb("Wsel", [P, 2, NS])
        rS = sb("reluS", [P, NKEY])
        sc = sb("scS", [NS, NKEY])
        m8 = sb("m8S", [NS, 8])
        msk = sb("mskS", [P, NKEY])
        relb, trow = sb("relbS", [TS * NBUCKET, H]), sb("trow", [TS * NBUCKET, TS])
        RB = sb("RB", [TS * NBUCKET, HB, H, TS])
        oh = sb("ohS", [TS * NBUCKET, NKEY])
        exp_rows = sb("exp_rows", [P, 2, P])
        hmask = sb("hmask", [P, 4, H])
        omask = sb("omask", [HT, 512])
        tsum = sb("tsum", [HT, TS])
        wmask = sb("wmask", [P, 2, NS])
        Q = sb("Qblk", [P, 2, HB, 4, P])
        Qall = sb("Qall", [P, 2, 4, P])
        PT = sb("PTS", [P, NPAGE + 1, P])
        mx, ngm, den = sb("mxS", [P, 2, NKC + 1]), sb("ngm", [P, 2]), sb("denS", [P, 2, NKC + 1])
        dsum, rden = sb("dsum", [P, 2]), sb("rdenS", [P, 2])
        Om = rS[0:HT, 0:1024].rearrange("r (a n) -> r a n", a=2)

        names = ("c_in", "swap_in", "wx", "wv_mm", "q_ready", "w_ready", "idx_mm", "relu",
                 "sel_mm", "sc_ready", "mask", "rb", "qblk", "log_mm", "logit", "mask_mm", "masked", "max", "exp",
                 "prob", "tr_mm", "pt", "pv_mm", "om", "ot_mm", "ot")
        s = {n: c.sem("dsas_" + n, n == "swap_in") for n in names}
        kv_in = [c.sem(f"kv_in{i}", i % 2 == 1) for i in range(RING)]
        kv_used = c.sem("kv_used")
        d_own, a_own = c.sem("dsas_dve"), c.sem("dsas_act")

        def unit(g, kind, b, q):
            return (kind * 2 + g) * HB * NKC + (b * NKC + q if kind else q * HB + b)

        def load_units(eng, parity):
            for kind, src in enumerate((A["kT_pages"], A["v_pages"])):
                for g in range(2):
                    for m in range(parity, HB * NKC, 2):
                        n = unit(g, kind, 0, 0) + m
                        b, q = (m // NKC, m % NKC) if kind else (m % HB, m // HB)
                        if n == 2 + parity:
                            eng.wait_ge(s["sel_mm"], 2)
                        if n >= RING:
                            eng.wait_ge(kv_used, n - RING + 1)
                        for j in range(UP):
                            at = (g * HB + b) * NPAGE + q * UP + j
                            page = eng.value_load(pt[0:1, at:at + 1], min_val=0, max_val=src.shape[0] - 1)
                            eng.dma_start(ring[:, n % RING, j * 512:(j + 1) * 512],
                                          src[bass.ds(page, 1)].rearrange("a p n -> p (a n)")
                                          ).then_inc(kv_in[n % RING], 16)

        with nc.Block() as block:
            @block.sync
            def _(sp):
                for t in range(TS):
                    sp.dma_start(relb[t * NBUCKET:(t + 1) * NBUCKET], A["rel_bias"]).then_inc(s["c_in"], 16)
                for dst, src in ((oh, "bucket_keys"), (trow, "t_rows"),
                                 (exp_rows, "expand_rows"), (hmask, "head_mask"), (omask, "out_mask"),
                                 (tsel, "t_sel"), (tsum, "t_sum"), (wmask, "w_mask")):
                    sp.dma_start(dst[:], A[src]).then_inc(s["c_in"], 16)
                load_units(sp, 0)

            @block.gpsimd
            def _(pool):
                for lo in (0, HD):
                    pool.dma_start(swapped[lo:lo + HD], c.qiT[HD - lo:P - lo, :, SEQ:NT]).then_inc(s["swap_in"], 16)
                pool.wait_ge(s["swap_in"], 32)
                load_units(pool, 1)

            @block.scalar
            def _(act):
                for g in range(2):
                    for q in range(NKC + 1):
                        n = g * (NKC + 1) + q
                        act.wait_ge(s["idx_mm"], n + 1)
                        if g and q == 0:
                            act.wait_ge(s["sel_mm"], g)
                        w = 512 if q < NKC else NS
                        nc.scalar.activation(rS[:, q * 512:q * 512 + w], bank[4 + q % 3][:, 0:w],
                                             ACT.Relu, scale=HD ** -0.5).then_inc(s["relu"], 1)
                for q in range(NKC + 1):
                    w = 512 if q < NKC else NS
                    src = bank[q] if q < NKC else bank[7]
                    if q == 0:
                        act.wait_ge(s["sel_mm"], 2)
                    nc.scalar.activation(sc[:, q * 512:q * 512 + w], src[0:NS, 0:w], ACT.Copy
                                         ).then_inc(s["sc_ready"], 1)
                for g in range(2):
                    for q in range(NKC + 1):
                        act.wait_ge(s["log_mm"], g * (NKC + 1) + q + 1)
                        w = 512 if q < NKC else NS
                        nc.scalar.activation(L[:, g, q * 512:q * 512 + w], bank[q][:, 0:w], ACT.Copy
                                             ).then_inc(s["logit"], 1)
                for g in range(2):
                    act.wait_ge(s["max"], g + 1)
                    for q in range(NKC + 1):
                        part = L[:, g, q * 512:q * 512 + (512 if q < NKC else NS)]
                        nc.scalar.activation(part, part, ACT.Exp, bias=ngm[:, g:g + 1],
                                             accum_out=den[:, g, q:q + 1]).then_inc(s["exp"], 1)
                for g in range(2):
                    for q in range(5):
                        act.wait_ge(s["tr_mm"], 5 * g + q + 1)
                        if g and q == 0:
                            act.wait_ge(s["pv_mm"], HB * g)
                        if q < 4:
                            nc.scalar.activation(PT[:, 4 * q:4 * q + 4],
                                                 bank[3 + q % 2][:].rearrange("p (k r) -> p k r", k=4),
                                                 ACT.Copy).then_inc(s["pt"], 1)
                        else:
                            nc.scalar.activation(PT[0:NS, NPAGE], bank[3 + q % 2][0:NS, 0:P], ACT.Copy
                                                 ).then_inc(s["pt"], 1)
                    act.wait_ge(s["ot_mm"], HB * (g + 1))
                    nc.scalar.activation(c.mixedT[:, 4:8, SEQ + HB * TS * g:SEQ + HB * TS * (g + 1)],
                                         bank[7][:, 128:128 + 4 * HB * TS].rearrange("p (k r) -> p k r", k=4),
                                         ACT.Copy).then_inc(s["ot"], 1)

            @block.tensor
            def _(pe):
                pe.wait_ge(s["wx"], 1)
                for b in range(HB):
                    ins = nc.tensor.matmul(bank[7][b * HT:(b + 1) * HT, 0:2], wx[:].rearrange("r h t -> r (h t)"),
                                           c.bsel[:].rearrange("r (g b) -> r b g", g=2)[:, b], start=True, stop=True)
                ins.then_inc(s["wv_mm"], 1)
                pe.wait_ge(s["q_ready"], 1)
                pe.wait_ge(s["w_ready"], 1)
                for g in range(2):
                    for q in range(NKC + 1):
                        n = g * (NKC + 1) + q
                        if q >= 3:
                            pe.wait_ge(s["relu"], n - 2)
                        elif g:
                            pe.wait_ge(s["relu"], g * (NKC + 1))
                        for i in range(2):
                            pair = 2 * g + i
                            w, rhs = (512, ring[:, 2 + pair, q * 512:(q + 1) * 512]) if q < NKC else (
                                NS, c.kiT[:, SEQ:NT])
                            ins = nc.tensor.matmul(bank[4 + q % 3][HD * i:HD * (i + 1), 0:w],
                                                   qiS[:, pair].rearrange("d b h t -> d (b h t)"), rhs,
                                                   start=True, stop=True)
                        ins.then_inc(s["idx_mm"], 1)
                    for q in range(NKC + 1):
                        pe.wait_ge(s["relu"], g * (NKC + 1) + q + 1)
                        w = 512 if q < NKC else NS
                        ins = nc.tensor.matmul(bank[q if q < NKC else 7][0:NS, 0:w], Wsel[:, g],
                                               rS[:, q * 512:q * 512 + w], start=g == 0, stop=g == 1)
                    ins.then_inc(s["sel_mm"], 1)

                pe.wait_ge(s["rb"], 1)
                pe.wait_ge(s["qblk"], 3)
                for g in range(2):
                    for q in range(NKC + 1):
                        if g:
                            pe.wait_ge(s["logit"], q + 1)
                        elif q == 0:
                            pe.wait_ge(s["sc_ready"], NKC + 1)
                        w = 512 if q < NKC else NS
                        for b in range(HB if q < NKC else 0):
                            n = unit(g, 0, b, q)
                            pe.wait_ge(kv_in[n % RING], 16 * UP * (n // RING + 1))
                            kk = ring[:, n % RING].rearrange("p (j k n) -> p k j n", j=UP, k=4)
                            for k in range(4):
                                ins = nc.tensor.matmul(bank[q][:], Q[:, g, b, k], kk[:, k],
                                                       start=b == 0 and k == 0, stop=False)
                            ins.then_inc(kv_used, 1)
                        if q == NKC:
                            for k in range(4):
                                nc.tensor.matmul(bank[NKC][:, 0:NS], Qall[:, g, k], c.kT[:, k, SEQ:NT],
                                                 start=k == 0, stop=False)
                        nc.tensor.matmul(bank[q][:, 0:w], RB[:].rearrange("k b h t -> k (b h t)"),
                                         oh[:, q * 512:q * 512 + w], start=False, stop=True).then_inc(s["log_mm"], 1)

                def masks(g):
                    for q in range(NKC + 1):
                        n = g * (NKC + 1) + q
                        if n >= 2:
                            pe.wait_ge(s["masked"], n - 1)
                        w = 512 if q < NKC else NS
                        nc.tensor.matmul(bank[1 + n % 2][:, 0:w], exp_rows[:, g], msk[:, q * 512:q * 512 + w],
                                         start=True, stop=True).then_inc(s["mask_mm"], 1)

                pe.wait_ge(s["mask"], 1)
                pe.wait_ge(s["logit"], 2 * (NKC + 1))
                masks(0)
                masks(1)
                for g in range(2):
                    pe.wait_ge(s["prob"], g + 1)
                    for q in range(5):
                        if q >= 2:
                            pe.wait_ge(s["pt"], 5 * g + q - 1)
                        for k in range(4 * q, min(4 * q + 4, NPAGE + 1)):
                            m = P if k < NPAGE else NS
                            ins = nc.tensor.transpose(bank[3 + q % 2][0:m, (k % 4) * P:(k % 4 + 1) * P],
                                                      L[:, g, k * P:k * P + m], c.ident[:])
                        ins.then_inc(s["tr_mm"], 1)
                    pe.wait_ge(s["pt"], 5 * (g + 1))

                    def out_T(b):
                        pe.wait_ge(s["om"], g * HB + b + 1)
                        for k in range(4):
                            at = 128 + k * HB * TS + b * TS
                            ins = nc.tensor.matmul(bank[7][:, at:at + TS], Om[:, b % 2, k * P:(k + 1) * P], tsum[:],
                                                   start=True, stop=True)
                        ins.then_inc(s["ot_mm"], 1)

                    for b in range(HB):
                        n0 = g * HB + b
                        if n0 >= 2:
                            pe.wait_ge(s["om"], n0 - 1)
                        for q in range(NKC):
                            n = unit(g, 1, b, q)
                            pe.wait_ge(kv_in[n % RING], 16 * UP * (n // RING + 1))
                            for j in range(UP):
                                ins = nc.tensor.matmul(bank[5 + b % 2][0:HT, :],
                                                       PT[:, q * UP + j, b * HT:(b + 1) * HT],
                                                       ring[:, n % RING, j * 512:(j + 1) * 512],
                                                       start=q == 0 and j == 0, stop=False)
                            ins.then_inc(kv_used, 1)
                        nc.tensor.matmul(bank[5 + b % 2][0:HT, :], PT[0:NS, NPAGE, b * HT:(b + 1) * HT],
                                         c.v[0:NS, STILE], start=False, stop=True).then_inc(s["pv_mm"], 1)
                        if b == 0 and g:
                            pe.wait_ge(s["ot"], g)
                        if b:
                            out_T(b - 1)
                    out_T(HB - 1)

            @block.vector
            def _(dve):
                V = nc.vector
                link = Link(dve, d_own)
                dve.wait_ge(s["c_in"], 16 * (TS + 8))
                dve.wait_ge(s["swap_in"], 32)
                qi = qiS[:].rearrange("d r par (k two) t -> d par two k r t", two=2)
                link(V.memset(qiS[:], 0.0))
                for k in range(4):
                    for half in range(2):
                        for i in range(2):
                            lo = HD * i
                            src = (c.qiT[:, :, SEQ:NT] if i == half else swapped[:])[lo:lo + HD, k]
                            link(V.tensor_copy(qi[lo:lo + HD, i, half, k],
                                               src.rearrange("d (r par t) -> d par r t", par=2, t=TS)[:, i]),
                                 s["q_ready"] if (k, half, i) == (3, 1, 1) else None)
                link(V.tensor_tensor(wx[:], c.small[0:NS, STILE, S_WI:S_WI + H].unsqueeze(2).to_broadcast([NS, H, TS]),
                                     tsel[:].unsqueeze(1).to_broadcast([NS, H, TS]), ALU.mult), s["wx"])
                dve.wait_ge(s["wv_mm"], 1)
                link(V.tensor_scalar(wv[:], bank[7][:, 0:2], H ** -0.5, None, ALU.mult))
                link(V.tensor_tensor(Wsel[:], wmask[:], wv[:].unsqueeze(2).to_broadcast([P, 2, NS]), ALU.mult),
                     s["w_ready"])
                for b in range(HB):
                    link(V.tensor_tensor(RB[:, b], relb[:].unsqueeze(2).to_broadcast([TS * NBUCKET, H, TS]),
                                         trow[:].unsqueeze(1).to_broadcast([TS * NBUCKET, H, TS]), ALU.mult),
                         s["rb"] if b == HB - 1 else None)
                link(V.memset(msk[:], 0.0))
                link(V.memset(Q[:], 0.0))
                for g in range(2):
                    for b in range(HB):
                        own = Q[:, g, b, :, b * HT:(b + 1) * HT].rearrange("p k (h t) -> p k h t", t=TS)
                        at = SEQ + (g * HB + b) * TS
                        for k in range(4):
                            link(V.tensor_tensor(own[:, k],
                                                 c.qT[:, k, at:at + TS].unsqueeze(1).to_broadcast([P, H, TS]),
                                                 hmask[:, k].unsqueeze(2).to_broadcast([P, H, TS]), ALU.mult),
                                 s["qblk"] if g and b == HB - 1 and k == 3 else None)
                for g in range(2):
                    link(V.reduce_sum(Qall[:, g], Q[:, g].rearrange("p b k n -> p k n b"), AX_X), s["qblk"])
                dve.wait_ge(s["sc_ready"], NKC + 1)
                new = sc[:, PAST:NKEY]
                link(V.tensor_tensor(new, new, c.lowS[:], ALU.mult))
                link(V.tensor_tensor(new, new, c.lowSneg[:], ALU.add))
                for _ in range(topk // 8):
                    link(V.max(m8[:], sc[:]))
                    link(V.match_replace(sc[:], m8[:], sc[:], PICKED))
                link(V.tensor_scalar(msk[0:NS], sc[:], -2.9e38, NOT_SELECTED, ALU.is_gt, ALU.mult), s["mask"])
                dve.wait_ge(s["logit"], 2 * (NKC + 1))
                for g in range(2):
                    for q in range(NKC + 1):
                        n = g * (NKC + 1) + q
                        dve.wait_ge(s["mask_mm"], n + 1)
                        w = 512 if q < NKC else NS
                        part = L[:, g, q * 512:q * 512 + w]
                        link(V.tensor_tensor(part, part, bank[1 + n % 2][:, 0:w], ALU.add), s["masked"])
                        link(V.reduce_max(mx[:, g, q:q + 1], part, AX_X))
                    link(V.reduce_max(ngm[:, g:g + 1], mx[:, g], AX_X))
                    link(V.tensor_scalar(ngm[:, g:g + 1], ngm[:, g:g + 1], -1.0, None, ALU.mult), s["max"])
                for g in range(2):
                    dve.wait_ge(s["exp"], 5 * (g + 1))
                    link(V.reduce_sum(dsum[:, g:g + 1], den[:, g], AX_X))
                    link(V.reciprocal(rden[:, g:g + 1], dsum[:, g:g + 1]))
                    link(V.tensor_scalar(L[:, g], L[:, g], rden[:, g:g + 1], None, ALU.mult), s["prob"])
                for g in range(2):
                    for b in range(HB):
                        n0 = g * HB + b
                        dve.wait_ge(s["pv_mm"], n0 + 1)
                        if n0 >= 2:
                            dve.wait_ge(s["ot_mm"], n0 - 1)
                        link(V.tensor_tensor(Om[:, b % 2], bank[5 + b % 2][0:HT, :], omask[:], ALU.mult), s["om"])


def layer_norm(c, link, r, mv, n, gb, out, pre, sqrt_done, count, done):
    V = c.nc.vector
    for q in range(2):
        link(V.bn_stats(mv[0:n, 6 * q:6 * q + 6], r[0:n, q * 512:(q + 1) * 512]))
    link(V.bn_aggr(mv[0:n, 12:14], mv[0:n, 0:12]))
    link(V.tensor_scalar(mv[0:n, 14:15], mv[0:n, 13:14], EPS, None, ALU.add), pre)
    link.eng.wait_ge(sqrt_done, count)
    link(V.reciprocal(mv[0:n, 15:16], mv[0:n, 14:15]))
    link(V.tensor_scalar(r[0:n, :], r[0:n, :], mv[0:n, 12:13], mv[0:n, 15:16], ALU.subtract, ALU.mult))
    link(V.tensor_tensor(r[0:n, :], r[0:n, :], gb[0:n, 0], ALU.mult))
    link(V.tensor_tensor(out[0:n, :], r[0:n, :], gb[0:n, 1], ALU.add), done)


def stage_mix(c):
    nc, A, bank = c.nc, c.A, c.bank
    with ExitStack() as es:
        def sb(name, shape, dt=F32):
            return es.enter_context(nc.sbuf_tensor(name, shape, dt))
        w = sb("w_out", [P, KD, D])
        x = sb("x_rows", [P, NTILE, D])
        r = sb("resid", [P, 2, D])
        mv = sb("mv", [P, 16])
        gb = sb("ln1", [P, 2, D])
        s = {n: c.sem("mix_" + n) for n in ("in", "mm", "res", "pre", "sqrt", "h", "tr_mm", "tr")}
        d_own = c.sem("mix_dve")
        w_in = [c.sem(f"w_out_in{k}") for k in range(KD)]
        with nc.Block() as block:
            @block.sync
            def _(sp):
                for k in range(KD):
                    sp.dma_start(w[:, k], A["w_out"][:, k]).then_inc(w_in[k], 16)
                sp.dma_start(x[:, 0:STILE], A["x_rows"][0:SEQ].rearrange("(t p) n -> p t n", p=P)).then_inc(s["in"], 16)
                sp.dma_start(x[0:NS, STILE], A["x_rows"][SEQ:NT]).then_inc(s["in"], 16)
                sp.dma_start(gb[:], A["ln1"].to_broadcast([P, 2, D])).then_inc(s["in"], 16)

            @block.tensor
            def _(pe):
                def trans(t):
                    n = rows(t)
                    pe.wait_ge(s["h"], t + 1)
                    if t:
                        pe.wait_ge(s["tr"], t)
                    for k in range(KD):
                        ins = nc.tensor.transpose(bank[4 + k // 4][:, (k % 4) * n:(k % 4 + 1) * n],
                                                  c.h[0:n, t, k * P:(k + 1) * P], c.ident[0:n, 0:n])
                    ins.then_inc(s["tr_mm"], 1)

                for t in range(NTILE):
                    if t >= 2:
                        pe.wait_ge(s["res"], t - 1)
                    for q in range(2):
                        for k in range(KD):
                            if t == 0 and q == 0:
                                pe.wait_ge(w_in[k], 16)
                            ins = nc.tensor.matmul(bank[2 * (t % 2) + q][0:rows(t), :], c.mixedT[:, k, cols(t)],
                                                   w[:, k, q * 512:(q + 1) * 512], start=k == 0, stop=k == KD - 1)
                    ins.then_inc(s["mm"], 1)
                    if t:
                        trans(t - 1)
                trans(STILE)

            @block.scalar
            def _(act):
                for t in range(NTILE):
                    n = rows(t)
                    act.wait_ge(s["pre"], t + 1)
                    nc.scalar.activation(mv[0:n, 14:15], mv[0:n, 14:15], ACT.Sqrt).then_inc(s["sqrt"], 1)
                    act.wait_ge(s["tr_mm"], t + 1)
                    nc.scalar.activation(c.hT[:, 0:4, cols(t)], bank[4][:, 0:4 * n].rearrange("p (k n) -> p k n", k=4),
                                         ACT.Copy)
                    nc.scalar.activation(c.hT[:, 4:8, cols(t)], bank[5][:, 0:4 * n].rearrange("p (k n) -> p k n", k=4),
                                         ACT.Copy).then_inc(s["tr"], 1)

            @block.vector
            def _(dve):
                V = nc.vector
                link = Link(dve, d_own)
                dve.wait_ge(s["in"], 48)
                for t in range(NTILE):
                    n = rows(t)
                    dve.wait_ge(s["mm"], t + 1)
                    for q in range(2):
                        cs = slice(q * 512, (q + 1) * 512)
                        link(V.scalar_tensor_tensor(r[0:n, t % 2, cs], x[0:n, t, cs], ALPHA,
                                                    bank[2 * (t % 2) + q][0:n, :], ALU.mult, ALU.add),
                             s["res"] if q else None)
                    layer_norm(c, link, r[:, t % 2], mv, n, gb, c.h[:, t], s["pre"], s["sqrt"], t + 1,
                               s["h"])


def stage_memory(c):
    nc, A, bank = c.nc, c.A, c.bank
    mkT, mv_ = c.mkT, c.mv
    with ExitStack() as es:
        def sb(name, shape, dt=F32):
            return es.enter_context(nc.sbuf_tensor(name, shape, dt))
        wcq = sb("w_cq", [P, KD, 512])
        wco = sb("w_co", [P, MH, D])
        mkS, mvS = sb("mkS", [P, 2, MH, MEM]), sb("mvS", [P, 2, 2, 512])
        q = sb("q_mem", [P, MH, NT])
        qm = sb("qm", [P, MH, NB, NS])
        Pm = sb("p_mem", [P, 2, MH, MEM])
        PT = sb("pT_mem", [P, MH, 2, P])
        oT = sb("oT_mem", [P, MH, P])
        mx, den, rden = sb("mx_m", [P, 2, MH]), sb("den_m", [P, 2, MH]), sb("rden_m", [P, MH])
        r = sb("resid2", [P, D])
        st = sb("mv2", [P, 16])
        gb = sb("ln2", [P, 2, D])
        names = ("wco", "q_mm", "q_ev", "qm", "log_mm", "max", "exp", "prob", "trp_mm", "pt",
                 "o_mm", "oT", "co_mm", "res", "pre", "sqrt", "h", "tr_mm", "tr", "ks0", "ks1", "vs0", "vs1", "vs_used",
                 "ks_used", "gb")
        s = {n: c.sem("mem_" + n) for n in names}
        wcq_in = [c.sem(f"wcq_in{h}") for h in range(MH)]
        d_own = c.sem("mem_dve")
        SCALE = MD ** -0.5
        ORDER = [0, STILE] + list(range(1, STILE))

        def logit_bank(t, h):
            if t < STILE:
                return bank[h // 2][:, (h % 2) * MEM:(h % 2 + 1) * MEM]
            return bank[h if h < 2 else h + 4][0:NS, 0:MEM]

        with nc.Block() as block:
            @block.sync
            def _(sp):
                for h in range(MH):
                    sp.dma_start(wcq[:, :, h * P:(h + 1) * P], A["w_cq"][:, :, h * P:(h + 1) * P]).then_inc(wcq_in[h], 16)
                sp.dma_start(wco[:], A["w_co"]).then_inc(s["wco"], 16)
                sp.dma_start(gb[:], A["ln2"].to_broadcast([P, 2, D])).then_inc(s["gb"], 16)
                for b in range(NB):
                    if b >= 2:
                        sp.wait_ge(s["ks_used"], b - 1)
                    sp.dma_start(mkS[:, b % 2], A["cmkT"][b]).then_inc(s[f"ks{b % 2}"], 16)
                for b in range(NB):
                    if b >= 2:
                        sp.wait_ge(s["vs_used"], b - 1)
                    sp.dma_start(mvS[:, b % 2], A["cmv"][b].rearrange("(k p) n -> p k n", p=P)).then_inc(s[f"vs{b % 2}"], 16)

            @block.tensor
            def _(pe):
                for h in range(MH):
                    pe.wait_ge(wcq_in[h], 16)
                    if h >= 2:
                        pe.wait_ge(s["q_ev"], h - 1)
                    for half in range(2):
                        for k in range(KD):
                            ins = nc.tensor.matmul(c.pair(h % 2)[:, half], wcq[:, k, h * P:(h + 1) * P],
                                                   c.hT[:, k, half * HALF:(half + 1) * HALF],
                                                   start=k == 0, stop=k == KD - 1)
                    ins.then_inc(s["q_mm"], 1)
                pe.wait_ge(s["q_ev"], MH)

                def logits(i):
                    t = ORDER[i]
                    if i:
                        pe.wait_ge(s["exp"], MH * i)
                    if t < STILE:
                        for h in range(MH):
                            ins = nc.tensor.matmul(logit_bank(t, h), q[:, h, cols(t)], mkT[:, h],
                                                   start=True, stop=True)
                    else:
                        pe.wait_ge(s["qm"], 1)
                        for b in range(NB):
                            pe.wait_ge(s[f"ks{b % 2}"], 16 * (b // 2 + 1))
                            for h in range(MH):
                                ins = nc.tensor.matmul(logit_bank(t, h), qm[:, h, b], mkS[:, b % 2, h],
                                                       start=b == 0, stop=b == NB - 1)
                            if b < NB - 1:
                                ins.then_inc(s["ks_used"], 1)
                    ins.then_inc(s["log_mm"], 1)

                def transposes(i):
                    t = ORDER[i]
                    n = rows(t)
                    pe.wait_ge(s["h"], i + 1)
                    if i == 0:
                        pe.wait_ge(s["exp"], 2 * MH)
                    for k in range(KD):
                        ins = nc.tensor.transpose(bank[(4, 7)[k // 4]][:, (k % 4) * n:(k % 4 + 1) * n],
                                                  c.h[0:n, t, k * P:(k + 1) * P], c.ident[0:n, 0:n])
                    ins.then_inc(s["tr_mm"], 1)

                logits(0)
                for i, t in enumerate(ORDER):
                    n = rows(t)
                    if i + 1 < NTILE:
                        logits(i + 1)
                    pe.wait_ge(s["prob"], i + 1)
                    if i:
                        pe.wait_ge(s["pt"], 2 * i)
                    for h in range(MH):
                        for m in range(2):
                            ins = nc.tensor.transpose(bank[2 + m][:, h * n:(h + 1) * n],
                                                      Pm[0:n, i % 2, h, m * P:(m + 1) * P], c.ident[0:n, 0:n])
                    ins.then_inc(s["trp_mm"], 1)
                    pe.wait_ge(s["pt"], 2 * (i + 1))
                    if i >= 2:
                        pe.wait_ge(s["tr"], i - 1)
                    if t < STILE:
                        for h in range(MH):
                            for m in range(2):
                                ins = nc.tensor.matmul(bank[4][:, h * P:(h + 1) * P], mv_[:, m, h * P:(h + 1) * P],
                                                       PT[:, h, m, 0:n], start=m == 0, stop=m == 1)
                    else:
                        for b in range(NB):
                            pe.wait_ge(s[f"vs{b % 2}"], 16 * (b // 2 + 1))
                            for h in range(MH):
                                for m in range(2):
                                    ins = nc.tensor.matmul(bank[4][:, h * n + b * TS:h * n + (b + 1) * TS],
                                                           mvS[:, b % 2, m, h * P:(h + 1) * P],
                                                           PT[:, h, m, b * TS:(b + 1) * TS], start=m == 0, stop=m == 1)
                            if b < NB - 1:
                                ins.then_inc(s["vs_used"], 1)
                    ins.then_inc(s["o_mm"], 1)
                    pe.wait_ge(s["oT"], i + 1)
                    if i == 0:
                        pe.wait_ge(s["wco"], 16)
                        pe.wait_ge(s["exp"], 2 * MH)
                    else:
                        pe.wait_ge(s["res"], i)
                    for half in range(2):
                        for h in range(MH):
                            ins = nc.tensor.matmul(bank[5 + half][0:n, :], oT[:, h, 0:n],
                                                   wco[:, h, half * 512:(half + 1) * 512], start=h == 0, stop=h == MH - 1)
                    ins.then_inc(s["co_mm"], 1)
                    if i:
                        transposes(i - 1)
                pe.wait_ge(s["tr"], NTILE - 1)
                transposes(NTILE - 1)

            @block.scalar
            def _(act):
                for h in range(MH):
                    act.wait_ge(s["q_mm"], h + 1)
                    nc.scalar.activation(q[:, h].rearrange("p (c t) -> p c t", c=2), c.pair(h % 2),
                                         ACT.Copy).then_inc(s["q_ev"], 1)

                def exps(i):
                    n = rows(ORDER[i])
                    act.wait_ge(s["max"], i + 1)
                    if i >= 2:
                        act.wait_ge(s["trp_mm"], i - 1)
                    for h in range(MH):
                        nc.scalar.activation(Pm[0:n, i % 2, h], logit_bank(ORDER[i], h), ACT.Exp,
                                             bias=mx[0:n, i % 2, h:h + 1], scale=SCALE,
                                             accum_out=den[0:n, i % 2, h:h + 1]).then_inc(s["exp"], 1)

                def store_hT(i):
                    n = rows(ORDER[i])
                    act.wait_ge(s["tr_mm"], i + 1)
                    for half in range(2):
                        ins = nc.scalar.activation(c.hT[:, 4 * half:4 * half + 4, cols(ORDER[i])],
                                                   bank[(4, 7)[half]][:, 0:4 * n].rearrange("p (k n) -> p k n", k=4),
                                                   ACT.Copy)
                    ins.then_inc(s["tr"], 1)

                exps(0)
                for i, t in enumerate(ORDER):
                    n = rows(t)
                    if i + 1 < NTILE:
                        exps(i + 1)
                    act.wait_ge(s["trp_mm"], i + 1)
                    if i:
                        act.wait_ge(s["o_mm"], i)
                    for m in range(2):
                        nc.scalar.activation(PT[:, :, m, 0:n], bank[2 + m][:, 0:MH * n].rearrange(
                            "p (h n) -> p h n", h=MH), ACT.Copy).then_inc(s["pt"], 1)
                    act.wait_ge(s["o_mm"], i + 1)
                    if i:
                        act.wait_ge(s["co_mm"], i)
                    nc.scalar.activation(oT[:, :, 0:n], bank[4][:, 0:MH * n].rearrange("p (h n) -> p h n", h=MH),
                                         ACT.Copy).then_inc(s["oT"], 1)
                    if i:
                        store_hT(i - 1)
                    act.wait_ge(s["pre"], i + 1)
                    nc.scalar.activation(st[0:n, 14:15], st[0:n, 14:15], ACT.Sqrt).then_inc(s["sqrt"], 1)
                store_hT(NTILE - 1)

            @block.vector
            def _(dve):
                V = nc.vector
                link = Link(dve, d_own)
                dve.wait_ge(s["q_ev"], MH)

                def softmax(i):
                    t = ORDER[i]
                    n, m, Pt = rows(t), mx[:, i % 2], Pm[:, i % 2]
                    dve.wait_ge(s["log_mm"], i + 1)
                    if t < STILE:
                        for half in range(2):
                            link(V.reduce_max(m[:, 2 * half:2 * half + 2],
                                              bank[half][:].rearrange("p (h m) -> p h m", h=2), AX_X))
                    else:
                        for h in range(MH):
                            link(V.reduce_max(m[0:n, h:h + 1], logit_bank(t, h), AX_X))
                    link(V.tensor_scalar(m[0:n, :], m[0:n, :], -SCALE, None, ALU.mult), s["max"])
                    dve.wait_ge(s["exp"], MH * (i + 1))
                    link(V.reciprocal(rden[0:n, :], den[0:n, i % 2]))
                    link(V.tensor_tensor(Pt[0:n], Pt[0:n], rden[0:n, :].unsqueeze(2).to_broadcast([n, MH, MEM]),
                                         ALU.mult), s["prob"])

                softmax(0)
                for h in range(MH):
                    link(V.tensor_tensor(qm[:, h], q[:, h, SEQ:NT].unsqueeze(1).to_broadcast([P, NB, NS]), c.bcol[:],
                                         ALU.mult), s["qm"] if h == MH - 1 else None)
                dve.wait_ge(s["gb"], 16)
                for i, t in enumerate(ORDER):
                    n = rows(t)
                    if i + 1 < NTILE:
                        softmax(i + 1)
                    dve.wait_ge(s["co_mm"], i + 1)
                    for half in range(2):
                        cs = slice(half * 512, (half + 1) * 512)
                        link(V.scalar_tensor_tensor(r[0:n, cs], c.h[0:n, t, cs], ALPHA, bank[5 + half][0:n, :],
                                                    ALU.mult, ALU.add), s["res"] if half else None)
                    layer_norm(c, link, r, st, n, gb, c.h[:, t], s["pre"], s["sqrt"], i + 1, s["h"])


def stage_scores(c):
    nc, A, bank = c.nc, c.A, c.bank
    NJ = 2 * PH
    RING = 3
    S, hH, hL = c.S, c.hH, c.hL
    with ExitStack() as es:
        def sb(name, shape, dt=F32):
            return es.enter_context(nc.sbuf_tensor(name, shape, dt))
        wq = sb("wq", [P, RING, KD, P])
        sk = sb("subkeys", [P, NJ, NKEYS])
        qp = sb("qp", [P, 2, NT])
        sk_in, q_mm, q_ev = c.sem("sk_in"), c.sem("rq_mm"), c.sem("rq_ev")
        wq_in = [c.sem(f"wq_in{i}") for i in range(RING)]
        s_mm, s_ev, zero = c.sem("rs_mm"), c.sem("rs_ev"), c.sem("r_zero")
        h_split = c.sem("h_split")

        with nc.Block() as block:
            @block.sync
            def _(sp):
                for j in range(NJ):
                    if j >= RING:
                        sp.wait_ge(q_mm, j - RING + 1)
                    sp.dma_start(wq[:, j % RING], A["wq_blk"][j]).then_inc(wq_in[j % RING], 16)
                    if j == 1:
                        sp.dma_start(sk[:], A["subkeysT"]).then_inc(sk_in, 16)

            @block.tensor
            def _(pe):
                def scores(j):
                    pe.wait_ge(q_ev, j + 1)
                    if j == 0:
                        pe.wait_ge(sk_in, 16)
                    if j >= 2:
                        pe.wait_ge(s_ev, 2 * (j - 1))
                    for t in range(NTILE):
                        dst = bank[4 + j % 2][:, t * P:(t + 1) * P] if t < STILE else bank[6 + j % 2][0:NS, 0:P]
                        ins = nc.tensor.matmul(dst, qp[:, j % 2, cols(t)], sk[:, j], start=True, stop=True)
                    ins.then_inc(s_mm, 1)

                for j in range(NJ):
                    pe.wait_ge(wq_in[j % RING], 16 * (j // RING + 1))
                    if j >= 2:
                        pe.wait_ge(q_ev, j - 1)
                    for q in range(2):
                        for k in range(KD):
                            ins = nc.tensor.matmul(c.pair(j % 2)[:, q], wq[:, j % RING, k],
                                                   c.hT[:, k, q * HALF:(q + 1) * HALF],
                                                   start=k == 0, stop=k == KD - 1)
                    ins.then_inc(q_mm, 1)
                    if j:
                        scores(j - 1)
                scores(NJ - 1)

            @block.scalar
            def _(act):
                def scores(j):
                    act.wait_ge(s_mm, j + 1)
                    if j == 0:
                        act.wait_ge(zero, 1)
                    nc.scalar.activation(S[:, 0:STILE, j * NKEYS:(j + 1) * NKEYS],
                                         bank[4 + j % 2][:].rearrange("p (t n) -> p t n", t=STILE),
                                         ACT.Copy).then_inc(s_ev, 1)
                    nc.scalar.activation(S[0:NS, STILE, j * NKEYS:(j + 1) * NKEYS], bank[6 + j % 2][0:NS, 0:P],
                                         ACT.Copy).then_inc(s_ev, 1)

                for j in range(NJ):
                    act.wait_ge(q_mm, j + 1)
                    if j >= 2:
                        act.wait_ge(s_mm, j - 1)
                    nc.scalar.activation(qp[:, j % 2].rearrange("p (c t) -> p c t", c=2), c.pair(j % 2),
                                         ACT.Copy).then_inc(q_ev, 1)
                    if j:
                        scores(j - 1)
                scores(NJ - 1)

            @block.vector
            def _(dve):
                V = nc.vector
                V.memset(S[:, STILE], 0.0).then_inc(zero, 1)
                for k in range(KD):
                    V.tensor_copy(hH[:, k], c.hT[:, k]).then_inc(h_split, 1)
                    dve.wait_ge(h_split, 2 * k + 1)
                    V.tensor_tensor(hL[:, k], c.hT[:, k], hH[:, k].bitcast(F32), ALU.subtract).then_inc(h_split, 1)
                dve.wait_ge(h_split, 2 * KD)


GS = 4
NG = NKEYS // GS
TB = NS
NTB = NT // TB
GCOL = GS * NT
RING_START = 2
UNIT = 4
C_STEP, U_STEP = 2, 4
STEPS = TB // (UNIT * U_STEP)
LEAD = 24


def stage_activate(c):
    nc, A, bank = c.nc, c.A, c.bank
    R = RING_START
    S, hH, hL = c.S, c.hH, c.hL
    with ExitStack() as es:
        def sb(name, shape, dt=F32):
            return es.enter_context(nc.sbuf_tensor(name, shape, dt))
        u, uH, uL = sb("u_raw", [P, 2, KD, P]), sb("uH", [P, 2, KD, P], F32R), sb("uL", [P, 2, KD, P], F32R)
        a = sb("acts", [P, 2, NT])
        slots = sb("slots", [P, 3, NT])
        work = sb("work", [P, 2, NKEYS])
        v16, i16, i16f = sb("v16", [P, 2, TOPK]), sb("i16", [P, 2, TOPK], U32), sb("i16f", [P, 2, TOPK])
        cand = sb("cand", [P, TOPK * TOPK])
        gi, ab, abf = sb("gi", [P, TOPK], U32), sb("ab", [P, 2, TOPK], U32), sb("abf", [P, 2, TOPK])
        eq = sb("eq", [P, TOPK, TOPK])
        head = sb("head_slots", [P, 3, TOPK])
        res, gsum = sb("res", [P, 3, PH * TOPK]), sb("gsum", [P, PH])
        hot_i, hot_j, raw_j = (sb(n, [P, 2, UNIT, P]) for n in ("hot_i", "hot_j", "raw_j"))
        G = sb("Gtile", [P, 2, NKEYS, TB])
        u_split, u_mm, u_act, g_mm, g_ev = (c.sem(n) for n in ("u_split", "u_mm", "u_act", "g_mm", "g_ev"))
        a_stored = [c.sem(f"a_stored{i}") for i in range(2)]
        G_stored = [c.sem(f"G_stored{i}") for i in range(2)]
        u_in = [c.sem(f"u_in{i}") for i in range(2)]
        u_hi, d_own = c.sem("u_hi"), c.sem("act_dve")
        hi_ready, hj_ready, rj_ready = c.sem("hot_i"), c.sem("hot_j"), c.sem("raw_j")
        g_pre, g_exp, res_ready, res_mm, slots_ready = (c.sem("r_" + n) for n in (
            "g_pre", "g_exp", "res", "res_mm", "slots"))

        def steps(eng, columns, tile_start=None, block_start=None, unit=None, block_end=None, between=None):
            nothing = lambda *_: None
            only_units = columns is None
            columns, tile_start, block_start, unit, block_end, between = (
                f or nothing for f in (columns, tile_start, block_start, unit, block_end, between))

            def step(n, n_unit, at, p, half_done):
                for q in range(C_STEP):
                    columns(n + q, q, False)
                    for k in range(U_STEP // C_STEP):
                        i = q * (U_STEP // C_STEP) + k
                        unit(n_unit + i, at + i, i % 2, p)
                    if q == 0:
                        half_done()

            if not only_units:
                with eng.Fori(0, LEAD // C_STEP) as r:
                    for q in range(C_STEP):
                        columns(r * C_STEP + q, q, False)
            PER = STEPS * C_STEP
            TBLK = P // TB
            for t in range(STILE):
                tile_start(t)
                with eng.Fori(0, TBLK // 2) as r:
                    block_start(None, None)
                    for p in range(2):
                        blk = r * 2 + (t * TBLK + p)
                        block_start(blk, p)
                        for st in range(STEPS):
                            step(r * (2 * PER) + (LEAD + (t * TBLK + p) * PER + st * C_STEP),
                                 r * (2 * STEPS * U_STEP) + ((t * TBLK + p) * STEPS + st) * U_STEP,
                                 st * U_STEP, p,
                                 lambda: between(t, r * (2 * STEPS) + (p * STEPS + st)))
                        block_end(blk, p)
            tile_start(STILE)
            block_start(STILE * TBLK, 0)
            for st in range(STEPS):
                step(LEAD + STILE * TBLK * PER + st * C_STEP, (STILE * TBLK * STEPS + st) * U_STEP,
                     st * U_STEP, 0, lambda: None)
            block_end(STILE * TBLK, 0)
            if only_units:
                return
            first = LEAD + NTB * PER
            with eng.Fori(0, (NKEYS - first) // C_STEP - 1) as r:
                for q in range(C_STEP):
                    columns(r * C_STEP + (first + q), q, False)
            for q in range(C_STEP):
                columns(NKEYS - C_STEP + q, q, q == C_STEP - 1)

        with nc.Block() as block:
            @block.sync
            def _(sp):
                def columns(n, q, last):
                    sp.wait_ge(u_split, n + 1)
                    src = A["uT"][bass.ds(n, 1)] if not isinstance(n, int) else A["uT"][n:n + 1]
                    sp.dma_start(u[:, q], src.rearrange("a p k n -> p (a k) n")).then_inc(u_in[q], 16)
                steps(sp, columns)

            @block.gpsimd
            def _(pool):
                pool.sem_inc(u_split, R)

                def low_u(n, q):
                    pool.wait_ge(u_hi, n + 1)
                    nc.gpsimd.tensor_tensor(uL[:, q], u[:, q], uH[:, q].bitcast(F32),
                                            ALU.subtract).then_inc(u_split, 1)

                low_u(0, 0)

                def columns(n, q, last):
                    if not last:
                        low_u(n + 1, 1 - q)

                def unit(n, at, slot, p):
                    pool.wait_ge(rj_ready, n + 1)
                    gates = slots[:, 2, bass.ds(n * UNIT, UNIT)] if not isinstance(n, int) else \
                        slots[:, 2, n * UNIT:(n + 1) * UNIT]
                    nc.gpsimd.tensor_tensor(hot_j[:, slot], raw_j[:, slot],
                                            gates.unsqueeze(2).to_broadcast([P, UNIT, P]),
                                            ALU.mult).then_inc(hj_ready, 1)
                steps(pool, columns, unit=unit)

            @block.scalar
            def _(act):
                act.sem_inc(u_act, R)
                act.sem_inc(g_ev, R)
                for i in range(2):
                    act.sem_inc(a_stored[i], 16)
                    act.sem_inc(G_stored[i], 16)

                def high_u(n, q):
                    act.wait_ge(u_in[q], (n - q) * 8 + 16)
                    act.wait_ge(u_mm, n + 1)
                    nc.scalar.activation(uH[:, q], u[:, q], ACT.Copy).then_inc(u_hi, 1)

                high_u(0, 0)

                def columns(n, q, last):
                    if not last:
                        high_u(n + 1, 1 - q)
                    act.wait_ge(u_mm, n + 1 + R)
                    act.wait_ge(a_stored[q], (n - q) * 8 + 16)
                    nc.scalar.activation(a[:, q].rearrange("p (c t) -> p c t", c=2), c.pair(q),
                                         ACT.Gelu_apprx_tanh).then_inc(u_act, 1)
                    act.wait_ge(u_act, n + 1 + R)
                    dst = A["acts"][bass.ds(n, 1)] if not isinstance(n, int) else A["acts"][n:n + 1]
                    act.dma_start(dst.rearrange("a p t -> p (a t)"), a[:, q]).then_inc(a_stored[q], 16)

                def tile_start(t):
                    act.wait_ge(g_pre, t + 1)
                    nc.scalar.activation(res[:, 2], res[:, 2], ACT.Exp).then_inc(g_exp, 1)
                    act.wait_ge(res_mm, t + 1)
                    nc.scalar.activation(slots[:, :, cols(t)],
                                         bank[6][:, 0:3 * P].rearrange("p (q n) -> p q n", q=3)[:, :, 0:rows(t)],
                                         ACT.Copy).then_inc(slots_ready, 1)

                def block_start(blk, p):
                    if blk is not None:
                        act.wait_ge(G_stored[p], (blk - p) * 8 + 16)

                def unit(n, at, slot, p):
                    act.wait_ge(g_mm, n + 1 + R)
                    nc.scalar.activation(G[:, p, :, at * UNIT:(at + 1) * UNIT].rearrange("p j t -> p t j"),
                                         bank[4 + slot][:].rearrange("p (t j) -> p t j", t=UNIT),
                                         ACT.Copy).then_inc(g_ev, 1)

                def block_end(blk, p):
                    act.wait_ge(g_ev, (blk + 1) * (TB // UNIT) + R)
                    dst = A["gates"][:, :, bass.ds(blk * (GS * TB), GS * TB)] if not isinstance(blk, int) else \
                        A["gates"][:, :, blk * GS * TB:(blk + 1) * GS * TB]
                    act.dma_start(dst.rearrange("g p n -> p g n"),
                                  G[:, p].rearrange("p (g j) t -> p g (j t)", j=GS)).then_inc(G_stored[p], 16)

                steps(act, columns, tile_start, block_start, unit, block_end)
                for i in range(2):
                    act.wait_ge(a_stored[i], 16 * (NKEYS // 2 + 1))
                    act.wait_ge(G_stored[i], 16 * ((NTB + 1 - i) // 2 + 1))

            @block.vector
            def _(dve):
                V = nc.vector
                link = Link(dve, d_own)

                def restart():
                    dve.sem_clear(d_own)
                    link.count.clear()

                def top16(val, idx, x):
                    link(V.max(val[:, 0:8], x))
                    link(V.max_index(idx[:, 0:8], val[:, 0:8], x))
                    link(V.match_replace(x, val[:, 0:8], x, PICKED))
                    link(V.max(val[:, 8:16], x))
                    link(V.max_index(idx[:, 8:16], val[:, 8:16], x))

                def route_head(t, h):
                    link(V.tensor_copy(work[:].rearrange("p j n -> p (j n)"),
                                       S[:, t, bass.ds(h * (2 * NKEYS), 2 * NKEYS)]))
                    for q in range(2):
                        top16(v16[:, q], i16[:, q], work[:, q])
                    link(V.tensor_tensor(cand[:].rearrange("p (a b) -> p a b", a=TOPK),
                                         v16[:, 0].unsqueeze(2).to_broadcast([P, TOPK, TOPK]),
                                         v16[:, 1].unsqueeze(1).to_broadcast([P, TOPK, TOPK]), ALU.add))
                    top16(head[:, 2], gi[:], cand[:])
                    link(V.tensor_scalar(ab[:, 0], gi[:], 4, None, ALU.logical_shift_right))
                    link(V.tensor_scalar(ab[:, 1], gi[:], TOPK - 1, None, ALU.bitwise_and))
                    link(V.tensor_copy(abf[:], ab[:]))
                    link(V.tensor_copy(i16f[:], i16[:]))
                    for q in range(2):
                        link(V.tensor_tensor(eq[:], abf[:, q].unsqueeze(2).to_broadcast([P, TOPK, TOPK]),
                                             c.iota[:, 0:TOPK].unsqueeze(1).to_broadcast([P, TOPK, TOPK]),
                                             ALU.is_equal))
                        link(V.tensor_tensor(eq[:], eq[:], i16f[:, q].unsqueeze(1).to_broadcast([P, TOPK, TOPK]),
                                             ALU.mult))
                        link(V.reduce_sum(head[:, q], eq[:], AX_X))
                    link(V.tensor_copy(res[:, :, bass.ds(h * TOPK, TOPK)], head[:]))

                def finish_tile(t):
                    restart()
                    gm = res[:, 2].rearrange("p (h s) -> p h s", h=PH)
                    link(V.reduce_max(gsum[:], gm, AX_X))
                    V.tensor_tensor(gm, gm, gsum[:].unsqueeze(2).to_broadcast([P, PH, TOPK]),
                                    ALU.subtract).then_inc(g_pre, 1)
                    dve.wait_ge(g_exp, t + 1)
                    link(V.reduce_sum(gsum[:], gm, AX_X))
                    link(V.reciprocal(gsum[:], gsum[:]))
                    V.tensor_tensor(gm, gm, gsum[:].unsqueeze(2).to_broadcast([P, PH, TOPK]),
                                    ALU.mult).then_inc(res_ready, 1)
                    dve.wait_ge(slots_ready, t + 1)

                with dve.Fori(0, PH) as h:
                    restart()
                    route_head(0, h)
                finish_tile(0)

                def unit(n, at, slot, p):
                    dve.wait_ge(g_mm, n + 1)
                    for q, (hot, ready) in enumerate(((raw_j, rj_ready), (hot_i, hi_ready))):
                        src = slots[:, 1 - q, bass.ds(n * UNIT, UNIT)] if not isinstance(n, int) else \
                            slots[:, 1 - q, n * UNIT:(n + 1) * UNIT]
                        V.tensor_tensor(hot[:, slot], c.iota[:].unsqueeze(1).to_broadcast([P, UNIT, P]),
                                        src.unsqueeze(2).to_broadcast([P, UNIT, P]), ALU.is_equal).then_inc(ready, 1)

                def tile_start(t):
                    if t:
                        finish_tile(t)

                def block_start(blk, p):
                    if blk is None:
                        restart()

                def between(t, h):
                    route_head(t + 1, h)

                steps(dve, None, tile_start, block_start, unit, between=between)

            @block.tensor
            def _(pe):
                pe.sem_inc(u_mm, R)
                pe.sem_inc(g_mm, R)

                def columns(n, q, last):
                    pe.wait_ge(u_split, n + 1 + R)
                    pe.wait_ge(u_act, n + 1)
                    for half in range(2):
                        parts = [(w, x, k) for k in range(KD) for w, x in ((uH, hH), (uH, hL), (uL, hH))]
                        for m, (w, x, k) in enumerate(parts):
                            ins = nc.tensor.matmul(c.pair(q)[:, half], w[:, q, k],
                                                   x[:, k, half * HALF:(half + 1) * HALF], start=m == 0,
                                                   stop=m == len(parts) - 1)
                    ins.then_inc(u_mm, 1)

                def tile_start(t):
                    pe.wait_ge(res_ready, t + 1)
                    for q in range(3):
                        ins = nc.tensor.transpose(bank[6][:, q * P:(q + 1) * P], res[:, q], c.ident[:])
                    ins.then_inc(res_mm, 1)

                def unit(n, at, slot, p):
                    pe.wait_ge(hi_ready, n + 1)
                    pe.wait_ge(hj_ready, n + 1)
                    pe.wait_ge(g_ev, n + 1)
                    for q in range(UNIT):
                        ins = nc.tensor.matmul(bank[4 + slot][:, q * P:(q + 1) * P], hot_i[:, slot, q],
                                               hot_j[:, slot, q], start=True, stop=True)
                    ins.then_inc(g_mm, 1)

                steps(pe, columns, tile_start, unit=unit)


def stage_experts(c):
    nc, A, bank = c.nc, c.A, c.bank
    NACC = 4
    with ExitStack() as es:
        def sb(name, shape, dt=F32):
            return es.enter_context(nc.sbuf_tensor(name, shape, dt))
        v, vH, vL = sb("v_raw", [P, 2, D]), sb("vH", [P, 2, GS, D], F32R), sb("vL", [P, 2, GS, D], F32R)
        G, a = sb("G", [P, 2, GCOL]), sb("a_group", [P, 2, GS, NT])
        wf = sb("wf", [P, 2, NT])
        wH, wL = sb("wH", [P, 2, GS, NT], F32R), sb("wL", [P, 2, GS, NT], F32R)
        y = c.hT
        d_own = c.sem("exp_dve")
        v_in = [c.sem(f"v_in{i}") for i in range(2)]
        G_in = [c.sem(f"G_in{i}", True) for i in range(2)]
        w_done, v_split, y_added = (c.sem(n) for n in ("w_done", "v_split", "y_added"))
        v_hi, v_mm = c.sem("v_hi"), c.sem("v_mm")
        R = RING_START

        def loop(eng, body):
            with eng.Fori(0, NG // 2 - 1) as r:
                for p in range(2):
                    body(r * 2 + p, p, False)
            for p in range(2):
                body(NG - 2 + p, p, True)

        with nc.Block() as block:
            @block.sync
            def _(sp):
                def body(g, p, last):
                    for j in range(GS):
                        n = g * GS + j
                        sp.wait_ge(v_split, n + 1)
                        src = A["v_rows"][bass.ds(n, 1)] if not isinstance(n, int) else A["v_rows"][n:n + 1]
                        sp.dma_start(v[:, j % 2], src.rearrange("a p n -> p (a n)")).then_inc(v_in[j % 2], 16)
                loop(sp, body)

            @block.gpsimd
            def _(pool):
                for g in range(2):
                    pool.dma_start(G[:, g], A["gates"][g]).then_inc(G_in[g], 16)
                    pool.dma_start(a[:, g], A["acts"][g * GS:(g + 1) * GS].rearrange("j p t -> p j t")
                                   ).then_inc(G_in[g], 16)

                def body(g, p, last):
                    if not last:
                        pool.wait_ge(w_done, (g + 1) * GS + R)
                        pool.dma_start(G[:, p], A["gates"][bass.ds(g + 2, 1)].rearrange("a p n -> p (a n)")
                                       ).then_inc(G_in[p], 16)
                        pool.dma_start(a[:, p], A["acts"][bass.ds(g * GS + 2 * GS, GS)].rearrange("j p t -> p j t")
                                       ).then_inc(G_in[p], 16)
                loop(pool, body)

            @block.scalar
            def _(act):
                def body(g, p, last):
                    for j in range(GS):
                        n = g * GS + j
                        act.wait_ge(v_in[j % 2], (n - j % 2) * 8 + 16)
                        act.wait_ge(v_mm, g * KD + 1)
                        nc.scalar.activation(vH[:, p, j], v[:, j % 2], ACT.Copy).then_inc(v_hi, 1)
                loop(act, body)

            @block.vector
            def _(dve):
                V = nc.vector
                for sem in (v_split, w_done):
                    dve.sem_inc(sem, R)
                dve.sem_inc(y_added, NACC)
                V.memset(y[:], 0.0).then_inc(d_own, 1)
                dve.wait_ge(d_own, 1)

                def prepare(g, p, j):
                    n = g * GS + j

                    def own(ins, k):
                        ins.then_inc(d_own, 1)
                        dve.wait_ge(d_own, n * 2 + k + 1)
                    if j == 0:
                        dve.wait_ge(G_in[p], (g - p) * 16 + 32)
                    own(V.tensor_tensor(wf[:, j % 2].rearrange("p (b t) -> p b t", b=NTB),
                                        a[:, p, j].rearrange("p (b t) -> p b t", b=NTB),
                                        G[:, p].rearrange("p (b j t) -> p b j t", b=NTB, j=GS)[:, :, j],
                                        ALU.mult), 1)
                    own(V.tensor_copy(wH[:, p, j], wf[:, j % 2]), 2)
                    V.tensor_tensor(wL[:, p, j], wf[:, j % 2], wH[:, p, j].bitcast(F32),
                                    ALU.subtract).then_inc(w_done, 1)
                    dve.wait_ge(v_hi, n + 1)
                    V.tensor_tensor(vL[:, p, j], v[:, j % 2], vH[:, p, j].bitcast(F32),
                                    ALU.subtract).then_inc(v_split, 1)

                for j in range(GS):
                    prepare(0, 0, j)

                def body(g, p, last):
                    for k in range(KD):
                        dve.wait_ge(v_mm, g * KD + k + 1 + KD + 1)
                        yk = y[:, k].rearrange("p (c t) -> p c t", c=2)
                        V.tensor_tensor(yk, yk, c.pair(k % NACC), ALU.add).then_inc(y_added, 1)
                        if k % 2 == 1 and not (last and p == 1):
                            prepare(g + 1, 1 - p, k // 2)
                loop(dve, body)

            @block.tensor
            def _(pe):
                pe.sem_inc(v_mm, KD + 1)

                def body(g, p, last):
                    for k in range(KD):
                        pe.wait_ge(y_added, g * KD + k + 1)
                        for q in range(2):
                            parts = [(w, x, j) for j in range(GS) for w, x in ((vH, wH), (vH, wL), (vL, wH))]
                            for m, (w, x, j) in enumerate(parts):
                                if k == 0 and q == 0 and m % 3 == 0:
                                    pe.wait_ge(v_split, g * GS + j + 1 + R)
                                    pe.wait_ge(w_done, g * GS + j + 1 + R)
                                ins = nc.tensor.matmul(c.pair(k % NACC)[:, q], w[:, p, j, k * P:(k + 1) * P],
                                                       x[:, p, j, q * HALF:(q + 1) * HALF], start=m == 0,
                                                       stop=m == len(parts) - 1)
                        ins.then_inc(v_mm, 1)
                loop(pe, body)


def stage_finish(c):
    nc, A, bank = c.nc, c.A, c.bank
    with ExitStack() as es:
        def sb(name, shape, dt=F32):
            return es.enter_context(nc.sbuf_tensor(name, shape, dt))
        r = sb("resid3", [P, D])
        out = sb("yout", [P, NTILE, D])
        st = sb("mv3", [P, 16])
        gb = sb("ln3", [P, 2, D])
        s = {n: c.sem("fin_" + n) for n in ("gb", "mm", "res", "pre", "sqrt", "out", "store")}
        d_own = c.sem("fin_dve")
        with nc.Block() as block:
            @block.tensor
            def _(pe):
                for t in range(NTILE):
                    n = rows(t)
                    if t >= 2:
                        pe.wait_ge(s["res"], t - 1)
                    for k in range(KD):
                        ins = nc.tensor.transpose(bank[2 * (t % 2) + k // 4][0:n, (k % 4) * P:(k % 4 + 1) * P],
                                                  c.hT[:, k, cols(t)], c.ident[:])
                    ins.then_inc(s["mm"], 1)

            @block.scalar
            def _(act):
                for t in range(NTILE):
                    n = rows(t)
                    act.wait_ge(s["pre"], t + 1)
                    nc.scalar.activation(st[0:n, 14:15], st[0:n, 14:15], ACT.Sqrt).then_inc(s["sqrt"], 1)

            @block.vector
            def _(dve):
                link = Link(dve, d_own)
                dve.wait_ge(s["gb"], 16)
                for t in range(NTILE):
                    n = rows(t)
                    dve.wait_ge(s["mm"], t + 1)
                    for q in range(2):
                        cs = slice(q * 512, (q + 1) * 512)
                        link(nc.vector.scalar_tensor_tensor(r[0:n, cs], c.h[0:n, t, cs], ALPHA,
                                                            bank[2 * (t % 2) + q][0:n, :], ALU.mult, ALU.add),
                             s["res"] if q else None)
                    layer_norm(c, link, r, st, n, gb, out[:, t], s["pre"], s["sqrt"], t + 1, s["out"])

            @block.sync
            def _(sp):
                sp.dma_start(gb[:], A["ln3"].to_broadcast([P, 2, D])).then_inc(s["gb"], 16)
                for t in range(NTILE):
                    sp.wait_ge(s["out"], t + 1)
                    dst = A["y_p"][t * P:(t + 1) * P] if t < STILE else A["y_s"]
                    sp.dma_start(dst, out[0:rows(t), t]).then_inc(s["store"], 16)
                sp.wait_ge(s["store"], 16 * NTILE)


def stage_constants(c):
    nc, A = c.nc, c.A
    names = list(c.const)
    const_in = c.sem("const_in")
    with nc.Block() as block:
        @block.sync
        def _(sp):
            for name in names:
                sp.dma_start(c.const[name][:], A["k_" + name]).then_inc(const_in, 16)
            sp.dma_start(c.vecs[:], A["vecs"].to_broadcast([P, NVEC])).then_inc(const_in, 16)
            sp.wait_ge(const_in, 16 * (len(names) + 1))


def build(nc, A, upto=99, dump=None):
    c = Ctx(nc, A)
    with c.stack, ExitStack() as right:
        c.ident = c.keep(c.stack, "ident", [P, P])
        c.iota = c.keep(c.stack, "iota", [P, P])
        c.tri = c.keep(c.stack, "tri", [P, P])
        c.low = c.keep(c.stack, "low", [P, P])
        c.lowneg = c.keep(c.stack, "lowneg", [P, P])
        c.ones = c.keep(c.stack, "ones", [P, P])
        c.triS = c.keep(c.stack, "triS", [NS, NS])
        c.lowS = c.keep(c.stack, "lowS", [NS, NS])
        c.lowSneg = c.keep(c.stack, "lowSneg", [NS, NS])
        c.onesS = c.keep(c.stack, "onesS", [NS, NS])
        c.bsel = c.keep(c.stack, "bsel", [NS, NB])
        c.bcol = c.keep(c.stack, "bcol", [P, NB, NS])
        c.vecs = c.keep(c.stack, "vecs", [P, NVEC])
        c.const = {"ident": c.ident, "iota": c.iota, "tri": c.tri, "low": c.low, "lowneg": c.lowneg, "ones": c.ones, "triS": c.triS, "lowS": c.lowS, "lowSneg": c.lowSneg, "onesS": c.onesS, "bsel": c.bsel, "bcol": c.bcol}
        stage_constants(c)
        memory = ExitStack()
        c.stack.enter_context(memory)
        c.mkT, c.mv = c.keep(memory, "mkT", [P, MH, MEM]), c.keep(memory, "mv_rows", [P, 2, 512])
        with ExitStack() as mid:
            c.mixedT = c.keep(mid, "mixedT", [P, KD, NT])
            with ExitStack() as att:
                c.qT = c.keep(att, "qT", [P, 4, NT])
                c.kT = c.keep(att, "kT", [P, 4, NT])
                c.qiT = c.keep(att, "qiT", [P, 4, NT])
                c.kiT = c.keep(att, "kiT", [P, NT])
                c.v = c.keep(att, "v", [P, NTILE, 512])
                c.small = c.keep(att, "small", [P, NTILE, NSMALL])
                with ExitStack() as ssd:
                    c.convin_p = c.keep(ssd, "convin_p", [P, KD, SEQ + 3])
                    c.convin_s = c.keep(ssd, "convin_s", [P, KD, NB, TS + 3])
                    c.z = c.keep(ssd, "z", [P, NTILE, 512])
                    stage_project(c)
                    if upto >= 2:
                        stage_ssd(c)
                c.pt_in, c.ki_in = c.sem("page_table_in"), c.sem("ki_in")
                c.ptab = att.enter_context(nc.sbuf_tensor("ptab", [1, NB * NPAGE], I32))
                c.kvring = c.keep(att, "kvring", [P, KV_RING, 4 * 512])
                if upto >= 3:
                    stage_dsa_prompt(c)
                if upto >= 4:
                    stage_dsa_sample(c)
            if dump and upto <= 4:
                return dump(c)
            c.reset_semaphores()
            c.h = c.keep(right, "h", [P, NTILE, D], "right")
            c.hT = c.keep(right, "hT", [P, KD, NT], "right")
            stage_mix(c)
        if dump and upto <= 5:
            return dump(c)
        stage_memory(c)
        memory.close()
        if dump and upto <= 6:
            return dump(c)
        with ExitStack() as routed:
            c.S = c.keep(routed, "S", [P, NTILE, 2 * PH * NKEYS])
            c.hH = routed.enter_context(nc.sbuf_tensor("hH", [P, KD, NT], F32R))
            c.hL = routed.enter_context(nc.sbuf_tensor("hL", [P, KD, NT], F32R))
            stage_scores(c)
            stage_activate(c)
        stage_experts(c)
        stage_finish(c)


def shape_constants():
    f = np.float32
    i, j = np.arange(P)[:, None], np.arange(P)[None, :]
    r, q = np.arange(NS)[:, None], np.arange(NS)[None, :]
    same = r // TS == q // TS
    k = {
        "k_ident": np.eye(P, dtype=f),
        "k_iota": np.broadcast_to(np.arange(P, dtype=f), (P, P)),
        "k_tri": (i <= j).astype(f),
        "k_low": (j <= i).astype(f),
        "k_lowneg": np.where(j <= i, 0.0, NOT_CAUSAL).astype(f),
        "k_ones": np.ones((P, P), f),
        "k_triS": (same & (r <= q)).astype(f),
        "k_lowS": (same & (q <= r)).astype(f),
        "k_lowSneg": np.where(same & (q <= r), 0.0, NOT_CAUSAL).astype(f),
        "k_onesS": same.astype(f),
        "k_bsel": (np.arange(NS)[:, None] // TS == np.arange(NB)[None, :]).astype(f),
        "k_bcol": np.broadcast_to((np.arange(NS)[None, :] // TS == np.arange(NB)[:, None]).astype(f), (P, NB, NS)),
    }

    def bucket(dist):
        n = np.maximum(dist, 0)
        nf = np.maximum(n, 1).astype(f)
        large = 16 + (np.log(nf / f(16)) / f(np.log(128 / 16)) * f(16)).astype(np.int32)
        return np.where(n < 16, n, np.minimum(large, NBUCKET - 1))

    def onehot(dist):
        return (np.arange(NBUCKET).reshape((-1,) + (1,) * np.ndim(dist)) == bucket(dist)[None]).astype(f)

    k["bucket_rev"] = onehot(2 * P - 1 - np.arange(3 * P))
    t = np.arange(TS)[:, None]
    k["bucket_keys"] = onehot(np.concatenate([PAST + t - np.arange(PAST)[None, :], t - (np.arange(NS) % TS)[None, :]], 1)
                              ).transpose(1, 0, 2).reshape(TS * NBUCKET, NKEY)
    k["t_rows"] = (np.arange(TS * NBUCKET)[:, None] // NBUCKET == np.arange(TS)[None, :]).astype(f)
    half = NB // 2
    b4, h, t = (x.ravel() for x in np.meshgrid(np.arange(half), np.arange(H), np.arange(TS), indexing="ij"))
    k["expand_rows"] = np.stack([(np.arange(P)[:, None] == ((g * half + b4) * TS + t)[None, :]) for g in range(2)],
                                1).astype(f)
    hh, tt = (x.ravel() for x in np.meshgrid(np.arange(H), np.arange(TS), indexing="ij"))
    k["head_mask"] = (HD ** -0.5 * (np.arange(H)[None, None, :] == 2 * np.arange(4)[None, :, None]
                                    + (np.arange(P) // HD)[:, None, None])).astype(f)
    k["out_mask"] = (hh[:, None] == (np.arange(512) // HD)[None, :]).astype(f)
    k["t_sum"] = (tt[:, None] == np.arange(TS)[None, :]).astype(f)
    k["t_sel"] = (np.arange(NS)[:, None] % TS == np.arange(TS)[None, :]).astype(f)
    k["w_mask"] = ((np.arange(2)[None, :, None] * half + b4[:, None, None]) * TS + t[:, None, None]
                   == np.arange(NS)[None, None, :]).astype(f)
    return {n: np.ascontiguousarray(a) for n, a in k.items()}


def layouts(x):
    c = np.ascontiguousarray

    def chunks(w):
        return c(w.reshape(-1, P, w.shape[1]).transpose(1, 0, 2))

    w_in = x["w_in"]
    cut = lambda at, n: w_in[:, at:at + n]
    wt = np.concatenate([cut(OFF_XBC, CONV), cut(OFF_Q, 512), cut(OFF_K, 512), cut(OFF_QI, 512), cut(OFF_KI, HD),
                         cut(OFF_KI, HD)], 1)
    xr = np.concatenate([x["x_prompt"].reshape(SEQ, D), x["x_sample"].reshape(NS, D)], 0)
    vec = {n: x[n].reshape(-1) for n in VEC if n != "bias_far"}
    vec["bias_far"] = x["rel_bias"][NBUCKET - 1]
    out = {
        "xT": chunks(c(xr.T)),
        "x_rows": xr,
        "w_blk": c(chunks(wt).reshape(P, KD, NBLK, P).transpose(2, 0, 1, 3)),
        "w_row": np.stack([chunks(cut(OFF_Z, 512)), chunks(cut(OFF_V, 512))]),
        "w_small": chunks(np.concatenate([cut(OFF_DT, H), cut(OFF_KI, HD), cut(OFF_WI, H)], 1)),
        "vecs": np.concatenate([vec[n] for n in VEC])[None],
        "state_convT": x["state_conv"].reshape(NB, 3, KD, P).transpose(3, 2, 0, 1),
        "conv_w": x["conv_w"].reshape(4, KD, P).transpose(2, 1, 0),
        "conv_b": x["conv_b"].reshape(KD, P).T,
        "state_ssmT": x["state_ssm"].reshape(NB, 512, P).transpose(2, 0, 1),
        "state_ssm": x["state_ssm"].reshape(NB, 4, P, P).transpose(2, 0, 1, 3),
        "rel_bias": x["rel_bias"],
        "ln1": np.stack([x["ln1_g"], x["ln1_b"]])[None],
        "ln2": np.stack([x["ln2_g"], x["ln2_b"]])[None],
        "ln3": np.stack([x["ln3_g"], x["ln3_b"]])[None],
        "page_table": x["page_table"].reshape(1, -1),
        "kidxT": x["cache_kidx"].transpose(0, 2, 1),
        "kT_pages": x["cache_k"].reshape(-1, PAGE, 4, P).transpose(0, 3, 2, 1).reshape(-1, P, 4 * PAGE),
        "v_pages": x["cache_v"].reshape(-1, PAGE, 512),
        "w_out": chunks(x["w_out"]),
        "memT": chunks(c(x["mem_prompt"][0].T)),
        "w_ck": chunks(x["w_ck"]), "w_cv": chunks(x["w_cv"]), "w_cq": chunks(x["w_cq"]), "w_co": chunks(x["w_co"]),
        "cmkT": x["cache_mem_k"].transpose(0, 3, 2, 1),
        "cmv": x["cache_mem_v"].reshape(NB, MEM, 512),
        "wq_blk": chunks(x["peer_wq"]).reshape(P, KD, 2 * PH, P).transpose(2, 0, 1, 3),
        "subkeysT": x["peer_subkeys"].reshape(2 * PH, NKEYS, P).transpose(2, 0, 1),
        "uT": x["peer_u"].reshape(NKEYS, NKEYS, KD, P).transpose(1, 3, 2, 0),
        "v_rows": x["peer_v"].reshape(NKEYS, NKEYS, D).transpose(1, 0, 2),
    }
    out.update(shape_constants())
    return {n: c(a) for n, a in out.items()}


OUTPUTS = {
    "y_p": (SEQ, D), "y_s": (NS, D), "k_p": (SEQ, 512), "v_p": (SEQ, 512), "kidx_p": (SEQ, HD),
    "memk_p": (MEM, 512), "memv_p": (MEM, 512), "ssm_p": (512, P), "conv_p": (1, 3, CONV),
    "k_s": (NS, 512), "v_s": (NS, 512), "kidx_s": (NS, HD), "ssm_s": (NB, 512, P), "conv_s": (NB, 3, CONV),
}
SHAPES = {
    "y_p": (1, SEQ, D), "y_s": (NB, TS, D), "k_p": (1, SEQ, H, HD), "v_p": (1, SEQ, H, HD), "kidx_p": (1, SEQ, HD),
    "memk_p": (1, MEM, MH, MD), "memv_p": (1, MEM, MH, MD), "ssm_p": (1, H, HD, P), "conv_p": (1, 3, CONV),
    "k_s": (NB, TS, H, HD), "v_s": (NB, TS, H, HD), "kidx_s": (NB, TS, HD), "ssm_s": (NB, H, HD, P),
    "conv_s": (NB, 3, CONV),
}


def kernel(**inputs):
    import concourse.bacc as bacc
    from concourse.bass_utils import run_bass_kernel_spmd

    nc = bacc.Bacc("TRN2", target_bir_lowering=False, num_devices=1)
    arrays, A = {}, {}
    for name, a in layouts({k: np.asarray(v) for k, v in inputs.items()}).items():
        arrays[f"in_{name}"] = a
        A[name] = nc.dram_tensor(f"in_{name}", a.shape, mybir.dt.from_np(a.dtype), kind="ExternalInput").ap()
    for name, shape in OUTPUTS.items():
        A[name] = nc.dram_tensor(f"out_{name}", shape, F32, kind="ExternalOutput").ap()
    A["gates"] = nc.dram_tensor("gate_table", [NG, P, GCOL], F32, kind="Internal").ap()
    A["acts"] = nc.dram_tensor("activation_table", [NKEYS, P, NT], F32, kind="Internal").ap()
    build(nc, A)
    r = run_bass_kernel_spmd(nc, [arrays], core_ids=[0])
    return tuple(r.results[0][f"out_{name}"].reshape(SHAPES[name]) for name in OUTPUTS)
```
